# Optimizing a Trainium2 kernel written in Bass

```python
import jax, jax.numpy as jnp
from jax import lax
import numpy as np

D_MODEL = 1024
BATCH = 1
SEQ = 512
DEPTH = 2

CHUNK = 64
N_META = 16
ROPE_THETA = 500000.0
ROPE_FRACTION = 4
NORM_EPS = 1e-6

HGRN_HEADS = 4
HGRN_HEAD_DIM = 128
HGRN_WIDTH = HGRN_HEADS * HGRN_HEAD_DIM

ATT_HEADS = 8
ATT_KV_HEADS = 2
ATT_HEAD_DIM = 64
ATT_GROUP = ATT_HEADS // ATT_KV_HEADS
ATT_WIDTH = ATT_HEADS * ATT_HEAD_DIM
ATT_KV_WIDTH = ATT_KV_HEADS * ATT_HEAD_DIM
IDX_HEADS = 8
IDX_HEAD_DIM = 32
TOPK_MAX = 256
Q_BLOCK = 128

N_BRANCHES = 2

N_GROUPS = 4
EXPERTS_PER_GROUP = 8
N_EXPERTS = N_GROUPS * EXPERTS_PER_GROUP
EXPERT_TOP_K = 2
EXPERT_FF = D_MODEL // 4

IN_SPLITS = (HGRN_WIDTH, HGRN_WIDTH, HGRN_WIDTH, HGRN_WIDTH,
             ATT_WIDTH, ATT_KV_WIDTH, ATT_KV_WIDTH,
             IDX_HEADS * IDX_HEAD_DIM, IDX_HEAD_DIM, IDX_HEADS,
             D_MODEL, D_MODEL)
IN_WIDTH = sum(IN_SPLITS)

kernel_name = "hybrid_hgrn2_dsa_hiermoe_streaming"

def rmsnorm(x, g):
    xf = x.astype(jnp.float32)
    y = xf * lax.rsqrt(jnp.mean(xf * xf, axis=-1, keepdims=True) + NORM_EPS)
    return (y * g.astype(jnp.float32)).astype(x.dtype)

def chunk_ids(pos):
    return jnp.where(pos < N_META, 0, (pos - N_META) // CHUNK + 1)

def rope_tables(n_pos, head_dim):
    rot = head_dim // ROPE_FRACTION
    inv = ROPE_THETA ** (-jnp.arange(0, rot, 2, dtype=jnp.float32) / rot)
    ang = jnp.arange(n_pos, dtype=jnp.float32)[:, None] * inv[None, :]
    return jnp.cos(ang), jnp.sin(ang)

def apply_partial_rope(x, cos, sin):
    half = cos.shape[-1]
    rot = 2 * half
    xf = x.astype(jnp.float32)
    x1, x2, rest = xf[..., :half], xf[..., half:rot], xf[..., rot:]
    c, s = cos[:, None, :], sin[:, None, :]
    out = jnp.concatenate([x1 * c - x2 * s, x2 * c + x1 * s, rest], axis=-1)
    return out.astype(x.dtype)

def hgrn_lower_bounds(lb_logits):
    p = jax.nn.softmax(lb_logits.astype(jnp.float32), axis=0)
    c = jnp.cumsum(p, axis=0)
    return c - c[0:1]

def hgrn2_mixer(q, f_pre, inp, g_out, lb, norm_g):
    B, L, _ = q.shape
    f32 = jnp.float32
    z = f_pre.astype(f32)
    f = lb + (1.0 - lb) * jax.nn.sigmoid(z)
    log_f = jnp.log(f)
    k = (1.0 - lb) * jax.nn.sigmoid(-z)
    front = (-N_META) % CHUNK
    back = (-(front + L)) % CHUNK
    T = front + L + back
    n_chunks = T // CHUNK

    def to_chunks(t):
        t = jnp.pad(t.astype(f32), ((0, 0), (front, back), (0, 0)))
        return t.reshape(B, n_chunks, CHUNK, HGRN_HEADS, HGRN_HEAD_DIM).transpose(1, 0, 3, 2, 4)

    qc, kc, vc, gc = to_chunks(q), to_chunks(k), to_chunks(inp), to_chunks(log_f)
    tri = jnp.tril(jnp.ones((CHUNK, CHUNK), dtype=bool))

    def step(S, xs):
        qb, kb, vb, gb = xs
        b = jnp.cumsum(gb, axis=2)
        inter = jnp.einsum('bhtd,bhde->bhte', qb * jnp.exp(b), S)
        diff = jnp.where(tri[None, None, :, :, None],
                         b[:, :, :, None, :] - b[:, :, None, :, :], -jnp.inf)
        A = jnp.einsum('bhtsd,bhsd->bhts', qb[:, :, :, None, :] * jnp.exp(diff), kb)
        intra = jnp.einsum('bhts,bhse->bhte', A, vb)
        b_last = b[:, :, -1:, :]
        S_new = (jnp.exp(b_last[:, :, 0, :])[..., None] * S
                 + jnp.einsum('bhsd,bhse->bhde', kb * jnp.exp(b_last - b), vb))
        return S_new, inter + intra

    S0 = jnp.zeros((B, HGRN_HEADS, HGRN_HEAD_DIM, HGRN_HEAD_DIM), f32)
    _, o = lax.scan(step, S0, (qc, kc, vc, gc))
    o = o.transpose(1, 0, 3, 2, 4).reshape(B, T, HGRN_HEADS, HGRN_HEAD_DIM)[:, front:front + L]
    o = rmsnorm(o, norm_g.reshape(HGRN_HEADS, HGRN_HEAD_DIM)).reshape(B, L, HGRN_WIDTH)
    return (o * jax.nn.silu(g_out.astype(f32))).astype(q.dtype)

def to_q_blocks(t, n_blk):
    pad = n_blk * Q_BLOCK - t.shape[1]
    t = jnp.pad(t, [(0, 0), (0, pad)] + [(0, 0)] * (t.ndim - 2))
    return jnp.moveaxis(t.reshape(t.shape[0], n_blk, Q_BLOCK, *t.shape[2:]), 1, 0)

def dsa_mixer(q, k, v, q_idx, k_idx, w_idx, k_idx_g, cos_a, sin_a, cos_i, sin_i, topk):
    B, L, _ = q.shape
    f32 = jnp.float32
    q = apply_partial_rope(q.reshape(B, L, ATT_HEADS, ATT_HEAD_DIM), cos_a, sin_a)
    k = apply_partial_rope(k.reshape(B, L, ATT_KV_HEADS, ATT_HEAD_DIM), cos_a, sin_a)
    v = v.reshape(B, L, ATT_KV_HEADS, ATT_HEAD_DIM)
    q_idx = apply_partial_rope(q_idx.reshape(B, L, IDX_HEADS, IDX_HEAD_DIM), cos_i, sin_i)
    k_idx = apply_partial_rope(rmsnorm(k_idx, k_idx_g)[:, :, None, :], cos_i, sin_i)[:, :, 0, :]
    w_idx = w_idx.astype(f32) * (IDX_HEADS ** -0.5 * IDX_HEAD_DIM ** -0.5)
    scale = ATT_HEAD_DIM ** -0.5
    n_blk = -(-L // Q_BLOCK)
    cid_k = chunk_ids(jnp.arange(L))
    cid_q = chunk_ids(jnp.arange(n_blk * Q_BLOCK)).reshape(n_blk, Q_BLOCK)

    def one_block(args):
        qb, qib, wb, cqb = args
        rel = jax.nn.relu(jnp.einsum('bqhd,bkd->bqhk', qib, k_idx).astype(f32))
        score = jnp.einsum('bqhk,bqh->bqk', rel, wb)
        admissible = cid_k[None, :] <= cqb[:, None]
        score = jnp.where(admissible[None], score, -jnp.inf)
        _, sel = lax.top_k(score, topk)
        valid = cid_k[sel] <= cqb[None, :, None]
        k_sel = jax.vmap(lambda kb, ib: kb[ib])(k, sel)
        v_sel = jax.vmap(lambda vb, ib: vb[ib])(v, sel)
        qg = qb.reshape(B, Q_BLOCK, ATT_KV_HEADS, ATT_GROUP, ATT_HEAD_DIM)
        s = jnp.einsum('bqgrd,bqkgd->bqgrk', qg, k_sel).astype(f32) * scale
        s = jnp.where(valid[:, :, None, None, :], s, -jnp.inf)
        p = jax.nn.softmax(s, axis=-1).astype(v.dtype)
        o = jnp.einsum('bqgrk,bqkgd->bqgrd', p, v_sel)
        return o.reshape(B, Q_BLOCK, ATT_WIDTH)

    out = lax.map(one_block, (to_q_blocks(q, n_blk), to_q_blocks(q_idx, n_blk),
                              to_q_blocks(w_idx, n_blk), cid_q))
    return jnp.moveaxis(out, 0, 1).reshape(B, n_blk * Q_BLOCK, ATT_WIDTH)[:, :L]

def hier_moe(h, wg_r, bg_r, we_r, be_r, w_gate, w_up, w_down):
    B, L, D = h.shape
    N = B * L
    f32 = jnp.float32
    hf = h.reshape(N, D)
    pg = jax.nn.softmax((hf @ wg_r).astype(f32) + bg_r.astype(f32), axis=-1)
    pg_top, g_sel = lax.top_k(pg, 1)
    le = ((hf @ we_r).astype(f32) + be_r.astype(f32)).reshape(N, N_GROUPS, EXPERTS_PER_GROUP)
    le_sel = jnp.take_along_axis(le, g_sel[:, :, None], axis=1)[:, 0]
    pe = jax.nn.softmax(le_sel, axis=-1)
    pe_top, e_sel = lax.top_k(pe, EXPERT_TOP_K)
    w_e = pe_top / jnp.sum(pe_top, axis=-1, keepdims=True) * pg_top
    g_onehot = jax.nn.one_hot(g_sel[:, 0], N_GROUPS, dtype=f32)
    e_w = jnp.sum(jax.nn.one_hot(e_sel, EXPERTS_PER_GROUP, dtype=f32) * w_e[..., None], axis=1)
    combine = (g_onehot[:, :, None] * e_w[:, None, :]).transpose(1, 0, 2)
    wg = w_gate.reshape(N_GROUPS, EXPERTS_PER_GROUP, D, EXPERT_FF)
    wu = w_up.reshape(N_GROUPS, EXPERTS_PER_GROUP, D, EXPERT_FF)
    wd = w_down.reshape(N_GROUPS, EXPERTS_PER_GROUP, EXPERT_FF, D)

    def group_out(args):
        g_w, u_w, d_w, c = args
        a = jnp.einsum('nd,edf->nef', hf, g_w)
        u = jnp.einsum('nd,edf->nef', hf, u_w)
        act = jax.nn.silu(a) * u * c[:, :, None].astype(h.dtype)
        return jnp.einsum('nef,efd->nd', act, d_w)

    y = jnp.sum(lax.map(group_out, (wg, wu, wd, combine)), axis=0)
    return y.reshape(B, L, D).astype(h.dtype)

def setup_inputs(seed: int = 0) -> dict:
    key = jax.random.key(seed)
    ks = jax.random.split(key, 20)
    f32 = jnp.float32
    nrm = lambda k, shape, s: jax.random.normal(k, shape, f32) * s
    D = D_MODEL
    return {
        "x": nrm(ks[0], (BATCH, SEQ, D), 1.0),
        "meta_tokens": nrm(ks[1], (N_META, D), 1.0),
        "mix_norm_g": 1.0 + nrm(ks[2], (DEPTH, D), 0.02),
        "w_in": nrm(ks[3], (DEPTH, D, IN_WIDTH), D ** -0.5),
        "hgrn_lb_logits": nrm(ks[4], (DEPTH, HGRN_WIDTH), 0.5),
        "hgrn_norm_g": 1.0 + nrm(ks[5], (DEPTH, HGRN_WIDTH), 0.02),
        "idx_k_norm_g": 1.0 + nrm(ks[6], (DEPTH, IDX_HEAD_DIM), 0.02),
        "w_branch_hgrn": nrm(ks[7], (DEPTH, HGRN_WIDTH, D), HGRN_WIDTH ** -0.5),
        "w_branch_dsa": nrm(ks[8], (DEPTH, ATT_WIDTH, D), ATT_WIDTH ** -0.5),
        "w_out": nrm(ks[9], (DEPTH, D, D), D ** -0.5),
        "ffn_norm_g": 1.0 + nrm(ks[10], (DEPTH, D), 0.02),
        "router_group_w": nrm(ks[11], (DEPTH, D, N_GROUPS), D ** -0.5),
        "router_group_b": nrm(ks[12], (DEPTH, N_GROUPS), 0.01),
        "router_expert_w": nrm(ks[13], (DEPTH, D, N_EXPERTS), D ** -0.5),
        "router_expert_b": nrm(ks[14], (DEPTH, N_EXPERTS), 0.01),
        "w_expert_gate": nrm(ks[15], (DEPTH, N_EXPERTS, D, EXPERT_FF), D ** -0.5),
        "w_expert_up": nrm(ks[16], (DEPTH, N_EXPERTS, D, EXPERT_FF), D ** -0.5),
        "w_expert_down": nrm(ks[17], (DEPTH, N_EXPERTS, EXPERT_FF, D), EXPERT_FF ** -0.5),
        "final_norm_g": 1.0 + nrm(ks[18], (D,), 0.02),
    }

def reference(x, meta_tokens, mix_norm_g, w_in, hgrn_lb_logits, hgrn_norm_g, idx_k_norm_g,
              w_branch_hgrn, w_branch_dsa, w_out, ffn_norm_g, router_group_w, router_group_b,
              router_expert_w, router_expert_b, w_expert_gate, w_expert_up, w_expert_down,
              final_norm_g):
    B = x.shape[0]
    meta = jnp.broadcast_to(meta_tokens[None].astype(x.dtype), (B, N_META, D_MODEL))
    h = jnp.concatenate([meta, x], axis=1)
    L = h.shape[1]
    cos_a, sin_a = rope_tables(L, ATT_HEAD_DIM)
    cos_i, sin_i = rope_tables(L, IDX_HEAD_DIM)
    topk = min(TOPK_MAX, L // 4)
    lower_bounds = hgrn_lower_bounds(hgrn_lb_logits)
    offsets = np.cumsum(IN_SPLITS)[:-1].tolist()
    for layer in range(DEPTH):
        xn = rmsnorm(h, mix_norm_g[layer])
        proj = xn @ w_in[layer]
        (hq, hf, hi, hg, aq, ak, av, iq, ik, iw, gate_a, gate_b) = jnp.split(proj, offsets, axis=-1)
        y_a = hgrn2_mixer(hq, hf, hi, hg, lower_bounds[layer], hgrn_norm_g[layer])
        y_b = dsa_mixer(aq, ak, av, iq, ik, iw, idx_k_norm_g[layer],
                        cos_a, sin_a, cos_i, sin_i, topk)
        merged = (jax.nn.sigmoid(gate_a) * (y_a @ w_branch_hgrn[layer])
                  + jax.nn.sigmoid(gate_b) * (y_b @ w_branch_dsa[layer]))
        h = h + merged @ w_out[layer]
        h = h + hier_moe(rmsnorm(h, ffn_norm_g[layer]), router_group_w[layer], router_group_b[layer],
                         router_expert_w[layer], router_expert_b[layer], w_expert_gate[layer],
                         w_expert_up[layer], w_expert_down[layer])
    return rmsnorm(h, final_norm_g)[:, N_META:]


_drawn_inputs = setup_inputs


def setup_inputs(seed=0):
    import zlib

    import numpy as np

    out = dict(_drawn_inputs(seed))
    spreads = {}
    factors = {}
    for name, (base, spread) in spreads.items():
        noise = np.random.default_rng([zlib.crc32(name.encode()), seed]).standard_normal(out[name].shape)
        drawn = base * np.exp(spread * noise) if base else spread * noise
        out[name] = __import__('jax').numpy.asarray(drawn.astype(out[name].dtype))
    for name, factor in factors.items():
        out[name] = (out[name] * factor).astype(out[name].dtype)
    return out
```

```python
from contextlib import ExitStack

import concourse.bass as bass
from concourse import mybir
import numpy as np

F32 = mybir.dt.float32
I32 = mybir.dt.int32
U8 = mybir.dt.uint8
ALU = mybir.AluOpType
ACT = mybir.ActivationFunctionType
AX = mybir.AxisListType.X

P = 128
D = 1024
KC = D // P
SEQ, NMETA = 512, 16
LT = SEQ + NMETA
DEPTH = 2
EPS = 1e-6
NT = 5
T0 = [0, 80, 208, 336, 464]
TS = [80, 128, 128, 128, 64]
W = [80, 208, 336, 464, 528]
TOPK = min(256, LT // 4)
HH, HD = 4, 128
AH, AD = 8, 64
IH, ID = 8, 32
NG, EPG = 4, 8
NE = NG * EPG
FF = D // 4
SLOTS = 64
XBLK = (2 * LT) // SLOTS
NBLK = NE + XBLK
KMAX = LT // SLOTS
REPL, HIDDEN, SENT, NEG = -3e38, -2e38, 3e38, -1e30
SCALAR_MIN = -3e38
INITS = 11

C_HQ, C_HF, C_HI, C_HG, C_AQ, C_AK, C_IK, C_GA, C_GB = 0, 512, 1024, 1536, 2048, 2560, 3072, 3112, 4136
CHUNKS = ["k3", "k2", "k1", "hi", "hf", "hq", "hg", "ga0", "ga1", "wa", "gb0", "gb1", "wb", "wo0", "wo1", "ro"]
LEVELS = 8


def plan_jobs():
    jobs, last = [], {}

    def add(*names):
        jobs.extend(names)
        return len(jobs) - 1

    add(*[("xt", i) for i in range(NT)])
    for c in ("k3", "k2", "k1", "hi"):
        last[c] = add(*[(c, i) for i in range(NT)])
    add(*[(n, i) for i in range(NT) for n in ("it", "at")])
    for c in ("hf", "hq"):
        last[c] = add(*[(c, j) for j in range(HH)])
    add(*[("ix", i, h) for i in range(1, NT) for h in range(IH)])
    add(*[("lv", h, l) for h in range(HH) for l in range(LEVELS)])
    for j in range(NT):
        add(("kt", j), ("ot", j))
        if j < NT - 1:
            add(("su", j))
    last["hg"] = add(*[("hg", j) for j in range(HH)])
    add(*[("on", h) for h in range(HH)])
    last["ga0"] = add(*[("ga", c) for c in range(4)])
    last["ga1"] = add(*[("ga", c) for c in range(4, 8)])
    last["wa"] = add(*[("wa", c) for c in range(8)])
    groups = [(i, g) for i in range(NT) for g in range(2)]
    add(*[("qk", 0, h) for h in range(4)])
    for n, (i, g) in enumerate(groups):
        if n + 1 < len(groups):
            ni, ng = groups[n + 1]
            add(*[("qk", ni, 4 * ng + r) for r in range(4)])
        add(*[("pt", i, g, k) for k in range(i + 1)])
        add(("pv", i, g))
    last["gb0"] = add(*[("gb", c) for c in range(4)])
    last["gb1"] = add(*[("gb", c) for c in range(4, 8)])
    last["wb"] = add(*[("wb", c) for c in range(8)])
    last["wo0"] = add(*[("wo", 0, i) for i in range(NT)])
    last["wo1"] = add(*[("wo", 1, i) for i in range(NT)])
    add(*[("xt2", i) for i in range(NT)])
    last["ro"] = add(*[("ro", i) for i in range(NT)])
    add(("rank",), ("slot",))
    return {j: n for n, j in enumerate(jobs)}, last


JOBS, LAST = plan_jobs()
NJ = len(JOBS)
PER_SLAB = [len([n for n in JOBS.values() if n % 4 == s]) for s in range(4)]

DVE_OPS, ACT_OPS = 268, 14
PER = dict(
    pe_done=NJ, dve=DVE_OPS, act=ACT_OPS, ss_ready=0, rms_ready=2, xn_ready=2 * NT, ksq_ready=1,
    kn_ready=1, rope_ready=1, e_ready=HH, lnf_ready=HH, f_done=HH, rel_used=32, d_ready=32, ex_ready=37, qe_ready=28,
    qb_ready=HH, kw_ready=HH, sq_ready=HH, ya_ready=1, mx_ready=40, p_ready=40, pn_ready=40, pt_used=20, mg_ready=8,
    xw0=48, xw1=32, rt_ready=2, rt_exp=2, c_ready=1, ab_ready=1, idx_ready=1, base_ready=1, sidx_ready=1,
    g_load=32, par_load=48, lb_ready=1, lb_ln=1, stg=NE, xg0=16 * NE // 2, xg1=16 * NE // 2, t_done=NE, xt_done=NE, g_done=NE,
    si_done=NE, am_done=NE, d_done=NE, y_done=NE, yd0=16 * NE // 2, yd1=16 * NE // 2, yg0=80, yg1=80, cb_done=10,
)
for _s in range(4):
    PER[f"free{_s}"] = PER_SLAB[_s]
for _s in range(2):
    PER[f"gu{_s}"] = 16 * len(CHUNKS) // 2 + 32 * NE // 2
    PER[f"dn{_s}"] = 16 * NE // 2
START = {"free0": 1, "free1": 1, "free2": 1, "free3": 1, "t_done": 2, "g_done": 2, "d_done": 2, "y_done": 2, "am_done": 2, "cb_done": 1}
OV = dict(ov_w=48, ov_stg=1, ov_x=16, ov_t=1, ov_xt=1, ov_g=1, ov_si=1, ov_am=1, ov_d=1, ov_y=1, ov_yd=16)
for _n, _k in OV.items():
    PER[_n] = _k * XBLK



def freed_at(job):
    return f"free{JOBS[job] % 4}", JOBS[job] // 4 + 1


PTS = [(i, g, k) for i in range(NT) for g in range(2) for k in range(i + 1)]
PT_COUNT = {b: len([x for x in PTS[:n + 1] if x[2] < x[0]]) for n, b in enumerate(PTS)}


def shape_constants():
    def rope(hd):
        rot = hd // 4
        inv = np.float32(500000.0) ** (-np.arange(0, rot, 2, dtype=np.float32) / np.float32(rot))
        ang = np.arange(LT, dtype=np.float32)[:, None] * inv[None, :]
        out = np.zeros((P, 2, NT, rot // 2), np.float32)
        for i in range(NT):
            out[:TS[i], 0, i] = np.cos(ang[T0[i]:T0[i] + TS[i]])
            out[:TS[i], 1, i] = np.sin(ang[T0[i]:T0[i] + TS[i]])
        return out.reshape(P, -1)

    s, t = np.arange(P)[:, None], np.arange(P)[None, :]
    lv = np.zeros((P, LEVELS, P), np.float32)
    lv[:, 0] = s == t
    for l in range(1, LEVELS):
        half = 2 ** (l - 1)
        lv[:, l] = (s // (2 * half) == t // (2 * half)) & (s % (2 * half) < half) & (t % (2 * half) >= half)
    cols = [
        np.eye(P), np.ones((P, P)), (s < t),
        rope(AD), rope(ID),
        np.broadcast_to(np.arange(64.0), (P, 64)), np.broadcast_to(np.arange(NBLK, dtype=float), (P, NBLK)),
        np.broadcast_to(np.arange(NE, dtype=float), (P, NE)),
        np.broadcast_to(np.arange(NG, 0, -1.0), (P, NG)), np.broadcast_to(np.arange(EPG, 0, -1.0), (P, EPG)),
        np.broadcast_to(SLOTS * np.arange(1.0, KMAX + 1), (P, KMAX)),
        np.arange(P)[:, None] + np.array(T0)[None, :],
        np.broadcast_to((np.arange(NT * P) % P != 0), (P, NT * P)),
        np.where((s < NMETA) & (np.arange(W[0])[None] >= NMETA), NEG, 0.0),
    ]
    sizes = [c.shape[1] for c in cols]
    return np.concatenate([np.asarray(c, np.float32) for c in cols], 1), sizes, lv.reshape(P, -1)


def program(nc, a, out):
    _, sizes, _ = shape_constants()
    with ExitStack() as ctx:
        def sb(name, shape, dt=F32):
            return ctx.enter_context(nc.sbuf_tensor(name, shape, dt))

        sem = {n: ctx.enter_context(nc.semaphore(n)) for n in PER}
        for n in ("const_load", "x_load", "init", "lbe", "out_done", "fin_ss", "fin_g", "fin_rms", "fin_y", "settled", "y_init"):
            sem[n] = ctx.enter_context(nc.semaphore(n))

        h = sb("resid", [P, NT, D])
        xnT = sb("xnT", [P, KC, LT])
        gu_ring = sb("gu_ring", [P, 2, 4096])
        dn_ring = sb("dn_ring", [P, 2, 2048])
        r1 = sb("r1", [P, 3 * 2560])
        pr = sb("pr", [P, 4224])
        r2 = sb("r2", [P, 3168 + 1584 + 2560])
        AT = sb("AT", [P, HH, NT, P])
        sc = sb("sc", [P, NT, 4 + LT])
        vA = sb("vA", [P, NT, 2 * AD])
        ptb = sb("ptb", [P, 2, 1024])
        S = sb("S", [P, HH, HD])
        consts = sb("tables", [P, sum(sizes)])
        lvm = sb("masks_u8", [P, LEVELS, P], U8)
        small = sb("small", [P, 1300])

        qtok = r1[:, 0:NT * 1064].rearrange("p (i n) -> p i n", i=NT)
        hq, hk, hb = (r1[:, n * 2560:(n + 1) * 2560].rearrange("p (h j t) -> p h j t", h=HH, j=NT) for n in range(3))
        sga = r1[:, 2560:2560 + 8 * LT].rearrange("p (c t) -> p c t", c=8)
        xg = r1[:, 0:2048].rearrange("p (u n) -> p u n", u=2)
        ysb = r1[:, 2048:4096].rearrange("p (u n) -> p u n", u=2)
        xgT = r1[:, 4096:5120].rearrange("p (u c s) -> p u c s", u=2, c=KC)
        sg = r1[:, 5120:5376].rearrange("p (u n) -> p u n", u=2)
        am = r1[:, 5376:5632].rearrange("p (u j s) -> p u j s", u=2, j=2)
        xn = pr[:, 0:2048].rearrange("p (u n) -> p u n", u=2)
        kdup = pr[:, 0:1280].rearrange("p (i g r d) -> p i g r d", i=NT, g=2, r=2)
        ikdup = pr[:, 1280:1920].rearrange("p (i r d) -> p i r d", i=NT, r=4)
        rt = pr[:, 1920:4224]
        ebuf, qe, ke = (pr[:, n * 1280:(n + 1) * 1280].rearrange("p (u t) -> p u t", u=2) for n in range(3))
        osq = pr[:, 0:2560].rearrange("p (h t) -> p h t", h=HH)
        pb = pr[:, :].rearrange("p (h t) -> p h t", h=8)
        sgb = pb
        aqk = r2[:, 0:3168].rearrange("p (c t) -> p c t", c=6)
        ixT = r2[:, 3168:4752].rearrange("p (c t) -> p c t", c=3)
        kwT = r2[:, 3168:4192].rearrange("p (u n) -> p u n", u=2)
        vH = r2[:, 4752:7312].rearrange("p (i n) -> p i n", i=NT)
        ybT = r2[:, 4752:4752 + 4 * LT].rearrange("p (c t) -> p c t", c=4)
        ovw = r2[:, 0:6144]
        gB = ptb[:, 0, :]
        rel = ptb[:, :, 0:LT]
        ptq = ptb[:, :, :].rearrange("p a (b n) -> p (a b) n", b=2)

        at_ = [0]

        def const(n):
            at_[0] += sizes[n]
            return consts[:, at_[0] - sizes[n]:at_[0]]

        ident, ones, tri, rope_a, rope_i, io64, ioblk, ioe, descg, desce, kthr, tokid, reset, mask0 = (
            const(n) for n in range(14))
        rope_a = rope_a.rearrange("p (a i d) -> p a i d", a=2, i=NT)
        rope_i = rope_i.rearrange("p (a i d) -> p a i d", a=2, i=NT)

        at_[0] = 0

        def tiny(n):
            at_[0] += n
            return small[:, at_[0] - n:at_[0]]

        ss, rms, rstd = tiny(NT), tiny(NT), tiny(NT)
        kss, krms = tiny(NT), tiny(NT)
        ik_g = tiny(ID)
        iw = tiny(NT * IH).rearrange("p (i h) -> p i h", i=NT)
        hn_g = tiny(HH)
        lb, lb1, omlb, llb = tiny(HH), tiny(HH), tiny(HH), tiny(HH)
        dec = tiny(HH * NT).rearrange("p (h j) -> p h j", h=HH)
        top8 = tiny(4 * 8).rearrange("p (i k) -> p i k", i=4)
        mx, nmx, psum_, pinv = tiny(8), tiny(8), tiny(8), tiny(8)
        rb = tiny(36)
        eps_t = tiny(1)
        one_t = tiny(1)
        lg = tiny(NT * 36).rearrange("p (i n) -> p i n", i=NT)
        wcomb = tiny(2 * NT).rearrange("p (a i) -> p a i", a=2)
        rto = [2048]

        def rtt(n):
            rto[0] += n
            return pr[:, rto[0] - n:rto[0]]

        gmax, gs = rtt(NT), rtt(NT)
        ge = rtt(NT * NG).rearrange("p (i g) -> p i g", i=NT)
        goh = rtt(NT * NG).rearrange("p (i g) -> p i g", i=NT)
        vmx = rtt(NT)
        lm = rtt(NT * NE).rearrange("p (i g e) -> p i g e", i=NT, g=NG)
        ls = rtt(NT * EPG).rearrange("p (i e) -> p i e", i=NT)
        ls2 = rtt(NT * EPG).rearrange("p (i e) -> p i e", i=NT)
        m12 = rtt(2 * NT).rearrange("p (a i) -> p a i", a=2)
        eq = rtt(NT * EPG).rearrange("p (i e) -> p i e", i=NT)
        oh = rtt(2 * NT * EPG).rearrange("p (a i e) -> p a i e", a=2, i=NT)
        dd = rtt(NT)
        ed = rtt(NT)
        CC = rtt(2 * NT * NE).rearrange("p (a i n) -> p a i n", a=2, i=NT)
        Cs = rtt(NT * NE).rearrange("p (i n) -> p i n", i=NT)
        tmpC = rtt(2 * NT * NE).rearrange("p (a i n) -> p a i n", a=2, i=NT)
        rk = rtt(6 * NE).rearrange("p (i n) -> p i n", i=6)
        rsel, esel, osel = (rtt(2 * NT).rearrange("p (a i) -> p a i", a=2) for _ in range(3))
        nxk = rtt(NE * KMAX).rearrange("p (n k) -> p n k", n=NE)
        nx, inc, off = rtt(NE), rtt(NE), rtt(NE)
        qk_ = rtt(2 * NT * KMAX).rearrange("p (a k) -> p a k", k=KMAX)
        qq, pos, blk, isov, slotf = (rtt(2 * NT) for _ in range(5))
        Bm = ptb[:, 0, 0:2 * NT * NBLK].rearrange("p (a n) -> p a n", n=NBLK)
        Am = ptb[:, 1, 0:2 * NT * SLOTS].rearrange("p (a n) -> p a n", n=SLOTS)
        xef = rtt(XBLK)
        xcmp = hb
        xcm = r1[:, 5632:5632 + XBLK * NE].rearrange("p (x n) -> p x n", n=NE)
        lbl = sb("lbl", [P, 2, HH])
        sidx = sb("sidx", [P, 2 * NT], I32)
        idx = sb("idx", [SLOTS, NBLK], I32)
        stage = sb("stage", [SLOTS, 2], I32)
        xei = sb("xei", [1, XBLK], I32)
        nov = sb("nov", [1, 1], I32)

        zrow = AT[:, :, :, :].rearrange("p h j t -> p (h j t)")[:, 0:2 * D]

        ps = ctx.enter_context(nc.psum_tensor("ps", [P, 4096], F32))

        def slab(n):
            return ps[:, (n % 4) * 1024:(n % 4 + 1) * 1024]

        def job_slab(job):
            return slab(JOBS[job])

        def wide(job):
            return job_slab(job)[:, 432:432 + LT]

        xrow = nc.dram_tensor("xrow", (LT, D), F32, kind="Internal").ap()
        yrow = nc.dram_tensor("yrow", (NBLK * SLOTS, D), F32, kind="Internal").ap()

        def bc(ap, axis, n):
            ap = ap.unsqueeze(axis)
            shape = list(ap.shape)
            shape[axis] = n
            return ap.broadcast_to(shape)

        xslices = [(0, 0, NMETA, "meta", 0), (0, NMETA, 64, "x", 0)] + [
            (i, 0, TS[i], "x", T0[i] - NMETA) for i in range(1, NT)]
        block = ctx.enter_context(nc.Block())

        def settle(eng):
            eng.sem_inc(sem["settled"], 1)

        @block.sync
        def _(sp):
            sp.dma_start(consts[:, :], a["consts"]).then_inc(sem["const_load"], 16)
            sp.dma_start(dn_ring[:, 0, 0:LEVELS * P], a["level_masks"]).then_inc(sem["const_load"], 16)
            sp.dma_start(lbl[:, :, :].rearrange("p a h -> p (a h)"), a["hgrn_lb_logits"]).then_inc(sem["const_load"], 16)
            for i, r, n, src, s0 in xslices:
                s = a["meta_tokens"] if src == "meta" else a["x"][s0:s0 + n, :]
                sp.dma_start(h[r:r + n, i, :], s).then_inc(sem["x_load"], 16)

            w_in = a["w_in"].rearrange("(l p c) n -> l p c n", l=DEPTH, p=P)

            with sp.Fori(0, DEPTH) as L:
                def at(name, k):
                    return sem[name], L * PER[name] + (START.get(name, 0) + k)

                def rows(name, per, r):
                    w = a[name]
                    return w[bass.ds(L * per + r, P), :]

                def load_chunk(n, name):
                    slot = gu_ring[:, n % 2, :]
                    if n >= 2:
                        sp.wait_ge(*at("pe_done", LAST[CHUNKS[n - 2]] + 1))
                    else:
                        sp.wait_ge(*at("g_done", 0))
                    settle(sp)
                    if name in ("wa", "wb"):
                        w = a["w_branch_hgrn" if name == "wa" else "w_branch_dsa"]
                        sp.dma_start(slot.rearrange("p (c n) -> p c n", c=4),
                                     w[bass.ds(L * 512, 512), :].rearrange("(c p) n -> p c n", p=P)).then_inc(
                                         sem[f"gu{n % 2}"], 16)
                    elif name[:2] == "wo":
                        c0 = 512 * int(name[2])
                        sp.dma_start(slot.rearrange("p (c n) -> p c n", c=8),
                                     a["w_out"][bass.ds(L * D, D), c0:c0 + 512].rearrange("(c p) n -> p c n", p=P)).then_inc(
                                         sem[f"gu{n % 2}"], 16)
                    elif name == "ro":
                        sp.dma_start(slot[:, 0:288].rearrange("p (c n) -> p c n", c=8),
                                     a["router_w"][bass.ds(L * D, D), :].rearrange("(p c) n -> p c n", p=P)).then_inc(
                                         sem[f"gu{n % 2}"], 16)
                    else:
                        c0, nn = {"k3": (C_IK, 40), "k2": (C_AK, 512), "k1": (C_AQ, 512), "hi": (C_HI, 512),
                                  "hf": (C_HF, 512), "hq": (C_HQ, 512), "hg": (C_HG, 512), "ga0": (C_GA, 512),
                                  "ga1": (C_GA + 512, 512), "gb0": (C_GB, 512), "gb1": (C_GB + 512, 512)}[name]
                        sp.dma_start(slot[:, 0:8 * nn].rearrange("p (c n) -> p c n", c=8),
                                     a["w_in"][bass.ds(L * D, D), c0:c0 + nn].rearrange("(p c) n -> p c n", p=P)).then_inc(
                                         sem[f"gu{n % 2}"], 16)

                def load_expert(e, u):
                    slot = gu_ring[:, u, :]
                    for m, name in enumerate(("w_expert_gate", "w_expert_up")):
                        sp.dma_start(slot[:, m * 2048:(m + 1) * 2048],
                                     a[name][bass.ds((L * NE + e) * D, D), :].rearrange("(p c) f -> p (c f)", p=P)).then_inc(
                                         sem[f"gu{u}"], 16)

                def load_down(e, u):
                    sp.dma_start(dn_ring[:, u, :].rearrange("p (j n) -> p j n", j=2),
                                 a["w_expert_down"][bass.ds((L * NE + e) * FF, FF), :].rearrange("(j p) n -> p j n", p=P)).then_inc(
                                     sem[f"dn{u}"], 16)

                for n, name in enumerate(CHUNKS):
                    load_chunk(n, name)
                settle(sp)
                for u in range(2):
                    sp.wait_ge(*at("pe_done", LAST[CHUNKS[len(CHUNKS) - 2 + u]] + 1))
                    load_expert(u, u)
                    sp.wait_ge(*at("d_done", 0))
                    load_down(u, u)
                with sp.Fori(1, NE // 2) as ep:
                    for u in range(2):
                        e = ep * 2 + u
                        sp.wait_ge(*at("g_done", e - 1))
                        load_expert(e, u)
                        sp.wait_ge(*at("d_done", e - 1))
                        load_down(e, u)

        @block.tensor
        def _(pe):
            mm, tr = nc.tensor.matmul, nc.tensor.transpose
            pe.wait_ge(sem["const_load"], 48)
            pe.wait_ge(sem["init"], INITS)
            with pe.Fori(0, DEPTH) as L:
                def at(name, k):
                    return sem[name], L * PER[name] + (START.get(name, 0) + k)

                def take(job):
                    n = JOBS[job]
                    pe.wait_ge(*at(f"free{n % 4}", n // 4))
                    return job_slab(job)

                def freed(job):
                    pe.wait_ge(*at(f"free{JOBS[job] % 4}", JOBS[job] // 4 + 1))

                def chunk(name):
                    n = CHUNKS.index(name)
                    pe.wait_ge(*at(f"gu{n % 2}", 16 * (n // 2 + 1)))
                    return gu_ring[:, n % 2, :]

                def norm_transposes(job, k0):
                    for i in range(NT):
                        s = take((job, i))
                        pe.wait_ge(*at("xn_ready", k0 + i + 1))
                        settle(pe)
                        for c in range(KC):
                            last = tr(s[:, c * P:c * P + TS[i]], xn[0:TS[i], i % 2, c:D:KC], ident[0:TS[i], 0:TS[i]])
                        last.then_inc(sem["pe_done"], 1)

                def token_major(name, n):
                    w = chunk(name)[:, 0:KC * n].rearrange("p (c n) -> p c n", c=KC)
                    for i in range(NT):
                        s = take((name, i))
                        for c in range(KC):
                            last = mm(s[0:TS[i], 0:n], xnT[:, c, T0[i]:T0[i] + TS[i]], w[:, c, :],
                                      start=c == 0, stop=c == KC - 1)
                        last.then_inc(sem["pe_done"], 1)

                def feature_major(job, lhs, rhs, nk):
                    take(job)
                    o = wide(job)
                    for lo, hi in ((0, 80), (80, LT)):
                        for c in range(nk):
                            last = mm(o[:, lo:hi], lhs(c), rhs(c, lo, hi), start=c == 0, stop=c == nk - 1)
                    last.then_inc(sem["pe_done"], 1)

                def project(name, key, j0, n):
                    w = chunk(name)[:, 0:KC * 512].rearrange("p (c n) -> p c n", c=KC)
                    for j in range(n):
                        feature_major((key, j0 + j), lambda c: w[:, c, j * P:(j + 1) * P],
                                      lambda c, lo, hi: xnT[:, c, lo:hi], KC)

                norm_transposes("xt", 0)
                freed(("xt", NT - 1))
                token_major("k3", 40)
                token_major("k2", 512)
                token_major("k1", 512)
                token_major("hi", 512)
                pe.wait_ge(*at("rope_ready", 1))
                for i in range(NT):
                    s = take(("it", i))
                    settle(pe)
                    n = TS[i]
                    idn = ident[0:n, 0:n]
                    tr(s[:, 0:n], qtok[0:n, i, 768:896], idn)
                    tr(s[:, 128:128 + n], qtok[0:n, i, 896:1024], idn)
                    tr(s[:, 256:256 + n], ikdup[0:n, i, :, :].rearrange("p r d -> p (r d)"), idn).then_inc(sem["pe_done"], 1)
                    s = take(("at", i))
                    settle(pe)
                    for c in range(4):
                        tr(s[:, c * P:c * P + n], qtok[0:n, i, c * P:(c + 1) * P], idn)
                    for g in range(2):
                        last = tr(s[:, (4 + g) * P:(4 + g) * P + n], kdup[0:n, i, g, :, :].rearrange("p r d -> p (r d)"), idn)
                    last.then_inc(sem["pe_done"], 1)
                project("hf", "hf", 0, 4)
                project("hq", "hq", 0, 4)

                freed(("it", NT - 1))
                freed(("at", NT - 1))
                for i in range(1, NT):
                    for hd in range(IH):
                        take(("ix", i, hd))
                        o = wide(("ix", i, hd))
                        r = 32 * (hd % 4)
                        for lo, hi in ((0, 80), (80, W[i])):
                            last = mm(o[0:TS[i], lo:hi], ixT[r:r + 32, hd // 4, T0[i]:T0[i] + TS[i]], ixT[r:r + 32, 2, lo:hi],
                                      start=True, stop=True, tile_position=(r, 0))
                        last.then_inc(sem["pe_done"], 1)

                freed(("hq", HH - 1))
                pe.wait_ge(*at("f_done", HH))
                for hd in range(HH):
                    for l in range(LEVELS):
                        s = take(("lv", hd, l))
                        if l > 0:
                            pe.wait_ge(*at("qe_ready", hd * 7 + l))
                        u = (hd * 7 + l - 1) % 2
                        for j in range(NT):
                            k_, q_ = (hk[:, hd, j, :], hq[:, hd, j, :]) if l == 0 else (
                                ke[:, u, j * P:(j + 1) * P], qe[:, u, j * P:(j + 1) * P])
                            last = mm(s[:, j * P:(j + 1) * P], k_, q_, start=True, stop=True)
                        last.then_inc(sem["pe_done"], 1)
                pe.wait_ge(*at("qb_ready", HH))
                pe.wait_ge(*at("kw_ready", HH))
                freed(("lv", HH - 1, LEVELS - 1))
                for j in range(NT):
                    n = TS[j]
                    s = take(("kt", j))
                    settle(pe)
                    for hd in range(HH):
                        last = tr(s[0:n, hd * P:(hd + 1) * P], hk[:, hd, j, 0:n], ident[:, :])
                    last.then_inc(sem["pe_done"], 1)
                    s = take(("ot", j))
                    if j > 0:
                        freed(("su", j - 1))
                    for hd in range(HH):
                        o = s[:, hd * P:hd * P + n]
                        if j > 0:
                            mm(o, S[:, hd, :], hq[:, hd, j, 0:n], start=True, stop=False)
                        last = mm(o, vH[0:n, j, hd * P:(hd + 1) * P], AT[0:n, hd, j, 0:n], start=j == 0, stop=True)
                    last.then_inc(sem["pe_done"], 1)
                    if j < NT - 1:
                        s = take(("su", j))
                        freed(("kt", j))
                        for hd in range(HH):
                            last = mm(s[:, hd * P:(hd + 1) * P], kwT[0:n, j % 2, hd * P:(hd + 1) * P],
                                      vH[0:n, j, hd * P:(hd + 1) * P], start=True, stop=True)
                        last.then_inc(sem["pe_done"], 1)
                project("hg", "hg", 0, 4)
                for hd in range(HH):
                    s = take(("on", hd))
                    pe.wait_ge(*at("sq_ready", hd + 1))
                    mm(s[:, 0:512], ones[:, :], osq[:, hd, 0:512], start=True, stop=True)
                    mm(s[:, 512:640], ones[:, :], osq[:, hd, 512:640], start=True, stop=True).then_inc(sem["pe_done"], 1)
                project("ga0", "ga", 0, 4)
                project("ga1", "ga", 4, 4)
                w = chunk("wa").rearrange("p (c n) -> p c n", c=4)
                pe.wait_ge(*at("ya_ready", 1))
                yflat = [hq[:, k, :, :].rearrange("p j t -> p (j t)") for k in range(HH)]
                for c in range(8):
                    feature_major(("wa", c), lambda k: w[:, k, c * P:(c + 1) * P],
                                  lambda k, lo, hi: yflat[k][:, 0:80] if lo == 0 else yflat[k][:, P:P + LT - 80], HH)

                def scores(i, g):
                    for hd in range(4 * g, 4 * g + 4):
                        take(("qk", i, hd))
                        if TS[i] <= 64:
                            settle(pe)
                        o = wide(("qk", i, hd))
                        r = 64 * (hd % 2)
                        for lo, hi in ((0, 80), (80, W[i])):
                            if lo < hi:
                                last = mm(o[0:TS[i], lo:hi], aqk[r:r + 64, hd // 2, T0[i]:T0[i] + TS[i]],
                                          aqk[r:r + 64, 4 + g, lo:hi], start=True, stop=True, tile_position=(r, 0))
                        last.then_inc(sem["pe_done"], 1)

                scores(0, 0)
                groups = [(i, g) for i in range(NT) for g in range(2)]
                kts = 0
                for n_, (i, g) in enumerate(groups):
                    if n_ + 1 < len(groups):
                        scores(*groups[n_ + 1])
                    n = TS[i]
                    pe.wait_ge(*at("pn_ready", 4 * n_ + 4))
                    for k in range(i + 1):
                        s = take(("pt", i, g, k))
                        settle(pe)
                        for r in range(4):
                            hd = 4 * g + (0, 2, 1, 3)[r]
                            last = tr(s[0:TS[k], r * n:(r + 1) * n], pb[0:n, hd, T0[k]:T0[k] + TS[k]], ident[0:n, 0:n])
                        last.then_inc(sem["pe_done"], 1)
                    s = take(("pv", i, g))
                    for k in range(i + 1):
                        freed(("pt", i, g, k))
                        settle(pe)
                        for par in range(2):
                            last = mm(s[64 * par:64 * par + 64, 0:2 * n], vA[0:TS[k], k, g * AD:(g + 1) * AD],
                                      ptq[0:TS[k], (kts + k) % 4, par * 2 * n:(par + 1) * 2 * n],
                                      start=k == 0, stop=k == i, tile_position=(0, 64 * par))
                        if k < i:
                            last.then_inc(sem["pt_used"], 1)
                    last.then_inc(sem["pe_done"], 1)
                    kts += i + 1
                project("gb0", "gb", 0, 4)
                project("gb1", "gb", 4, 4)
                w = chunk("wb").rearrange("p (c n) -> p c n", c=4)
                freed(("pv", NT - 1, 1))
                for c in range(8):
                    feature_major(("wb", c), lambda k: w[:, k, c * P:(c + 1) * P], lambda k, lo, hi: ybT[:, k, lo:hi], 4)
                for half in range(2):
                    w = chunk(f"wo{half}").rearrange("p (c n) -> p c n", c=KC)
                    pe.wait_ge(*at("mg_ready", 8))
                    for i in range(NT):
                        s = take(("wo", half, i))
                        for c in range(KC):
                            last = mm(s[0:TS[i], 0:512], sga[:, c, T0[i]:T0[i] + TS[i]], w[:, c, :],
                                      start=c == 0, stop=c == KC - 1)
                        last.then_inc(sem["pe_done"], 1)

                norm_transposes("xt2", NT)
                freed(("xt2", NT - 1))
                w = chunk("ro")[:, 0:288].rearrange("p (c n) -> p c n", c=KC)
                for i in range(NT):
                    s = take(("ro", i))
                    for c in range(KC):
                        last = mm(s[0:TS[i], 0:36], xnT[:, c, T0[i]:T0[i] + TS[i]], w[:, c, :], start=c == 0, stop=c == KC - 1)
                    last.then_inc(sem["pe_done"], 1)
                s = take(("rank",))
                pe.wait_ge(*at("c_ready", 1))
                for i in range(NT + 1):
                    for k in range(min(i + 1, NT)):
                        last = mm(s[:, i * NE:(i + 1) * NE], (tri if k == i else ones)[0:TS[k], :], Cs[0:TS[k], k, :],
                                  start=k == 0, stop=k == min(i, NT - 1))
                last.then_inc(sem["pe_done"], 1)
                s = take(("slot",))
                pe.wait_ge(*at("ab_ready", 1))
                for n in range(2 * NT):
                    last = mm(s[0:SLOTS, 0:NBLK], Am[0:TS[n % NT], n, :], Bm[0:TS[n % NT], n, :], start=n == 0, stop=n == 2 * NT - 1)
                last.then_inc(sem["pe_done"], 1)

                for s_ in range(4):
                    pe.wait_ge(*at(f"free{s_}", PER_SLAB[s_]))

                def transposes(e, u):
                    pe.wait_ge(*at(f"xg{u}", (e - u) * 8 + 16))
                    settle(pe)
                    for c in range(KC):
                        last = tr(slab(0)[:, u * 512 + c * SLOTS:u * 512 + (c + 1) * SLOTS], xg[0:SLOTS, u, c:D:KC], ident[0:SLOTS, 0:SLOTS])
                    last.then_inc(sem["t_done"], 1)

                def gate_up(e, u):
                    pe.wait_ge(*at("xt_done", e + 1))
                    pe.wait_ge(*at(f"gu{u}", 16 * len(CHUNKS) // 2 + (e - u) * 16 + 32))
                    w = gu_ring[:, u, :].rearrange("p (m c f) -> p m c f", m=2, c=KC)
                    for m in range(2):
                        for j in range(2):
                            o = slab(1)[:, u * 512 + (2 * m + j) * SLOTS:u * 512 + (2 * m + j + 1) * SLOTS]
                            for c in range(KC):
                                last = mm(o, w[:, m, c, j * P:(j + 1) * P], xgT[:, u, c, :], start=c == 0, stop=c == KC - 1)
                    last.then_inc(sem["g_done"], 1)

                def down(e, u):
                    pe.wait_ge(*at("am_done", e + 1))
                    pe.wait_ge(*at(f"dn{u}", (e - u) * 8 + 16))
                    settle(pe)
                    w = dn_ring[:, u, :].rearrange("p (j n) -> p j n", j=2)
                    for half in range(2):
                        for j in range(2):
                            last = mm(slab(2 + u)[0:SLOTS, half * 512:(half + 1) * 512], am[:, u, j, :],
                                      w[:, j, half * 512:(half + 1) * 512], start=j == 0, stop=j == 1)
                    last.then_inc(sem["d_done"], 1)

                transposes(0, 0)
                transposes(1, 1)
                gate_up(0, 0)
                gate_up(1, 1)
                down(0, 0)
                with pe.Fori(1, NE // 2) as ep:
                    for u in range(2):
                        e = ep * 2 + u
                        pe.wait_ge(*at("xt_done", e - 1))
                        transposes(e, u)
                        pe.wait_ge(*at("am_done", e - 1))
                        gate_up(e, u)
                        pe.wait_ge(*at("y_done", e - 2))
                        down(e - 1, 1 - u)
                pe.wait_ge(*at("y_done", NE - 2))
                down(NE - 1, 1)

                pe.wait_ge(*at("base_ready", 1))
                settle(pe)
                n_over = pe.value_load(nov[0:1, 0:1], min_val=0, max_val=XBLK)
                with pe.If(n_over > 0):
                    with pe.Fori(0, XBLK) as x:
                        def ov(name, k=1):
                            return sem[name], (L * XBLK + x) * OV[name] + k * OV[name]

                        pe.wait_ge(*ov("ov_x"))
                        settle(pe)
                        for c in range(KC):
                            last = tr(slab(0)[:, c * SLOTS:(c + 1) * SLOTS], xg[0:SLOTS, 0, c:D:KC], ident[0:SLOTS, 0:SLOTS])
                        last.then_inc(sem["ov_t"], 1)
                        pe.wait_ge(*ov("ov_xt"))
                        pe.wait_ge(*ov("ov_w"))
                        w = ovw[:, 0:4096].rearrange("p (m c f) -> p m c f", m=2, c=KC)
                        for m in range(2):
                            for j in range(2):
                                o = slab(1)[:, (2 * m + j) * SLOTS:(2 * m + j + 1) * SLOTS]
                                for c in range(KC):
                                    last = mm(o, w[:, m, c, j * P:(j + 1) * P], xgT[:, 0, c, :], start=c == 0, stop=c == KC - 1)
                        last.then_inc(sem["ov_g"], 1)
                        pe.wait_ge(*ov("ov_am"))
                        settle(pe)
                        w = ovw[:, 4096:6144].rearrange("p (j n) -> p j n", j=2)
                        for half in range(2):
                            for j in range(2):
                                last = mm(slab(2)[0:SLOTS, half * 512:(half + 1) * 512], am[:, 0, j, :],
                                          w[:, j, half * 512:(half + 1) * 512], start=j == 0, stop=j == 1)
                        last.then_inc(sem["ov_d"], 1)
                with pe.Else():
                    for name in ("ov_t", "ov_g", "ov_d"):
                        pe.sem_inc(sem[name], XBLK)

        @block.vector
        def _(dve):
            V = nc.vector
            tt, ts, stt = V.tensor_tensor, V.tensor_scalar, V.scalar_tensor_tensor
            for r in (r1, r2):
                V.memset(r[:, :], 0.0).then_inc(sem["init"], 1)
            V.memset(small[:, :], 1.0).then_inc(sem["init"], 1)
            V.memset(sc[:, :, :], 0.0).then_inc(sem["init"], 1)
            for name in ("free0", "free1", "free2", "free3", "t_done", "g_done", "d_done", "y_done", "am_done", "cb_done"):
                dve.sem_inc(sem[name], START[name])
            dve.wait_ge(sem["const_load"], 48)
            V.tensor_copy(lvm[:, :, :].rearrange("p l t -> p (l t)"), dn_ring[:, 0, 0:LEVELS * P]).then_inc(sem["init"], 1)
            dve.wait_ge(sem["init"], INITS)
            V.tensor_copy(sc[:, 0, 4:4 + W[0]], mask0).then_inc(sem["init"], 1)
            V.memset(lb, 0.0).then_inc(sem["init"], 1)
            tt(lb1, lbl[:, 0, :], lbl[:, 1, :], ALU.subtract).then_inc(sem["init"], 1)
            dve.wait_ge(sem["lbe"], 1)
            V.tensor_scalar_add(lb1, lb1, 1.0).then_inc(sem["init"], 1)
            dve.wait_ge(sem["init"], INITS + 4)
            V.reciprocal(lb1, lb1).then_inc(sem["init"], 1)
            dve.wait_ge(sem["init"], INITS + 5)

            with dve.Fori(0, DEPTH) as L:
                n_ = [0]

                def at(name, k):
                    return sem[name], L * PER[name] + (START.get(name, 0) + k)

                def chained(ins):
                    n_[0] += 1
                    ins.then_inc(sem["dve"], 1)
                    return n_[0]

                def after(n):
                    dve.wait_ge(*at("dve", n))

                def link(ins):
                    after(chained(ins))

                def done(job):
                    dve.wait_ge(*at("pe_done", JOBS[job] + 1))

                def free(job):
                    return sem[f"free{JOBS[job] % 4}"], 1

                def freed(job):
                    dve.wait_ge(*at(f"free{JOBS[job] % 4}", JOBS[job] // 4 + 1))

                def norm_rows(k0):
                    dve.wait_ge(*at("rms_ready", 1 + (k0 > 0)))
                    dve.wait_ge(*at("g_load", 16 * (1 + (k0 > 0))))
                    link(V.reciprocal(rstd, rms))
                    for i in range(NT):
                        n = TS[i]
                        if i >= 2:
                            done(("xt2" if k0 else "xt", i - 2))
                            if k0:
                                dve.wait_ge(*at(f"xw{i % 2}", 16 * (i // 2)))
                        stt(xn[0:n, i % 2, :], h[0:n, i, :], rstd[0:n, i:i + 1], gB[0:n, :], ALU.mult, ALU.mult).then_inc(
                            sem["xn_ready"], 1)

                norm_rows(0)

                dve.wait_ge(*at("par_load", 48))
                link(ts(llb, lb, 1e-18, None, ALU.max))
                ts(omlb, lb, -1.0, 1.0, ALU.mult, ALU.add).then_inc(sem["lb_ready"], 1)
                link(ts(dec[:, :, 0], lb, 1e-18, NEG, ALU.is_lt, ALU.mult))
                dve.wait_ge(*at("lb_ln", 1))
                link(tt(llb, llb, dec[:, :, 0], ALU.add))

                ik = qtok[:, :, 1024:1056]
                for i in range(NT):
                    freed(("k3", i))
                ikq = rt[:, 0:NT * ID].rearrange("p (i d) -> p i d", i=NT)
                link(tt(ikq, ik, ik, ALU.mult))
                V.tensor_reduce(kss, ikq, AX, ALU.add).then_inc(sem["ksq_ready"], 1)
                ts(iw, qtok[:, :, 1056:1064], IH ** -0.5 * ID ** -0.5, None, ALU.mult)
                dve.wait_ge(*at("ksq_ready", 1))

                def rope(x, heads, tab, half):
                    x1, x2 = x[:, :, :, 0:half], x[:, :, :, half:2 * half]
                    c, s = bc(tab[:, 0], 2, heads), bc(tab[:, 1], 2, heads)
                    n = NT * heads * half
                    t = [rt[:, k * n:(k + 1) * n].rearrange("p (i h d) -> p i h d", i=NT, h=heads) for k in range(4)]
                    tt(t[0], x1, c, ALU.mult)
                    tt(t[1], x2, s, ALU.mult)
                    tt(t[2], x2, c, ALU.mult)
                    link(tt(t[3], x1, s, ALU.mult))
                    tt(x1, t[0], t[1], ALU.subtract)
                    link(tt(x2, t[2], t[3], ALU.add))

                for i in range(NT):
                    freed(("k2", i))
                    freed(("k1", i))
                V.tensor_copy(vA[:, :, :], qtok[:, :, 640:768])
                rope(qtok[:, :, 0:640].rearrange("p i (h d) -> p i h d", d=AD), 10, rope_a, 8)
                for g in range(2):
                    V.tensor_copy(kdup[:, :, g, :, :], bc(qtok[:, :, 512 + g * AD:512 + (g + 1) * AD], 2, 2))
                dve.wait_ge(*at("kn_ready", 1))
                link(V.reciprocal(krms, krms))
                link(tt(ik, ik, bc(krms, 2, ID), ALU.mult))
                link(tt(ik, ik, bc(ik_g, 1, NT), ALU.mult))
                rope(qtok[:, :, 768:1056].rearrange("p i (h d) -> p i h d", d=ID), 9, rope_i, 4)
                V.tensor_copy(ikdup[:, :, :, :], bc(ik, 2, 4)).then_inc(sem["rope_ready"], 1)

                fb = pr[:, :].rearrange("p (k u t) -> p k u t", k=4, u=2)
                done(("at", NT - 1))
                pads = r1[:, :].rearrange("p (a j t) -> p a j t", a=3 * HH, j=NT)
                V.memset(pads[:, :, 0, TS[0]:], 0.0)
                link(V.memset(pads[:, :, NT - 1, TS[NT - 1]:], 0.0))

                def gate_in(j):
                    done(("hf", j))
                    z = wide(("hf", j))
                    ts(fb[:, 0, j % 2, :], z, -1.0, 40.0, ALU.mult, ALU.min).then_inc(sem["e_ready"], 1)
                    ts(fb[:, 1, j % 2, :], z, -1.0, 40.0, ALU.mult, ALU.max).then_inc(*free(("hf", j)))

                def padded(dst, j):
                    flat = dst[:, j, :, :].rearrange("p j t -> p (j t)")
                    return (flat[:, 0:80], slice(0, 80)), (flat[:, P:P + LT - 80], slice(80, LT))

                def gate_out(j):
                    e, ov, l1, l2 = (fb[:, k, j % 2, :] for k in range(4))
                    dve.wait_ge(*at("lnf_ready", j + 1))
                    link(tt(l2, l2, l1, ALU.subtract))
                    n1 = chained(stt(l2, l2, 40.0, ov, ALU.add, ALU.subtract))
                    n2 = chained(V.tensor_scalar_add(l1, e, 1.0))
                    after(n2)
                    n2 = chained(V.reciprocal(l1, l1))
                    for dst, cols in padded(hb, j):
                        ts(dst, l2[:, cols], llb[:, j:j + 1], None, ALU.max)
                    after(n2)
                    for dst, cols in padded(hk, j):
                        last = stt(dst, e[:, cols], omlb[:, j:j + 1], l1[:, cols], ALU.mult, ALU.mult)
                    link(last)
                    flat = hb[:, j, :, :].rearrange("p j t -> p (j t)")
                    V.tensor_tensor_scan(flat, reset, flat, 0.0, ALU.mult, ALU.add).then_inc(sem["f_done"], 1)

                gate_in(0)
                for j in range(HH):
                    if j + 1 < HH:
                        gate_in(j + 1)
                    gate_out(j)

                for i in range(1, NT):
                    n = TS[i]
                    V.memset(sc[0:n, i, 0:4], SENT)
                    for hd in range(IH):
                        m = (i - 1) * IH + hd
                        freed(("ix", i, hd))
                        if hd > 0:
                            dve.wait_ge(*at("rel_used", m))
                        acc, r_, w_ = sc[0:n, i, 4:4 + W[i]], rel[0:n, m % 2, 0:W[i]], iw[0:n, i, hd:hd + 1]
                        (ts(acc, r_, w_, None, ALU.mult) if hd == 0 else stt(acc, r_, w_, acc, ALU.mult, ALU.add)).then_inc(
                            sem["rel_used"], 1)
                    if i < NT - 1:
                        dve.wait_ge(*at("rel_used", i * IH))
                        V.memset(sc[0:64, i, 4 + W[i] - 64:4 + W[i]], HIDDEN)

                def differences(m):
                    hd, l = m // 7, m % 7 + 1
                    half = 2 ** (l - 1)
                    if m >= 2:
                        dve.wait_ge(*at("qe_ready", m - 1))
                    b = hb[:, hd, :, :].rearrange("p j t -> p (j t)").rearrange("p (n a t) -> p n a t", a=2, t=half)
                    e = ebuf[:, m % 2, :].rearrange("p (n a t) -> p n a t", a=2, t=half)
                    mid = b[:, :, 0, half - 1:half].broadcast_to([P, 640 // (2 * half), half])
                    tt(e[:, :, 1, :], b[:, :, 1, :], mid, ALU.subtract)
                    tt(e[:, :, 0, :], mid, b[:, :, 0, :], ALU.subtract).then_inc(sem["d_ready"], 1)

                def take_level(hd, l):
                    done(("lv", hd, l))
                    if l > 0:
                        freed(("lv", hd, l - 1))
                    settle(dve)
                    V.copy_predicated(AT[:, hd, :, :], bc(lvm[:, l, :], 1, NT),
                                      job_slab(("lv", hd, l))[:, 0:640].rearrange("p (j t) -> p j t", j=NT)).then_inc(
                                          *free(("lv", hd, l)))

                dve.wait_ge(*at("f_done", HH))
                dve.wait_ge(sem["y_init"], 16 * XBLK * SLOTS // (2 * P))
                differences(0)
                differences(1)
                for m in range(HH * 7):
                    if m % 7 == 0:
                        take_level(m // 7, 0)
                    take_level(m // 7, m % 7 + 1)
                    if m + 2 < HH * 7:
                        differences(m + 2)

                for hd in range(HH):
                    if hd >= 2:
                        dve.wait_ge(*at("kw_ready", hd - 1))
                    else:
                        dve.wait_ge(*at("qe_ready", 27 + hd))
                    b = hb[:, hd, :, :]
                    tt(ebuf[:, hd % 2, :].rearrange("p (j t) -> p j t", j=NT), b[:, :, P - 1:P].broadcast_to([P, NT, P]), b,
                       ALU.subtract).then_inc(sem["d_ready"], 1)
                    dve.wait_ge(*at("ex_ready", 28 + 2 * hd + 1))
                    q_ = hq[:, hd, :, :].rearrange("p j t -> p (j t)")
                    k_ = hk[:, hd, :, :].rearrange("p j t -> p (j t)")
                    tt(q_, q_, qe[:, hd % 2, :], ALU.mult).then_inc(sem["qb_ready"], 1)
                    dve.wait_ge(*at("ex_ready", 28 + 2 * hd + 2))
                    tt(k_, k_, ebuf[:, hd % 2, :], ALU.mult).then_inc(sem["kw_ready"], 1)

                dve.wait_ge(*at("ex_ready", 37))
                for j in range(NT - 1):
                    done(("su", j))
                    s = job_slab(("su", j))
                    if j == 0:
                        V.tensor_copy(S[:, :, :].rearrange("p h e -> p (h e)"), s[:, 0:512]).then_inc(*free(("su", j)))
                    else:
                        for hd in range(HH):
                            last = stt(S[:, hd, :], S[:, hd, :], dec[:, hd, j:j + 1], s[:, hd * P:(hd + 1) * P], ALU.mult, ALU.add)
                        last.then_inc(*free(("su", j)))

                for hd in range(HH):
                    freed(("on", hd))
                    q_, k_, b_ = (r[:, hd, :, :].rearrange("p j t -> p (j t)") for r in (hq, hk, hb))
                    link(V.reciprocal(b_, b_))
                    link(stt(q_, q_, hn_g[:, hd:hd + 1], b_, ALU.mult, ALU.mult))
                    last = tt(q_, q_, k_, ALU.mult)
                    if hd == HH - 1:
                        last.then_inc(sem["ya_ready"], 1)

                prev = {}
                for r in range((TOPK + 4) // 8):
                    cur = {}
                    for i in range(1, NT):
                        if r:
                            after(prev[i])
                            settle(dve)
                        cur[i] = chained(V.max(top8[0:TS[i], i - 1, :], sc[0:TS[i], i, 0:4 + W[i]]))
                    for i in range(1, NT):
                        after(cur[i])
                        settle(dve)
                        s_ = sc[0:TS[i], i, 0:4 + W[i]]
                        prev[i] = chained(V.match_replace(s_, top8[0:TS[i], i - 1, :], s_, REPL))
                for i in range(1, NT):
                    after(prev[i])
                    s_ = sc[0:TS[i], i, 4:4 + W[i]]
                    prev[i] = chained(ts(s_, s_, 0.5 * (REPL + HIDDEN), NEG, ALU.is_gt, ALU.mult))
                after(prev[NT - 1])

                for c in range(8):
                    freed(("ga", c))
                    done(("wa", c))
                    tt(sga[:, c, :], wide(("wa", c)), sga[:, c, :], ALU.mult).then_inc(*free(("wa", c)))

                def score_max(m):
                    i, hd = m // 8, m % 8
                    n = TS[i]
                    done(("qk", i, hd))
                    settle(dve)
                    V.tensor_tensor_reduce(out=pb[0:n, hd, 0:W[i]], in0=wide(("qk", i, hd))[0:n, 0:W[i]], in1=sc[0:n, i, 4:4 + W[i]],
                                           scale=1.0, scalar=SCALAR_MIN, op0=ALU.add, op1=ALU.max,
                                           accum_out=mx[0:n, hd:hd + 1]).then_inc(*free(("qk", i, hd)))
                    freed(("qk", i, hd))
                    ts(nmx[0:n, hd:hd + 1], mx[0:n, hd:hd + 1], -AD ** -0.5, None, ALU.mult).then_inc(sem["mx_ready"], 1)

                def normalise(m):
                    i, hd = m // 8, m % 8
                    n = TS[i]
                    dve.wait_ge(*at("p_ready", m + 1))
                    link(V.reciprocal(pinv[0:n, hd:hd + 1], psum_[0:n, hd:hd + 1]))
                    ts(pb[0:n, hd, 0:W[i]], pb[0:n, hd, 0:W[i]], pinv[0:n, hd:hd + 1], None, ALU.mult).then_inc(sem["pn_ready"], 1)

                score_max(0)
                score_max(1)
                for m in range(40):
                    if m + 2 < 40:
                        score_max(m + 2)
                    normalise(m)

                for c in range(8):
                    freed(("gb", c))
                    done(("wb", c))
                    tt(sgb[:, c, :], wide(("wb", c)), sgb[:, c, :], ALU.mult).then_inc(*free(("wb", c)))
                    freed(("wb", c))
                    tt(sga[:, c, :], sga[:, c, :], sgb[:, c, :], ALU.add).then_inc(sem["mg_ready"], 1)
                for half in range(2):
                    for i in range(NT):
                        n = TS[i]
                        done(("wo", half, i))
                        o = h[0:n, i, half * 512:(half + 1) * 512]
                        tt(o, job_slab(("wo", half, i))[0:n, 0:512], o, ALU.add).then_inc(*free(("wo", half, i)))

                norm_rows(NT)
                for i in range(NT):
                    done(("ro", i))
                    tt(lg[0:TS[i], i, :], job_slab(("ro", i))[0:TS[i], 0:36], rb[0:TS[i], :], ALU.add).then_inc(*free(("ro", i)))
                for i in range(NT):
                    freed(("ro", i))

                lgg, lge = lg[:, :, 0:NG], lg[:, :, NG:].rearrange("p i (g e) -> p i g e", g=NG)
                link(V.tensor_reduce(gmax, lgg, AX, ALU.max))
                tt(ge, lgg, bc(gmax, 2, NG), ALU.subtract).then_inc(sem["rt_ready"], 1)

                def first_of(x, mval, oh_, desc, nn, tmp):
                    link(tt(tmp, x, bc(mval, 2, nn), ALU.is_equal))
                    link(tt(tmp, tmp, bc(desc, 1, NT), ALU.mult))
                    link(V.tensor_reduce(vmx, tmp, AX, ALU.max))
                    link(tt(oh_, tmp, bc(vmx, 2, nn), ALU.is_equal))

                first_of(lgg, gmax, goh, descg, NG, goh)
                link(tt(lm, lge, bc(goh, 3, EPG), ALU.mult))
                link(V.tensor_reduce(ls, lm.rearrange("p i g e -> p i e g"), AX, ALU.add))
                link(V.tensor_reduce(m12[:, 0], ls, AX, ALU.max))
                first_of(ls, m12[:, 0], oh[:, 0], desce, EPG, eq)
                link(stt(ls2, oh[:, 0], NEG, ls, ALU.mult, ALU.add))
                link(V.tensor_reduce(m12[:, 1], ls2, AX, ALU.max))
                tt(dd, m12[:, 1], m12[:, 0], ALU.subtract).then_inc(sem["rt_ready"], 1)
                first_of(ls2, m12[:, 1], oh[:, 1], desce, EPG, eq)
                for c in range(2):
                    for g in range(NG):
                        last = tt(CC[:, c].rearrange("p i (g e) -> p i g e", g=NG)[:, :, g, :], bc(goh[:, :, g], 2, EPG), oh[:, c], ALU.mult)
                link(last)
                tt(Cs, CC[:, 0], CC[:, 1], ALU.add).then_inc(sem["c_ready"], 1)
                dve.wait_ge(*at("rt_exp", 2))
                link(V.tensor_reduce(gs, ge, AX, ALU.add))
                link(stt(gs, ed, 1.0, gs, ALU.add, ALU.mult))
                link(V.reciprocal(wcomb[:, 0], gs))
                link(tt(wcomb[:, 1], wcomb[:, 0], ed, ALU.mult))
                link(tt(tmpC, CC, bc(bc(ioe, 1, NT), 1, 2), ALU.mult))
                link(V.tensor_reduce(esel, tmpC, AX, ALU.add))
                done(("rank",))
                V.tensor_copy(rk.rearrange("p i n -> p (i n)"), job_slab(("rank",))[:, 0:6 * NE]).then_inc(*free(("rank",)))
                freed(("rank",))
                for c in range(2):
                    last = tt(tmpC[:, c], CC[:, c], rk[:, 0:NT, :], ALU.mult)
                link(last)
                link(V.tensor_reduce(rsel, tmpC, AX, ALU.add))
                link(tt(nxk, bc(rk[:, NT, :], 2, KMAX), bc(kthr, 1, NE), ALU.is_gt))
                link(V.tensor_reduce(nx, nxk, AX, ALU.add))
                link(V.tensor_tensor_scan(inc, ones[:, 0:NE], nx, 0.0, ALU.mult, ALU.add))
                link(tt(off, inc, nx, ALU.subtract))
                link(tt(tmpC, CC, bc(bc(off, 1, NT), 1, 2), ALU.mult))
                link(V.tensor_reduce(osel, tmpC, AX, ALU.add))
                r_, e_, o_ = (x.rearrange("p a i -> p (a i)") for x in (rsel, esel, osel))
                link(tt(qk_, bc(r_, 2, KMAX), bc(kthr, 1, 2 * NT), ALU.is_ge))
                link(V.tensor_reduce(qq, qk_, AX, ALU.add))
                link(stt(pos, qq, -float(SLOTS), r_, ALU.mult, ALU.add))
                link(ts(isov, qq, 1.0, None, ALU.min))
                link(tt(blk, o_, qq, ALU.add))
                link(stt(blk, blk, float(NE - 1), e_, ALU.add, ALU.subtract))
                link(tt(blk, blk, isov, ALU.mult))
                link(tt(blk, blk, e_, ALU.add))
                link(stt(slotf, blk, float(SLOTS), pos, ALU.mult, ALU.add))
                V.tensor_copy(sidx[:, :], slotf).then_inc(sem["sidx_ready"], 1)
                tt(Am, bc(io64, 1, 2 * NT), bc(pos, 2, SLOTS), ALU.is_equal)
                link(tt(Bm, bc(ioblk, 1, 2 * NT), bc(blk, 2, NBLK), ALU.is_equal))
                bm4 = Bm.rearrange("p (c i) n -> p c i n", c=2)
                tt(bm4[:, 0], bm4[:, 0], bc(tokid, 2, NBLK), ALU.mult)
                tt(bm4[:, 1], bm4[:, 1], bc(tokid, 2, NBLK), ALU.mult).then_inc(sem["ab_ready"], 1)
                link(tt(xcm, bc(inc, 1, XBLK), bc(ioblk[:, 0:XBLK], 2, NE), ALU.is_le))
                link(V.tensor_reduce(xef, xcm, AX, ALU.add))
                link(ts(xei[0:1, :], xef[0:1, :], float(NE - 1), None, ALU.min))
                V.tensor_copy(nov[0:1, 0:1], inc[0:1, NE - 1:NE]).then_inc(sem["base_ready"], 1)
                done(("slot",))
                V.tensor_copy(idx[:, :], job_slab(("slot",))[0:SLOTS, 0:NBLK]).then_inc(*free(("slot",)))
                V.tensor_copy(lb, lb1)

                with dve.Fori(0, NE // 2) as ep:
                    for u in range(2):
                        e = ep * 2 + u
                        dve.wait_ge(*at("si_done", e + 1))
                        dve.wait_ge(*at("d_done", e - 1))
                        tt(am[:, u, :, :].rearrange("p j s -> p (j s)"), slab(1)[:, u * 512 + 128:u * 512 + 256], sg[:, u, :], ALU.mult).then_inc(
                            sem["am_done"], 1)
                dve.wait_ge(*at("base_ready", 1))
                settle(dve)
                n_over = dve.value_load(nov[0:1, 0:1], min_val=0, max_val=XBLK)
                with dve.If(n_over > 0):
                    with dve.Fori(0, XBLK) as x:
                        dve.wait_ge(sem["ov_si"], L * XBLK + x + 1)
                        tt(am[:, 0, :, :].rearrange("p j s -> p (j s)"), slab(1)[:, 128:256], sg[:, 0, :], ALU.mult).then_inc(sem["ov_am"], 1)
                with dve.Else():
                    dve.sem_inc(sem["ov_am"], XBLK)

                for k in range(2 * NT):
                    c, i = k // NT, k % NT
                    n = TS[i]
                    dve.wait_ge(*at(f"yg{k % 2}", 16 * (k // 2 + 1)))
                    if c:
                        dve.wait_ge(*at("cb_done", k - NT + 1))
                    stt(h[0:n, i, :], xg[0:n, k % 2, :], wcomb[0:n, c, i:i + 1], h[0:n, i, :], ALU.mult, ALU.add).then_inc(
                        sem["cb_done"], 1)
                assert n_[0] == PER["dve"], n_[0]

            dve.wait_ge(sem["fin_rms"], 1)
            dve.wait_ge(sem["fin_g"], 16)
            V.reciprocal(rstd, rms).then_inc(sem["fin_rms"], 1)
            dve.wait_ge(sem["fin_rms"], 2)
            for i in range(NT):
                n = TS[i]
                stt(h[0:n, i, :], h[0:n, i, :], rstd[0:n, i:i + 1], gB[0:n, :], ALU.mult, ALU.mult).then_inc(sem["fin_y"], 1)

        @block.scalar
        def _(act):
            A = nc.scalar.activation
            act.wait_ge(sem["init"], INITS + 3)
            A(lb1, lb1, ACT.Exp).then_inc(sem["lbe"], 1)
            act.wait_ge(sem["x_load"], 16 * len(xslices))

            def squares(rms_sem, value):
                pass

            with act.Fori(0, DEPTH) as L:
                n_ = [0]

                def at(name, k):
                    return sem[name], L * PER[name] + (START.get(name, 0) + k)

                def link(ins):
                    n_[0] += 1
                    ins.then_inc(sem["act"], 1)
                    act.wait_ge(*at("act", n_[0]))

                def done(job):
                    act.wait_ge(*at("pe_done", JOBS[job] + 1))

                def free(job):
                    return sem[f"free{JOBS[job] % 4}"], 1

                def freed(job):
                    act.wait_ge(*at(f"free{JOBS[job] % 4}", JOBS[job] // 4 + 1))

                def row_rms(weight):
                    act.dma_start(gB, a[weight][bass.ds(L, 1), :].broadcast_to([P, D])).then_inc(sem["g_load"], 16)
                    for i in range(NT):
                        if weight == "ffn_norm_g":
                            freed(("wo", 0, i))
                            freed(("wo", 1, i))
                        n = TS[i]
                        link(A(pr[0:n, 2048:3072], h[0:n, i, :], ACT.Square, accum_out=ss[0:n, i:i + 1]))
                    A(rms, ss, ACT.Sqrt, scale=1.0 / D, bias=eps_t).then_inc(sem["rms_ready"], 1)

                def padded(dst, j):
                    flat = dst[:, j, :, :].rearrange("p j t -> p (j t)")
                    return (flat[:, 0:80], slice(0, 80)), (flat[:, P:P + LT - 80], slice(80, LT))

                def evacuate(job, key):
                    for i in range(NT):
                        done((key, i))
                        A(xnT[:, :, T0[i]:T0[i] + TS[i]], job_slab((key, i)).rearrange("p (c t) -> p c t", c=KC)[:, :, 0:TS[i]],
                          ACT.Copy).then_inc(*free((key, i)))

                act.wait_ge(*at("cb_done", 0))
                act.dma_start(ik_g, a["idx_k_norm_g"][bass.ds(L, 1), :].broadcast_to([P, ID])).then_inc(sem["par_load"], 16)
                act.dma_start(rb, a["router_b"][bass.ds(L, 1), :].broadcast_to([P, 36])).then_inc(sem["par_load"], 16)
                act.dma_start(hn_g, a["hgrn_norm_g"][bass.ds(L * P, P), :]).then_inc(sem["par_load"], 16)
                row_rms("mix_norm_g")
                evacuate("xt", "xt")
                act.wait_ge(*at("lb_ready", 1))
                A(llb, llb, ACT.Ln).then_inc(sem["lb_ln"], 1)
                for name, c0, n in (("k3", 1024, 40), ("k2", 512, 512), ("k1", 0, 512), ("hi", None, 512)):
                    if name == "hi":
                        act.wait_ge(*at("ksq_ready", 1))
                        A(krms, kss, ACT.Sqrt, scale=1.0 / ID, bias=eps_t).then_inc(sem["kn_ready"], 1)
                    for i in range(NT):
                        done((name, i))
                        dst = vH[0:TS[i], i, :] if name == "hi" else qtok[0:TS[i], i, c0:c0 + n]
                        A(dst, job_slab((name, i))[0:TS[i], 0:n], ACT.Copy).then_inc(*free((name, i)))
                for i in range(NT):
                    done(("it", i))
                    A(ixT[:, :, T0[i]:T0[i] + TS[i]], job_slab(("it", i))[:, 0:384].rearrange("p (c t) -> p c t", c=3)[:, :, 0:TS[i]],
                      ACT.Copy).then_inc(*free(("it", i)))
                    done(("at", i))
                    A(aqk[:, :, T0[i]:T0[i] + TS[i]], job_slab(("at", i))[:, 0:768].rearrange("p (c t) -> p c t", c=6)[:, :, 0:TS[i]],
                      ACT.Copy).then_inc(*free(("at", i)))
                fb = pr[:, :].rearrange("p (k u t) -> p k u t", k=4, u=2)
                for j in range(HH):
                    e, l1, l2 = fb[:, 0, j % 2, :], fb[:, 2, j % 2, :], fb[:, 3, j % 2, :]
                    act.wait_ge(*at("e_ready", j + 1))
                    link(A(e, e, ACT.Exp))
                    A(l1, e, ACT.Ln, bias=one_t)
                    A(l2, e, ACT.Ln, bias=one_t, scale=lb[:, j:j + 1]).then_inc(sem["lnf_ready"], 1)
                for j in range(HH):
                    done(("hq", j))
                    o = wide(("hq", j))
                    (d0, c0), (d1, c1) = padded(hq, j)
                    A(d0, o[:, c0], ACT.Copy)
                    A(d1, o[:, c1], ACT.Copy).then_inc(*free(("hq", j)))
                for i in range(1, NT):
                    for hd in range(IH):
                        m = (i - 1) * IH + hd
                        done(("ix", i, hd))
                        if m >= 2:
                            act.wait_ge(*at("rel_used", m - 1))
                        A(rel[0:TS[i], m % 2, 0:W[i]], wide(("ix", i, hd))[0:TS[i], 0:W[i]], ACT.Relu).then_inc(*free(("ix", i, hd)))
                for m in range(HH * 7):
                    act.wait_ge(*at("d_ready", m + 1))
                    A(ebuf[:, m % 2, :], ebuf[:, m % 2, :], ACT.Exp).then_inc(sem["ex_ready"], 1)
                for hd in range(HH):
                    done(("lv", HH - 1, LEVELS - 1))
                    if hd >= 2:
                        act.wait_ge(*at("qb_ready", hd - 1))
                    A(qe[:, hd % 2, :], hb[:, hd, :, :].rearrange("p j t -> p (j t)"), ACT.Exp).then_inc(sem["ex_ready"], 1)
                    act.wait_ge(*at("d_ready", 28 + hd + 1))
                    A(ebuf[:, hd % 2, :], ebuf[:, hd % 2, :], ACT.Exp).then_inc(sem["ex_ready"], 1)
                A(dec, hb[:, :, :, P - 1], ACT.Exp).then_inc(sem["ex_ready"], 1)
                for j in range(NT):
                    n = TS[j]
                    done(("kt", j))
                    A(kwT[0:n, j % 2, :], job_slab(("kt", j))[0:n, 0:512], ACT.Copy).then_inc(*free(("kt", j)))
                    done(("ot", j))
                    A(hq[:, :, j, 0:n], job_slab(("ot", j))[:, 0:512].rearrange("p (h t) -> p h t", h=HH)[:, :, 0:n], ACT.Copy).then_inc(
                        *free(("ot", j)))
                for j in range(HH):
                    done(("hg", j))
                    o = wide(("hg", j))
                    (d0, c0), (d1, c1) = padded(hk, j)
                    A(d0, o[:, c0], ACT.Silu)
                    A(d1, o[:, c1], ACT.Silu).then_inc(*free(("hg", j)))
                for hd in range(HH):
                    done(("on", hd))
                    A(hb[:, hd, :, :].rearrange("p j t -> p (j t)"), job_slab(("on", hd))[:, 0:640], ACT.Sqrt, scale=1.0 / HD, bias=eps_t).then_inc(
                        *free(("on", hd)))
                act.wait_ge(*at("ya_ready", 1))
                for c in range(8):
                    done(("ga", c))
                    A(sga[:, c, :], wide(("ga", c)), ACT.Sigmoid).then_inc(*free(("ga", c)))

                def softmax_exp(m):
                    i, hd = m // 8, m % 8
                    n = TS[i]
                    act.wait_ge(*at("mx_ready", m + 1))
                    A(pb[0:n, hd, 0:W[i]], pb[0:n, hd, 0:W[i]], ACT.Exp, bias=nmx[0:n, hd:hd + 1], scale=AD ** -0.5,
                      accum_out=psum_[0:n, hd:hd + 1]).then_inc(sem["p_ready"], 1)

                for m in range(4):
                    softmax_exp(m)
                for n0 in range(2 * NT):
                    i, g = n0 // 2, n0 % 2
                    n = TS[i]
                    if n0 + 1 < 2 * NT:
                        for m in range(4 * n0 + 4, 4 * n0 + 8):
                            softmax_exp(m)
                    for k in range(i + 1):
                        m = PTS.index((i, g, k))
                        done(("pt", i, g, k))
                        if m >= 4:
                            b = PTS[m - 4]
                            if b[2] < b[0]:
                                act.wait_ge(*at("pt_used", PT_COUNT[b]))
                            else:
                                done(("pv", b[0], b[1]))
                        A(ptq[0:TS[k], m % 4, 0:4 * n], job_slab(("pt", i, g, k))[0:TS[k], 0:4 * n], ACT.Copy).then_inc(*free(("pt", i, g, k)))
                    done(("pv", i, g))
                    A(ybT[:, 2 * g:2 * g + 2, T0[i]:T0[i] + n], job_slab(("pv", i, g))[:, 0:2 * n].rearrange("p (c t) -> p c t", c=2),
                      ACT.Copy).then_inc(*free(("pv", i, g)))
                for c in range(8):
                    done(("gb", c))
                    A(sgb[:, c, :], wide(("gb", c)), ACT.Sigmoid).then_inc(*free(("gb", c)))
                row_rms("ffn_norm_g")
                for i in range(NT):
                    act.wait_ge(*at("xn_ready", NT + i + 1))
                    act.dma_start(xrow[T0[i]:T0[i] + TS[i], :], xn[0:TS[i], i % 2, :]).then_inc(sem[f"xw{i % 2}"], 16)
                    done(("xt2", i))
                    A(xnT[:, :, T0[i]:T0[i] + TS[i]], job_slab(("xt2", i)).rearrange("p (c t) -> p c t", c=KC)[:, :, 0:TS[i]],
                      ACT.Copy).then_inc(*free(("xt2", i)))
                act.wait_ge(*at("rt_ready", 1))
                A(ge, ge, ACT.Exp).then_inc(sem["rt_exp"], 1)
                act.wait_ge(*at("rt_ready", 2))
                A(ed, dd, ACT.Exp).then_inc(sem["rt_exp"], 1)

                def rows_in(e, u):
                    act.wait_ge(*at("t_done", e + 1))
                    act.wait_ge(*at("g_done", e - 1))
                    A(xgT[:, u, :, :].rearrange("p c s -> p (c s)"), slab(0)[:, u * 512:(u + 1) * 512], ACT.Copy).then_inc(sem["xt_done"], 1)

                def gate(e, u):
                    act.wait_ge(*at("g_done", e + 1))
                    act.wait_ge(*at("am_done", e - 1))
                    A(sg[:, u, :], slab(1)[:, u * 512:u * 512 + 128], ACT.Silu).then_inc(sem["si_done"], 1)

                def rows_out(e, u, first=False):
                    act.wait_ge(*at("d_done", e + 1))
                    if not first:
                        act.wait_ge(*at(f"yd{u}", (e - u) * 8))
                    A(ysb[0:SLOTS, u, :], slab(2 + u)[0:SLOTS, :], ACT.Copy).then_inc(sem["y_done"], 1)
                    act.wait_ge(*at("y_done", e + 1))
                    act.dma_start(yrow[bass.ds(e * SLOTS, SLOTS), :] if not isinstance(e, int) else yrow[e * SLOTS:(e + 1) * SLOTS, :],
                                  ysb[0:SLOTS, u, :]).then_inc(sem[f"yd{u}"], 16)

                rows_in(0, 0)
                rows_in(1, 1)
                gate(0, 0)
                gate(1, 1)
                rows_out(0, 0, first=True)
                rows_in(2, 0)
                gate(2, 0)
                rows_out(1, 1, first=True)
                rows_in(3, 1)
                gate(3, 1)
                rows_out(2, 0)
                with act.Fori(2, NE // 2) as ep:
                    for u in range(2):
                        e = ep * 2 + u
                        rows_in(e, u)
                        gate(e, u)
                        rows_out(e - 1, 1 - u)
                rows_out(NE - 1, 1)
                for u in range(2):
                    act.wait_ge(*at(f"yd{u}", 8 * NE))
                act.wait_ge(*at("base_ready", 1))
                settle(act)
                n_over = act.value_load(nov[0:1, 0:1], min_val=0, max_val=XBLK)
                with act.If(n_over > 0):
                    with act.Fori(0, XBLK) as x:
                        def ov(name):
                            return sem[name], (L * XBLK + x) * OV[name] + OV[name]

                        act.wait_ge(*ov("ov_t"))
                        A(xgT[:, 0, :, :].rearrange("p c s -> p (c s)"), slab(0)[:, 0:512], ACT.Copy).then_inc(sem["ov_xt"], 1)
                        act.wait_ge(*ov("ov_g"))
                        A(sg[:, 0, :], slab(1)[:, 0:128], ACT.Silu).then_inc(sem["ov_si"], 1)
                        act.wait_ge(*ov("ov_d"))
                        A(ysb[0:SLOTS, 0, :], slab(2)[0:SLOTS, :], ACT.Copy).then_inc(sem["ov_y"], 1)
                        act.wait_ge(*ov("ov_y"))
                        act.dma_start(yrow[bass.ds((x + NE) * SLOTS, SLOTS), :], ysb[0:SLOTS, 0, :]).then_inc(sem["ov_yd"], 16)
                        act.wait_ge(*ov("ov_yd"))
                with act.Else():
                    for name in ("ov_xt", "ov_si", "ov_y", "ov_yd"):
                        act.sem_inc(sem[name], XBLK * OV[name])
                assert n_[0] == PER["act"], n_[0]

            act.wait_ge(sem["cb_done"], DEPTH * PER["cb_done"] + START["cb_done"])
            act.dma_start(gB, a["final_norm_g"].broadcast_to([P, D])).then_inc(sem["fin_g"], 16)
            for i in range(NT):
                n = TS[i]
                A(pr[0:n, 2048:3072], h[0:n, i, :], ACT.Square, accum_out=ss[0:n, i:i + 1]).then_inc(sem["fin_ss"], 1)
                act.wait_ge(sem["fin_ss"], i + 1)
            A(rms, ss, ACT.Sqrt, scale=1.0 / D, bias=eps_t).then_inc(sem["fin_rms"], 1)
            outs = [(0, NMETA, 64, 0)] + [(i, 0, TS[i], T0[i] - NMETA) for i in range(1, NT)]
            for i, r, n, s0 in outs:
                act.wait_ge(sem["fin_y"], i + 1)
                act.dma_start(out[s0:s0 + n, :], h[r:r + n, i, :]).then_inc(sem["out_done"], 16)
            act.wait_ge(sem["out_done"], 16 * len(outs))

        @block.gpsimd
        def _(pool):
            G = nc.gpsimd
            for r in (pr[:, :], ptb[:, :, :], AT[:, :, :, :], vA[:, :, :], S[:, :, :]):
                G.memset(r, 0.0).then_inc(sem["init"], 1)
            pool.wait_ge(sem["init"], INITS - 1)
            G.memset(eps_t, EPS).then_inc(sem["init"], 1)
            pool.wait_ge(sem["init"], INITS)
            for n in range(XBLK * SLOTS // (2 * P)):
                r0 = NE * SLOTS + n * 2 * P
                pool.dma_start(yrow[r0:r0 + 2 * P, :].rearrange("(p a) n -> p (a n)", a=2),
                               zrow).then_inc(sem["y_init"], 16)
            with pool.Fori(0, DEPTH) as L:
                def at(name, k):
                    return sem[name], L * PER[name] + (START.get(name, 0) + k)

                pool.wait_ge(*at(*freed_at(("hq", HH - 1))))
                for m in range(HH * 7):
                    hd, l, u = m // 7, m % 7 + 1, m % 2
                    half = 2 ** (l - 1)
                    pool.wait_ge(*at("ex_ready", m + 1))
                    if m >= 2:
                        pool.wait_ge(*at("pe_done", JOBS[("lv", (m - 2) // 7, (m - 2) % 7 + 1)] + 1))
                    q_, k_, e_, qo, ko = (x.rearrange("p (n a t) -> p n a t", a=2, t=half) for x in (
                        hq[:, hd, :, :].rearrange("p j t -> p (j t)"), hk[:, hd, :, :].rearrange("p j t -> p (j t)"),
                        ebuf[:, u, :], qe[:, u, :], ke[:, u, :]))
                    G.tensor_tensor(qo[:, :, 1, :], q_[:, :, 1, :], e_[:, :, 1, :], ALU.mult)
                    G.tensor_tensor(ko[:, :, 0, :], k_[:, :, 0, :], e_[:, :, 0, :], ALU.mult).then_inc(sem["qe_ready"], 1)
                for hd in range(HH):
                    pool.wait_ge(*at(*freed_at(("ot", NT - 1))))
                    q_ = hq[:, hd, :, :].rearrange("p j t -> p (j t)")
                    G.tensor_tensor(osq[:, hd, :], q_, q_, ALU.mult).then_inc(sem["sq_ready"], 1)

                pool.wait_ge(*at("xw0", 48))
                pool.wait_ge(*at("xw1", 32))
                pool.wait_ge(*at(*freed_at(("slot",))))
                settle(pool)
                with pool.Fori(0, NE // 2) as ep:
                    for u in range(2):
                        e = ep * 2 + u
                        pool.wait_ge(*at("t_done", e - 1))
                        G.tensor_copy(stage[:, u:u + 1], idx[:, bass.ds(e, 1)]).then_inc(sem["stg"], 1)
                        pool.wait_ge(*at("stg", e + 1))
                        settle(pool)
                        pool.indirect_dma_start(xg[0:SLOTS, u, :], None, xrow, bass.IndirectOffsetOnAxis(ap=stage[:, u:u + 1], axis=0)).then_inc(
                            sem[f"xg{u}"], 16)
                pool.wait_ge(*at("base_ready", 1))
                settle(pool)
                n_over = pool.value_load(nov[0:1, 0:1], min_val=0, max_val=XBLK)
                with pool.If(n_over > 0):
                    pool.wait_ge(*at("d_done", NE))
                    settle(pool)
                    with pool.Fori(0, XBLK) as x:
                        def ov(name, k=0):
                            return sem[name], (L * XBLK + x) * OV[name] + OV[name]

                        ex = pool.value_load(xei[0:1, bass.ds(x, 1)], min_val=0, max_val=NE - 1)
                        for m, name in enumerate(("w_expert_gate", "w_expert_up")):
                            pool.dma_start(ovw[:, m * 2048:(m + 1) * 2048],
                                           a[name][bass.ds((L * NE + ex) * D, D), :].rearrange("(p c) f -> p (c f)", p=P)).then_inc(sem["ov_w"], 16)
                        pool.dma_start(ovw[:, 4096:6144].rearrange("p (j n) -> p j n", j=2),
                                       a["w_expert_down"][bass.ds((L * NE + ex) * FF, FF), :].rearrange("(j p) n -> p j n", p=P)).then_inc(
                                           sem["ov_w"], 16)
                        G.tensor_copy(stage[:, 0:1], idx[:, bass.ds(x + NE, 1)]).then_inc(sem["ov_stg"], 1)
                        pool.wait_ge(*ov("ov_stg"))
                        settle(pool)
                        pool.indirect_dma_start(xg[0:SLOTS, 0, :], None, xrow, bass.IndirectOffsetOnAxis(ap=stage[:, 0:1], axis=0)).then_inc(
                            sem["ov_x"], 16)
                        pool.wait_ge(*ov("ov_yd"))
                with pool.Else():
                    for name in ("ov_w", "ov_stg", "ov_x"):
                        pool.sem_inc(sem[name], XBLK * OV[name])

                pool.wait_ge(*at("t_done", NE))
                for u in range(2):
                    pool.wait_ge(*at(f"yd{u}", 8 * NE))
                pool.wait_ge(sem["ov_yd"], L * (16 * XBLK) + 16 * XBLK)
                pool.wait_ge(*at("sidx_ready", 1))
                settle(pool)
                for k in range(2 * NT):
                    if k >= 2:
                        pool.wait_ge(*at("cb_done", k - 1))
                        settle(pool)
                    n = TS[k % NT]
                    pool.indirect_dma_start(xg[0:n, k % 2, :], None, yrow, bass.IndirectOffsetOnAxis(ap=sidx[0:n, k:k + 1], axis=0)).then_inc(
                        sem[f"yg{k % 2}"], 16)


def kernel(x, meta_tokens, mix_norm_g, w_in, hgrn_lb_logits, hgrn_norm_g, idx_k_norm_g, w_branch_hgrn,
           w_branch_dsa, w_out, ffn_norm_g, router_group_w, router_group_b, router_expert_w, router_expert_b,
           w_expert_gate, w_expert_up, w_expert_down, final_norm_g):
    import concourse.bacc as bacc
    from concourse.bass_utils import run_bass_kernel_spmd

    consts, _, lvm = shape_constants()
    arrays = dict(
        consts=consts, level_masks=lvm,
        x=x.reshape(SEQ, D), meta_tokens=meta_tokens, mix_norm_g=mix_norm_g, w_in=w_in.reshape(DEPTH * D, -1),
        hgrn_lb_logits=hgrn_lb_logits.reshape(DEPTH, HH, P).transpose(2, 0, 1).reshape(P, DEPTH * HH),
        hgrn_norm_g=hgrn_norm_g.reshape(DEPTH, HH, P).transpose(0, 2, 1).reshape(DEPTH * P, HH), idx_k_norm_g=idx_k_norm_g,
        w_branch_hgrn=w_branch_hgrn.reshape(-1, D), w_branch_dsa=w_branch_dsa.reshape(-1, D), w_out=w_out.reshape(-1, D),
        ffn_norm_g=ffn_norm_g, router_w=np.concatenate([router_group_w, router_expert_w], -1).reshape(DEPTH * D, NG + NE),
        router_b=np.concatenate([router_group_b, router_expert_b], -1),
        w_expert_gate=w_expert_gate.reshape(-1, FF), w_expert_up=w_expert_up.reshape(-1, FF),
        w_expert_down=w_expert_down.reshape(-1, D), final_norm_g=final_norm_g.reshape(1, D),
    )
    nc = bacc.Bacc("TRN2", target_bir_lowering=False, num_devices=1)
    arrays = {n: np.ascontiguousarray(v) for n, v in arrays.items()}
    aps = {n: nc.dram_tensor(n, v.shape, mybir.dt.from_np(v.dtype), kind="ExternalInput").ap() for n, v in arrays.items()}
    out = nc.dram_tensor("out", (SEQ, D), F32, kind="ExternalOutput").ap()
    program(nc, aps, out)
    return run_bass_kernel_spmd(nc, [arrays], core_ids=[0]).results[0]["out"].reshape(1, SEQ, D)
```

```python
from contextlib import ExitStack

import concourse.bass as bass
from concourse import mybir
import numpy as np

F32 = mybir.dt.float32
F32R = mybir.dt.float32r
I32 = mybir.dt.int32
U8 = mybir.dt.uint8
ALU = mybir.AluOpType
ACT = mybir.ActivationFunctionType
AX = mybir.AxisListType.X

P = 128
D = 1024
KC = D // P
SEQ, NMETA = 512, 16
LT = SEQ + NMETA
DEPTH = 2
EPS = 1e-6
NT = 5
T0 = [0, 80, 208, 336, 464]
TS = [80, 128, 128, 128, 64]
W = [80, 208, 336, 464, 528]
TOPK = min(256, LT // 4)
HH, HD = 4, 128
AH, AD = 8, 64
IH, ID = 8, 32
NG, EPG = 4, 8
NE = NG * EPG
FF = D // 4
SLOTS = 64
XBLK = (2 * LT) // SLOTS
NBLK = NE + XBLK
KMAX = LT // SLOTS
REPL, HIDDEN, SENT, NEG = -3e38, -2e38, 3e38, -1e30
SCALAR_MIN = -3e38
INITS = 11

C_HQ, C_HF, C_HI, C_HG, C_AQ, C_AK, C_IK, C_GA, C_GB = 0, 512, 1024, 1536, 2048, 2560, 3072, 3112, 4136
CHUNKS = ["k3", "k2", "k1", "hi", "hf", "hq", "hg", "ga0", "ga1", "wa", "gb0", "gb1", "wb", "wo0", "wo1", "ro"]
LEVELS = 8


def plan_jobs():
    jobs, last = [], {}

    def add(*names):
        jobs.extend(names)
        return len(jobs) - 1

    add(*[("xt", i) for i in range(NT)])
    for c in ("k3", "k2", "k1", "hi"):
        last[c] = add(*[(c, i) for i in range(NT)])
    add(*[(n, i) for i in range(NT) for n in ("it", "at")])
    for c in ("hf", "hq"):
        last[c] = add(*[(c, j) for j in range(HH)])
    add(*[("ix", i, h) for i in range(1, NT) for h in range(IH)])
    add(*[("lv", h, l) for h in range(HH) for l in range(LEVELS)])
    for j in range(NT - 1):
        add(("kt", j), ("su", j))
        if j > 0:
            add(("ot", j - 1))
    add(("ot", NT - 2), ("ot", NT - 1))
    last["hg"] = add(*[("hg", j) for j in range(HH)])
    add(*[("on", h) for h in range(HH)])
    last["ga0"] = add(*[("ga", c) for c in range(4)])
    last["ga1"] = add(*[("ga", c) for c in range(4, 8)])
    last["wa"] = add(*[("wa", c) for c in range(8)])
    groups = [(i, g) for i in range(NT) for g in range(2)]
    add(*[("qk", 0, h) for h in range(4)])
    for n, (i, g) in enumerate(groups):
        if n + 1 < len(groups):
            ni, ng = groups[n + 1]
            add(*[("qk", ni, 4 * ng + r) for r in range(4)])
        add(*[("pt", i, g, k) for k in range(i + 1)])
        add(("pv", i, g))
    last["gb0"] = add(*[("gb", c) for c in range(4)])
    last["gb1"] = add(*[("gb", c) for c in range(4, 8)])
    last["wb"] = add(*[("wb", c) for c in range(8)])
    last["wo0"] = add(*[("wo", 0, i) for i in range(NT)])
    last["wo1"] = add(*[("wo", 1, i) for i in range(NT)])
    add(("xt2", 0), ("xt2", 1))
    for i in range(2, NT):
        add(("ro", i - 2), ("xt2", i))
    last["ro"] = add(("ro", NT - 2), ("ro", NT - 1))
    add(("rank",), ("slot",))
    return {j: n for n, j in enumerate(jobs)}, last


JOBS, LAST = plan_jobs()
NJ = len(JOBS)
PER_SLAB = [len([n for n in JOBS.values() if n % 4 == s]) for s in range(4)]

DVE_OPS, ACT_OPS = 268, 14
PER = dict(
    pe_done=NJ, dve=DVE_OPS, act=ACT_OPS, ss_ready=0, rms_ready=2, xn_ready=2 * NT, ksq_ready=1,
    kn_ready=1, rope_ready=1, e_ready=HH, lnf_ready=HH, f_done=HH, rel_used=32, d_ready=32, ex_ready=37, qe_ready=28,
    qb_ready=HH, kw_ready=HH, sq_ready=HH, ya_ready=1, mx_ready=40, p_ready=40, pn_ready=40, pt_used=20, mg_ready=8,
    xw0=48, xw1=32, rt_ready=2, rt_exp=2, c_ready=1, ab_ready=1, idx_ready=1, base_ready=1, sidx_ready=1,
    g_load=32, par_load=48, lb_ready=1, lb_ln=1, stg=NE, xg0=16 * NE // 2, xg1=16 * NE // 2, t_done=NE, xs_hi=NE, xs_done=NE, wg_done=NE, g_done=NE,
    ge_done=NE, ft_done=NE, si_done=NE, af_done=NE, ah_done=NE, am_done=NE, wh_gate=NE, wh_up=NE, wh_down=NE, wl_gate=NE, wl_up=NE, wl_down=NE, d_done=NE, y_done=NE, yd0=16 * NE // 2, yd1=16 * NE // 2, yg0=48, yg1=48, yg2=32, yg3=32, cb_done=2 * NT, r1_clear=1,
)
for _s in range(4):
    PER[f"free{_s}"] = PER_SLAB[_s]
for _s in range(2):
    PER[f"gu{_s}"] = 16 * len(CHUNKS) // 2 + 16 * NE // 2
    PER[f"up{_s}"] = 16 * NE // 2
    PER[f"dn{_s}"] = 16 * NE // 2
START = {"free0": 1, "free1": 1, "free2": 1, "free3": 1, "cb_done": 2 * NT + 1, "r1_clear": 1,
         **{n: 2 for n in ("t_done", "xs_done", "wg_done", "g_done", "ge_done", "ft_done", "af_done", "am_done", "d_done", "y_done")}}
OV = dict(ov_w=48, ov_stg=1, ov_x=16, ov_t=1, ov_xt=1, ov_g=1, ov_si=1, ov_am=1, ov_d=1, ov_y=1, ov_yd=16)
for _n, _k in OV.items():
    PER[_n] = _k * XBLK



def freed_at(job):
    return f"free{JOBS[job] % 4}", JOBS[job] // 4 + 1


PTS = [(i, g, k) for i in range(NT) for g in range(2) for k in range(i + 1)]
PT_COUNT = {b: len([x for x in PTS[:n + 1] if x[2] < x[0]]) for n, b in enumerate(PTS)}


def shape_constants():
    def rope(hd):
        rot = hd // 4
        inv = np.float32(500000.0) ** (-np.arange(0, rot, 2, dtype=np.float32) / np.float32(rot))
        ang = np.arange(LT, dtype=np.float32)[:, None] * inv[None, :]
        out = np.zeros((P, 2, NT, rot // 2), np.float32)
        for i in range(NT):
            out[:TS[i], 0, i] = np.cos(ang[T0[i]:T0[i] + TS[i]])
            out[:TS[i], 1, i] = np.sin(ang[T0[i]:T0[i] + TS[i]])
        return out.reshape(P, -1)

    s, t = np.arange(P)[:, None], np.arange(P)[None, :]
    lv = np.zeros((P, LEVELS, P), np.float32)
    lv[:, 0] = s == t
    for l in range(1, LEVELS):
        half = 2 ** (l - 1)
        lv[:, l] = (s // (2 * half) == t // (2 * half)) & (s % (2 * half) < half) & (t % (2 * half) >= half)
    cols = [
        np.eye(P), np.ones((P, P)), (s < t),
        rope(AD), rope(ID),
        np.broadcast_to(np.arange(64.0), (P, 64)), np.broadcast_to(np.arange(NBLK, dtype=float), (P, NBLK)),
        np.broadcast_to(np.arange(NE, dtype=float), (P, NE)),
        np.broadcast_to(np.arange(NG, 0, -1.0), (P, NG)), np.broadcast_to(np.arange(EPG, 0, -1.0), (P, EPG)),
        np.broadcast_to(SLOTS * np.arange(1.0, KMAX + 1), (P, KMAX)),
        np.arange(P)[:, None] + np.array(T0)[None, :],
        np.broadcast_to((np.arange(NT * P) % P != 0), (P, NT * P)),
        np.where((s < NMETA) & (np.arange(W[0])[None] >= NMETA), NEG, 0.0),
        np.arange(P)[:, None] % SLOTS == np.arange(SLOTS)[None],
    ]
    sizes = [c.shape[1] for c in cols]
    return np.concatenate([np.asarray(c, np.float32) for c in cols], 1), sizes, lv.reshape(P, -1)


def program(nc, a, out):
    _, sizes, _ = shape_constants()
    with ExitStack() as ctx:
        start = {}

        def sb(name, shape, dt=F32):
            start[name] = nc.sbuf_base
            return ctx.enter_context(nc.sbuf_tensor(name, shape, dt))

        def rounded(name, over, first, n):
            return nc.alloc_sbuf_tensor_at(name, [P, n], F32R, offset=start[over] + 4 * first)[:, :]

        sem = {n: ctx.enter_context(nc.semaphore(n)) for n in PER}
        for n in ("const_load", "x_load", "init", "lbe", "out_done", "fin_ss", "fin_g", "fin_rms", "fin_y", "settled", "y_init"):
            sem[n] = ctx.enter_context(nc.semaphore(n))

        h = sb("resid", [P, NT, D])
        xnT = sb("xnT", [P, KC, LT])
        gu_ring = sb("gu_ring", [P, 2, 4096])
        dn_ring = sb("dn_ring", [P, 2, 2048])
        r1 = sb("r1", [P, 3 * 2560])
        pr = sb("pr", [P, 4224])
        r2 = sb("r2", [P, 3168 + 1584 + 2560])
        AT = sb("AT", [P, HH, NT, P])
        sc = sb("sc", [P, NT, 4 + LT])
        vA = sb("vA", [P, NT, 2 * AD])
        ptb = sb("ptb", [P, 2, 1024])
        S0 = sb("S", [P, HH, HD])
        consts = sb("tables", [P, sum(sizes)])
        lvm = sb("masks_u8", [P, LEVELS, P], U8)
        small = sb("small", [P, 1300])

        qtok = r1[:, 0:NT * 1064].rearrange("p (i n) -> p i n", i=NT)
        hq, hk, hb = (r1[:, n * 2560:(n + 1) * 2560].rearrange("p (h j t) -> p h j t", h=HH, j=NT) for n in range(3))
        sga = r1[:, 2560:2560 + 8 * LT].rearrange("p (c t) -> p c t", c=8)
        xg = r1[:, 0:2048].rearrange("p (u n) -> p u n", u=2)
        ysb = r1[:, 2048:4096].rearrange("p (u n) -> p u n", u=2)
        yg = r1[:, 0:4096].rearrange("p (u n) -> p u n", u=4)
        xs = rounded("x_parts", "r1", 4096, 2048).rearrange("p (u c a s) -> p u c a s", u=2, c=KC, a=2)
        guo = r1[:, 6144:7168].rearrange("p (u n) -> p u n", u=2)
        ams = rounded("act_parts", "r1", 7168, 512).rearrange("p (u j a s) -> p u j a s", u=2, j=2, a=2)
        xgT = r1[:, 4096:4608].rearrange("p (c s) -> p c s", c=KC)
        am = r1[:, 7168:7296].rearrange("p (j s) -> p j s", j=2)
        xn = pr[:, 0:2048].rearrange("p (u n) -> p u n", u=2)
        kdup = pr[:, 0:1280].rearrange("p (i g r d) -> p i g r d", i=NT, g=2, r=2)
        ikdup = pr[:, 1280:1920].rearrange("p (i r d) -> p i r d", i=NT, r=4)
        rt = pr[:, 1920:4224]
        ebuf, qe, ke = (pr[:, n * 1280:(n + 1) * 1280].rearrange("p (u t) -> p u t", u=2) for n in range(3))
        osq = pr[:, 0:2560].rearrange("p (h t) -> p h t", h=HH)
        pb = pr[:, :].rearrange("p (h t) -> p h t", h=8)
        sgb = pb
        aqk = r2[:, 0:3168].rearrange("p (c t) -> p c t", c=6)
        ixT = r2[:, 3168:4752].rearrange("p (c t) -> p c t", c=3)
        kwT = r2[:, 3168:4192].rearrange("p (u n) -> p u n", u=2)
        vH = r2[:, 4752:7312].rearrange("p (i n) -> p i n", i=NT)
        ybT = r2[:, 4752:4752 + 4 * LT].rearrange("p (c t) -> p c t", c=4)
        ovw = r2[:, 0:6144]
        sg, amf = (r2[:, 6144 + n * 256:6400 + n * 256].rearrange("p (u n) -> p u n", u=2) for n in range(2))
        gu_high = [rounded("gate_up_high0", "r2", 0, 4096), rounded("gate_up_high1", "xnT", 0, 4096)]
        dn_high = [rounded("down_high0", "r2", 4096, 2048), rounded("down_high1", "ptb", 0, 2048)]
        gu_low = [rounded(f"gate_up_low{u}", "gu_ring", 4096 * u, 4096) for u in range(2)]
        dn_low = [rounded(f"down_low{u}", "dn_ring", 2048 * u, 2048) for u in range(2)]
        gB = ptb[:, 0, :]
        rel = ptb[:, :, 0:LT]
        S = [S0, ptb[:, 1, 0:HH * HD].rearrange("p (h e) -> p h e", h=HH)]
        ptq = ptb[:, :, :].rearrange("p a (b n) -> p (a b) n", b=2)

        at_ = [0]

        def const(n):
            at_[0] += sizes[n]
            return consts[:, at_[0] - sizes[n]:at_[0]]

        ident, ones, tri, rope_a, rope_i, io64, ioblk, ioe, descg, desce, kthr, tokid, reset, mask0, fold = (
            const(n) for n in range(15))
        rope_a = rope_a.rearrange("p (a i d) -> p a i d", a=2, i=NT)
        rope_i = rope_i.rearrange("p (a i d) -> p a i d", a=2, i=NT)

        at_[0] = 0

        def tiny(n):
            at_[0] += n
            return small[:, at_[0] - n:at_[0]]

        ss, rms, rstd = tiny(NT), tiny(NT), tiny(NT)
        kss, krms = tiny(NT), tiny(NT)
        ik_g = tiny(ID)
        iw = tiny(NT * IH).rearrange("p (i h) -> p i h", i=NT)
        hn_g = tiny(HH)
        lb, lb1, omlb, llb = tiny(HH), tiny(HH), tiny(HH), tiny(HH)
        dec = tiny(HH * NT).rearrange("p (h j) -> p h j", h=HH)
        top8 = tiny(4 * 8).rearrange("p (i k) -> p i k", i=4)
        mx, nmx, psum_, pinv = tiny(8), tiny(8), tiny(8), tiny(8)
        rb = tiny(36)
        eps_t = tiny(1)
        one_t = tiny(1)
        lg = tiny(NT * 36).rearrange("p (i n) -> p i n", i=NT)
        wcomb = tiny(2 * NT).rearrange("p (a i) -> p a i", a=2)
        rto = [2048]

        def rtt(n):
            rto[0] += n
            return pr[:, rto[0] - n:rto[0]]

        gmax, gs = rtt(NT), rtt(NT)
        ge = rtt(NT * NG).rearrange("p (i g) -> p i g", i=NT)
        goh = rtt(NT * NG).rearrange("p (i g) -> p i g", i=NT)
        vmx = rtt(NT)
        lm = rtt(NT * NE).rearrange("p (i g e) -> p i g e", i=NT, g=NG)
        ls = rtt(NT * EPG).rearrange("p (i e) -> p i e", i=NT)
        ls2 = rtt(NT * EPG).rearrange("p (i e) -> p i e", i=NT)
        m12 = rtt(2 * NT).rearrange("p (a i) -> p a i", a=2)
        eq = rtt(NT * EPG).rearrange("p (i e) -> p i e", i=NT)
        oh = rtt(2 * NT * EPG).rearrange("p (a i e) -> p a i e", a=2, i=NT)
        dd = rtt(NT)
        ed = rtt(NT)
        CC = rtt(2 * NT * NE).rearrange("p (a i n) -> p a i n", a=2, i=NT)
        Cs = rtt(NT * NE).rearrange("p (i n) -> p i n", i=NT)
        tmpC = rtt(2 * NT * NE).rearrange("p (a i n) -> p a i n", a=2, i=NT)
        rk = rtt(6 * NE).rearrange("p (i n) -> p i n", i=6)
        rsel, esel, osel = (rtt(2 * NT).rearrange("p (a i) -> p a i", a=2) for _ in range(3))
        nxk = rtt(NE * KMAX).rearrange("p (n k) -> p n k", n=NE)
        nx, inc, off = rtt(NE), rtt(NE), rtt(NE)
        qk_ = rtt(2 * NT * KMAX).rearrange("p (a k) -> p a k", k=KMAX)
        qq, pos, blk, isov, slotf = (rtt(2 * NT) for _ in range(5))
        Bm = ptb[:, 0, 0:2 * NT * NBLK].rearrange("p (a n) -> p a n", n=NBLK)
        Am = ptb[:, 1, 0:2 * NT * SLOTS].rearrange("p (a n) -> p a n", n=SLOTS)
        xef = rtt(XBLK)
        xcmp = hb
        xcm = r1[:, 5632:5632 + XBLK * NE].rearrange("p (x n) -> p x n", n=NE)
        lbl = sb("lbl", [P, 2, HH])
        sidx = sb("sidx", [P, 2 * NT], I32)
        idx = sb("idx", [SLOTS, NBLK], I32)
        stage = sb("stage", [SLOTS, 2], I32)
        xei = sb("xei", [1, XBLK], I32)
        nov = sb("nov", [1, 1], I32)

        zrow = AT[:, :, :, :].rearrange("p h j t -> p (h j t)")[:, 0:2 * D]

        ps = ctx.enter_context(nc.psum_tensor("ps", [P, 4096], F32))

        def slab(n):
            return ps[:, (n % 4) * 1024:(n % 4 + 1) * 1024]

        def job_slab(job):
            return slab(JOBS[job])

        def wide(job):
            return job_slab(job)[:, 432:432 + LT]

        xrow = nc.dram_tensor("xrow", (LT, D), F32, kind="Internal").ap()
        yrow = nc.dram_tensor("yrow", (NBLK * SLOTS, D), F32, kind="Internal").ap()

        def bc(ap, axis, n):
            ap = ap.unsqueeze(axis)
            shape = list(ap.shape)
            shape[axis] = n
            return ap.broadcast_to(shape)

        xslices = [(0, 0, NMETA, "meta", 0), (0, NMETA, 64, "x", 0)] + [
            (i, 0, TS[i], "x", T0[i] - NMETA) for i in range(1, NT)]
        block = ctx.enter_context(nc.Block())

        def settle(eng):
            eng.sem_inc(sem["settled"], 1)

        @block.sync
        def _(sp):
            sp.dma_start(consts[:, :], a["consts"]).then_inc(sem["const_load"], 16)
            sp.dma_start(dn_ring[:, 0, 0:LEVELS * P], a["level_masks"]).then_inc(sem["const_load"], 16)
            sp.dma_start(lbl[:, :, :].rearrange("p a h -> p (a h)"), a["hgrn_lb_logits"]).then_inc(sem["const_load"], 16)
            for i, r, n, src, s0 in xslices:
                s = a["meta_tokens"] if src == "meta" else a["x"][s0:s0 + n, :]
                sp.dma_start(h[r:r + n, i, :], s).then_inc(sem["x_load"], 16)

            w_in = a["w_in"].rearrange("(l p c) n -> l p c n", l=DEPTH, p=P)

            with sp.Fori(0, DEPTH) as L:
                def at(name, k):
                    return sem[name], L * PER[name] + (START.get(name, 0) + k)

                def rows(name, per, r):
                    w = a[name]
                    return w[bass.ds(L * per + r, P), :]

                def load_chunk(n, name):
                    slot = gu_ring[:, n % 2, :]
                    if n >= 2:
                        sp.wait_ge(*at("pe_done", LAST[CHUNKS[n - 2]] + 1))
                    else:
                        sp.wait_ge(*at("g_done", 0))
                    settle(sp)
                    if name in ("wa", "wb"):
                        w = a["w_branch_hgrn" if name == "wa" else "w_branch_dsa"]
                        sp.dma_start(slot.rearrange("p (c n) -> p c n", c=4),
                                     w[bass.ds(L * 512, 512), :].rearrange("(c p) n -> p c n", p=P)).then_inc(
                                         sem[f"gu{n % 2}"], 16)
                    elif name[:2] == "wo":
                        c0 = 512 * int(name[2])
                        sp.dma_start(slot.rearrange("p (c n) -> p c n", c=8),
                                     a["w_out"][bass.ds(L * D, D), c0:c0 + 512].rearrange("(c p) n -> p c n", p=P)).then_inc(
                                         sem[f"gu{n % 2}"], 16)
                    elif name == "ro":
                        sp.dma_start(slot[:, 0:288].rearrange("p (c n) -> p c n", c=8),
                                     a["router_w"][bass.ds(L * D, D), :].rearrange("(p c) n -> p c n", p=P)).then_inc(
                                         sem[f"gu{n % 2}"], 16)
                    else:
                        c0, nn = {"k3": (C_IK, 40), "k2": (C_AK, 512), "k1": (C_AQ, 512), "hi": (C_HI, 512),
                                  "hf": (C_HF, 512), "hq": (C_HQ, 512), "hg": (C_HG, 512), "ga0": (C_GA, 512),
                                  "ga1": (C_GA + 512, 512), "gb0": (C_GB, 512), "gb1": (C_GB + 512, 512)}[name]
                        sp.dma_start(slot[:, 0:8 * nn].rearrange("p (c n) -> p c n", c=8),
                                     a["w_in"][bass.ds(L * D, D), c0:c0 + nn].rearrange("(p c) n -> p c n", p=P)).then_inc(
                                         sem[f"gu{n % 2}"], 16)

                def load_expert(e, u, name, m, done):
                    sp.dma_start(gu_ring[:, u, m * 2048:(m + 1) * 2048],
                                 a[name][bass.ds((L * NE + e) * D, D), :].rearrange("(p c) f -> p (c f)", p=P)).then_inc(
                                     sem[done], 16)

                def load_down(e, u):
                    sp.dma_start(dn_ring[:, u, :].rearrange("p (j n) -> p j n", j=2),
                                 a["w_expert_down"][bass.ds((L * NE + e) * FF, FF), :].rearrange("(j p) n -> p j n", p=P)).then_inc(
                                     sem[f"dn{u}"], 16)

                for n, name in enumerate(CHUNKS):
                    load_chunk(n, name)
                settle(sp)
                for u in range(2):
                    sp.wait_ge(*at("pe_done", LAST[CHUNKS[len(CHUNKS) - 2 + u]] + 1))
                    load_expert(u, u, "w_expert_gate", 0, f"gu{u}")
                    load_expert(u, u, "w_expert_up", 1, f"up{u}")
                sp.wait_ge(*at("d_done", 0))
                load_down(0, 0)
                with sp.Fori(1, NE // 2) as ep:
                    for u in range(2):
                        e = ep * 2 + u
                        sp.wait_ge(*at("wg_done", e - 1))
                        load_expert(e, u, "w_expert_gate", 0, f"gu{u}")
                        sp.wait_ge(*at("g_done", e - 1))
                        load_expert(e, u, "w_expert_up", 1, f"up{u}")
                        sp.wait_ge(*at("d_done", e - 2))
                        load_down(e - 1, 1 - u)
                sp.wait_ge(*at("d_done", NE - 2))
                load_down(NE - 1, 1)

        @block.tensor
        def _(pe):
            mm, tr = nc.tensor.matmul, nc.tensor.transpose
            pe.wait_ge(sem["const_load"], 48)
            pe.wait_ge(sem["init"], INITS)
            with pe.Fori(0, DEPTH) as L:
                def at(name, k):
                    return sem[name], L * PER[name] + (START.get(name, 0) + k)

                def take(job):
                    n = JOBS[job]
                    pe.wait_ge(*at(f"free{n % 4}", n // 4))
                    return job_slab(job)

                def freed(job):
                    pe.wait_ge(*at(f"free{JOBS[job] % 4}", JOBS[job] // 4 + 1))

                def chunk(name):
                    n = CHUNKS.index(name)
                    pe.wait_ge(*at(f"gu{n % 2}", 16 * (n // 2 + 1)))
                    return gu_ring[:, n % 2, :]

                def norm_transposes(job, k0, then=None):
                    for i in range(NT):
                        if then and i >= 2:
                            then(i - 2)
                        s = take((job, i))
                        pe.wait_ge(*at("xn_ready", k0 + i + 1))
                        settle(pe)
                        for c in range(KC):
                            last = tr(s[:, c * P:c * P + TS[i]], xn[0:TS[i], i % 2, c:D:KC], ident[0:TS[i], 0:TS[i]])
                        last.then_inc(sem["pe_done"], 1)

                def token_major(name, n):
                    w = chunk(name)[:, 0:KC * n].rearrange("p (c n) -> p c n", c=KC)
                    for i in range(NT):
                        s = take((name, i))
                        for c in range(KC):
                            last = mm(s[0:TS[i], 0:n], xnT[:, c, T0[i]:T0[i] + TS[i]], w[:, c, :],
                                      start=c == 0, stop=c == KC - 1)
                        last.then_inc(sem["pe_done"], 1)

                def feature_major(job, lhs, rhs, nk):
                    take(job)
                    o = wide(job)
                    for lo, hi in ((0, 80), (80, LT)):
                        for c in range(nk):
                            last = mm(o[:, lo:hi], lhs(c), rhs(c, lo, hi), start=c == 0, stop=c == nk - 1)
                    last.then_inc(sem["pe_done"], 1)

                def project(name, key, j0, n):
                    w = chunk(name)[:, 0:KC * 512].rearrange("p (c n) -> p c n", c=KC)
                    for j in range(n):
                        feature_major((key, j0 + j), lambda c: w[:, c, j * P:(j + 1) * P],
                                      lambda c, lo, hi: xnT[:, c, lo:hi], KC)

                norm_transposes("xt", 0)
                freed(("xt", NT - 1))
                token_major("k3", 40)
                token_major("k2", 512)
                token_major("k1", 512)
                token_major("hi", 512)
                pe.wait_ge(*at("rope_ready", 1))
                for i in range(NT):
                    s = take(("it", i))
                    settle(pe)
                    n = TS[i]
                    idn = ident[0:n, 0:n]
                    tr(s[:, 0:n], qtok[0:n, i, 768:896], idn)
                    tr(s[:, 128:128 + n], qtok[0:n, i, 896:1024], idn)
                    tr(s[:, 256:256 + n], ikdup[0:n, i, :, :].rearrange("p r d -> p (r d)"), idn).then_inc(sem["pe_done"], 1)
                    s = take(("at", i))
                    settle(pe)
                    for c in range(4):
                        tr(s[:, c * P:c * P + n], qtok[0:n, i, c * P:(c + 1) * P], idn)
                    for g in range(2):
                        last = tr(s[:, (4 + g) * P:(4 + g) * P + n], kdup[0:n, i, g, :, :].rearrange("p r d -> p (r d)"), idn)
                    last.then_inc(sem["pe_done"], 1)
                project("hf", "hf", 0, 4)
                project("hq", "hq", 0, 4)

                freed(("it", NT - 1))
                freed(("at", NT - 1))
                for i in range(1, NT):
                    for hd in range(IH):
                        take(("ix", i, hd))
                        o = wide(("ix", i, hd))
                        r = 32 * (hd % 4)
                        for lo, hi in ((0, 80), (80, W[i])):
                            last = mm(o[0:TS[i], lo:hi], ixT[r:r + 32, hd // 4, T0[i]:T0[i] + TS[i]], ixT[r:r + 32, 2, lo:hi],
                                      start=True, stop=True, tile_position=(r, 0))
                        last.then_inc(sem["pe_done"], 1)

                freed(("hq", HH - 1))
                pe.wait_ge(*at("f_done", HH))
                for hd in range(HH):
                    for l in range(LEVELS):
                        s = take(("lv", hd, l))
                        if l > 0:
                            pe.wait_ge(*at("qe_ready", hd * 7 + l))
                        u = (hd * 7 + l - 1) % 2
                        for j in range(NT):
                            k_, q_ = (hk[:, hd, j, :], hq[:, hd, j, :]) if l == 0 else (
                                ke[:, u, j * P:(j + 1) * P], qe[:, u, j * P:(j + 1) * P])
                            last = mm(s[:, j * P:(j + 1) * P], k_, q_, start=True, stop=True)
                        last.then_inc(sem["pe_done"], 1)
                pe.wait_ge(*at("qb_ready", HH))
                pe.wait_ge(*at("kw_ready", HH))
                freed(("lv", HH - 1, LEVELS - 1))
                def update(j):
                    n = TS[j]
                    s = take(("kt", j))
                    settle(pe)
                    for hd in range(HH):
                        last = tr(s[0:n, hd * P:(hd + 1) * P], hk[:, hd, j, 0:n], ident[:, :])
                    last.then_inc(sem["pe_done"], 1)
                    s = take(("su", j))
                    settle(pe)
                    freed(("kt", j))
                    for hd in range(HH):
                        last = mm(s[:, hd * P:(hd + 1) * P], kwT[0:n, j % 2, hd * P:(hd + 1) * P],
                                  vH[0:n, j, hd * P:(hd + 1) * P], start=True, stop=True)
                    last.then_inc(sem["pe_done"], 1)

                def output(j):
                    n = TS[j]
                    s = take(("ot", j))
                    if j > 0:
                        settle(pe)
                        freed(("su", j - 1))
                    for hd in range(HH):
                        o = s[:, hd * P:hd * P + n]
                        if j > 0:
                            mm(o, S[(j - 1) % 2][:, hd, :], hq[:, hd, j, 0:n], start=True, stop=False)
                        last = mm(o, vH[0:n, j, hd * P:(hd + 1) * P], AT[0:n, hd, j, 0:n], start=j == 0, stop=True)
                    last.then_inc(sem["pe_done"], 1)

                for j in range(NT - 1):
                    update(j)
                    if j > 0:
                        output(j - 1)
                output(NT - 2)
                output(NT - 1)
                project("hg", "hg", 0, 4)
                for hd in range(HH):
                    s = take(("on", hd))
                    pe.wait_ge(*at("sq_ready", hd + 1))
                    mm(s[:, 0:512], ones[:, :], osq[:, hd, 0:512], start=True, stop=True)
                    mm(s[:, 512:640], ones[:, :], osq[:, hd, 512:640], start=True, stop=True).then_inc(sem["pe_done"], 1)
                project("ga0", "ga", 0, 4)
                project("ga1", "ga", 4, 4)
                w = chunk("wa").rearrange("p (c n) -> p c n", c=4)
                pe.wait_ge(*at("ya_ready", 1))
                yflat = [hq[:, k, :, :].rearrange("p j t -> p (j t)") for k in range(HH)]
                for c in range(8):
                    feature_major(("wa", c), lambda k: w[:, k, c * P:(c + 1) * P],
                                  lambda k, lo, hi: yflat[k][:, 0:80] if lo == 0 else yflat[k][:, P:P + LT - 80], HH)

                def scores(i, g):
                    for hd in range(4 * g, 4 * g + 4):
                        take(("qk", i, hd))
                        if TS[i] <= 64:
                            settle(pe)
                        o = wide(("qk", i, hd))
                        r = 64 * (hd % 2)
                        for lo, hi in ((0, 80), (80, W[i])):
                            if lo < hi:
                                last = mm(o[0:TS[i], lo:hi], aqk[r:r + 64, hd // 2, T0[i]:T0[i] + TS[i]],
                                          aqk[r:r + 64, 4 + g, lo:hi], start=True, stop=True, tile_position=(r, 0))
                        last.then_inc(sem["pe_done"], 1)

                scores(0, 0)
                groups = [(i, g) for i in range(NT) for g in range(2)]
                kts = 0
                for n_, (i, g) in enumerate(groups):
                    if n_ + 1 < len(groups):
                        scores(*groups[n_ + 1])
                    n = TS[i]
                    pe.wait_ge(*at("pn_ready", 4 * n_ + 4))
                    for k in range(i + 1):
                        s = take(("pt", i, g, k))
                        settle(pe)
                        for r in range(4):
                            hd = 4 * g + (0, 2, 1, 3)[r]
                            last = tr(s[0:TS[k], r * n:(r + 1) * n], pb[0:n, hd, T0[k]:T0[k] + TS[k]], ident[0:n, 0:n])
                        last.then_inc(sem["pe_done"], 1)
                    s = take(("pv", i, g))
                    for k in range(i + 1):
                        freed(("pt", i, g, k))
                        settle(pe)
                        for par in range(2):
                            last = mm(s[64 * par:64 * par + 64, 0:2 * n], vA[0:TS[k], k, g * AD:(g + 1) * AD],
                                      ptq[0:TS[k], (kts + k) % 4, par * 2 * n:(par + 1) * 2 * n],
                                      start=k == 0, stop=k == i, tile_position=(0, 64 * par))
                        if k < i:
                            last.then_inc(sem["pt_used"], 1)
                    last.then_inc(sem["pe_done"], 1)
                    kts += i + 1
                project("gb0", "gb", 0, 4)
                project("gb1", "gb", 4, 4)
                w = chunk("wb").rearrange("p (c n) -> p c n", c=4)
                freed(("pv", NT - 1, 1))
                for c in range(8):
                    feature_major(("wb", c), lambda k: w[:, k, c * P:(c + 1) * P], lambda k, lo, hi: ybT[:, k, lo:hi], 4)
                for half in range(2):
                    w = chunk(f"wo{half}").rearrange("p (c n) -> p c n", c=KC)
                    pe.wait_ge(*at("mg_ready", 8))
                    for i in range(NT):
                        s = take(("wo", half, i))
                        for c in range(KC):
                            last = mm(s[0:TS[i], 0:512], sga[:, c, T0[i]:T0[i] + TS[i]], w[:, c, :],
                                      start=c == 0, stop=c == KC - 1)
                        last.then_inc(sem["pe_done"], 1)

                def router(i):
                    s = take(("ro", i))
                    settle(pe)
                    freed(("xt2", i))
                    w = gu_ring[:, CHUNKS.index("ro") % 2, 0:288].rearrange("p (c n) -> p c n", c=KC)
                    for c in range(KC):
                        last = mm(s[0:TS[i], 0:36], xnT[:, c, T0[i]:T0[i] + TS[i]], w[:, c, :], start=c == 0, stop=c == KC - 1)
                    last.then_inc(sem["pe_done"], 1)

                chunk("ro")
                norm_transposes("xt2", NT, router)
                router(NT - 2)
                router(NT - 1)
                s = take(("rank",))
                pe.wait_ge(*at("c_ready", 1))
                for i in range(NT + 1):
                    for k in range(min(i + 1, NT)):
                        last = mm(s[:, i * NE:(i + 1) * NE], (tri if k == i else ones)[0:TS[k], :], Cs[0:TS[k], k, :],
                                  start=k == 0, stop=k == min(i, NT - 1))
                last.then_inc(sem["pe_done"], 1)
                s = take(("slot",))
                pe.wait_ge(*at("ab_ready", 1))
                for n in range(2 * NT):
                    last = mm(s[0:SLOTS, 0:NBLK], Am[0:TS[n % NT], n, :], Bm[0:TS[n % NT], n, :], start=n == 0, stop=n == 2 * NT - 1)
                last.then_inc(sem["pe_done"], 1)

                for s_ in range(4):
                    pe.wait_ge(*at(f"free{s_}", PER_SLAB[s_]))

                def transposes(e, u):
                    pe.wait_ge(*at(f"xg{u}", (e - u) * 8 + 16))
                    settle(pe)
                    for c in range(KC):
                        last = tr(slab(0)[:, u * 512 + c * SLOTS:u * 512 + (c + 1) * SLOTS], xg[0:SLOTS, u, c:D:KC], ident[0:SLOTS, 0:SLOTS])
                    last.then_inc(sem["t_done"], 1)

                def gate_or_up(e, u, m):
                    pe.wait_ge(*at(("wl_gate", "wl_up")[m], e + 1))
                    settle(pe)
                    parts = [w[:, m * 2048:(m + 1) * 2048].rearrange("p (c f) -> p c f", c=KC)
                             for w in (gu_high[u], gu_low[u])]
                    o = slab(1)[:, u * 512 + m * FF:u * 512 + (m + 1) * FF]
                    for c in range(KC):
                        for w in parts:
                            last = mm(o, xs[:, u, c, :, :].rearrange("p a s -> p (a s)"), w[:, c, :],
                                      start=c == 0 and w is parts[0], stop=c == KC - 1 and w is parts[1])
                    last.then_inc(sem[("wg_done", "g_done")[m]], 1)

                def gate_up(e, u):
                    pe.wait_ge(*at("xs_done", e + 1))
                    pe.wait_ge(*at("ge_done", e - 1))
                    gate_or_up(e, u, 0)
                    gate_or_up(e, u, 1)

                def fold_transposed(e, u):
                    pe.wait_ge(*at("ge_done", e + 1))
                    pe.wait_ge(*at("af_done", e - 1))
                    settle(pe)
                    for j in range(4):
                        last = mm(slab(3)[:, u * 512 + j * SLOTS:u * 512 + (j + 1) * SLOTS], guo[:, u, j * P:(j + 1) * P],
                                  fold, start=True, stop=True)
                    last.then_inc(sem["ft_done"], 1)

                def down(e, u):
                    pe.wait_ge(*at("am_done", e + 1))
                    pe.wait_ge(*at("wl_down", e + 1))
                    pe.wait_ge(*at("y_done", e))
                    settle(pe)
                    high, low = (w.rearrange("p (j n) -> p j n", j=2) for w in (dn_high[u], dn_low[u]))
                    for half in range(2):
                        cols = slice(half * 512, (half + 1) * 512)
                        for j in range(2):
                            for n, (part, w) in enumerate(((0, high), (0, low), (1, high))):
                                last = mm(slab(2)[0:SLOTS, cols], ams[:, u, j, part, :], w[:, j, cols],
                                          start=j == 0 and n == 0, stop=j == 1 and n == 2)
                    last.then_inc(sem["d_done"], 1)

                def expert(e, u, first=False, last=False):
                    gate_up(e, u)
                    if not last:
                        pe.wait_ge(*at("xs_done", e))
                        transposes(e + 1, 1 - u)
                    if not first:
                        down(e - 1, 1 - u)
                    fold_transposed(e, u)

                transposes(0, 0)
                expert(0, 0, first=True)
                expert(1, 1)
                with pe.Fori(1, NE // 2 - 1) as ep:
                    for u in range(2):
                        expert(ep * 2 + u, u)
                expert(NE - 2, 0)
                expert(NE - 1, 1, last=True)
                down(NE - 1, 1)

                pe.wait_ge(*at("base_ready", 1))
                settle(pe)
                n_over = pe.value_load(nov[0:1, 0:1], min_val=0, max_val=XBLK)
                with pe.If(n_over > 0):
                    with pe.Fori(0, XBLK) as x:
                        def ov(name, k=1):
                            return sem[name], (L * XBLK + x) * OV[name] + k * OV[name]

                        pe.wait_ge(*ov("ov_x"))
                        settle(pe)
                        for c in range(KC):
                            last = tr(slab(0)[:, c * SLOTS:(c + 1) * SLOTS], xg[0:SLOTS, 0, c:D:KC], ident[0:SLOTS, 0:SLOTS])
                        last.then_inc(sem["ov_t"], 1)
                        pe.wait_ge(*ov("ov_xt"))
                        pe.wait_ge(*ov("ov_w"))
                        w = ovw[:, 0:4096].rearrange("p (m c f) -> p m c f", m=2, c=KC)
                        for m in range(2):
                            for j in range(2):
                                o = slab(1)[:, (2 * m + j) * SLOTS:(2 * m + j + 1) * SLOTS]
                                for c in range(KC):
                                    last = mm(o, w[:, m, c, j * P:(j + 1) * P], xgT[:, c, :], start=c == 0, stop=c == KC - 1)
                        last.then_inc(sem["ov_g"], 1)
                        pe.wait_ge(*ov("ov_am"))
                        settle(pe)
                        w = ovw[:, 4096:6144].rearrange("p (j n) -> p j n", j=2)
                        for half in range(2):
                            for j in range(2):
                                last = mm(slab(2)[0:SLOTS, half * 512:(half + 1) * 512], am[:, j, :],
                                          w[:, j, half * 512:(half + 1) * 512], start=j == 0, stop=j == 1)
                        last.then_inc(sem["ov_d"], 1)
                with pe.Else():
                    for name in ("ov_t", "ov_g", "ov_d"):
                        pe.sem_inc(sem[name], XBLK)

        @block.vector
        def _(dve):
            V = nc.vector
            tt, ts, stt = V.tensor_tensor, V.tensor_scalar, V.scalar_tensor_tensor
            for r in (r1, r2):
                V.memset(r[:, :], 0.0).then_inc(sem["init"], 1)
            V.memset(small[:, :], 1.0).then_inc(sem["init"], 1)
            V.memset(sc[:, :, :], 0.0).then_inc(sem["init"], 1)
            for name in START:
                dve.sem_inc(sem[name], START[name])
            dve.wait_ge(sem["const_load"], 48)
            V.tensor_copy(lvm[:, :, :].rearrange("p l t -> p (l t)"), dn_ring[:, 0, 0:LEVELS * P]).then_inc(sem["init"], 1)
            dve.wait_ge(sem["init"], INITS)
            V.tensor_copy(sc[:, 0, 4:4 + W[0]], mask0).then_inc(sem["init"], 1)
            V.memset(lb, 0.0).then_inc(sem["init"], 1)
            tt(lb1, lbl[:, 0, :], lbl[:, 1, :], ALU.subtract).then_inc(sem["init"], 1)
            dve.wait_ge(sem["lbe"], 1)
            V.tensor_scalar_add(lb1, lb1, 1.0).then_inc(sem["init"], 1)
            dve.wait_ge(sem["init"], INITS + 4)
            V.reciprocal(lb1, lb1).then_inc(sem["init"], 1)
            dve.wait_ge(sem["init"], INITS + 5)

            with dve.Fori(0, DEPTH) as L:
                n_ = [0]

                def at(name, k):
                    return sem[name], L * PER[name] + (START.get(name, 0) + k)

                def chained(ins):
                    n_[0] += 1
                    ins.then_inc(sem["dve"], 1)
                    return n_[0]

                def after(n):
                    dve.wait_ge(*at("dve", n))

                def link(ins):
                    after(chained(ins))

                def done(job):
                    dve.wait_ge(*at("pe_done", JOBS[job] + 1))

                def free(job):
                    return sem[f"free{JOBS[job] % 4}"], 1

                def freed(job):
                    dve.wait_ge(*at(f"free{JOBS[job] % 4}", JOBS[job] // 4 + 1))

                def norm_rows(k0, then=None):
                    dve.wait_ge(*at("rms_ready", 1 + (k0 > 0)))
                    dve.wait_ge(*at("g_load", 16 * (1 + (k0 > 0))))
                    link(V.reciprocal(rstd, rms))
                    for i in range(NT):
                        n = TS[i]
                        if i >= 2:
                            done(("xt2" if k0 else "xt", i - 2))
                            if k0:
                                dve.wait_ge(*at(f"xw{i % 2}", 16 * (i // 2)))
                        stt(xn[0:n, i % 2, :], h[0:n, i, :], rstd[0:n, i:i + 1], gB[0:n, :], ALU.mult, ALU.mult).then_inc(
                            sem["xn_ready"], 1)
                        if then and i >= 2:
                            then(i - 2)

                norm_rows(0)

                dve.wait_ge(*at("par_load", 48))
                link(ts(llb, lb, 1e-18, None, ALU.max))
                ts(omlb, lb, -1.0, 1.0, ALU.mult, ALU.add).then_inc(sem["lb_ready"], 1)
                link(ts(dec[:, :, 0], lb, 1e-18, NEG, ALU.is_lt, ALU.mult))
                dve.wait_ge(*at("lb_ln", 1))
                link(tt(llb, llb, dec[:, :, 0], ALU.add))

                ik = qtok[:, :, 1024:1056]
                for i in range(1, NT):
                    freed(("k3", i))
                ikq = rt[:, 0:NT * ID].rearrange("p (i d) -> p i d", i=NT)
                link(tt(ikq, ik, ik, ALU.mult))
                V.tensor_reduce(kss, ikq, AX, ALU.add).then_inc(sem["ksq_ready"], 1)
                ts(iw, qtok[:, :, 1056:1064], IH ** -0.5 * ID ** -0.5, None, ALU.mult)
                dve.wait_ge(*at("ksq_ready", 1))

                def rope(x, heads, tab, half):
                    x1, x2 = x[:, :, :, 0:half], x[:, :, :, half:2 * half]
                    c, s = bc(tab[:, 0], 2, heads), bc(tab[:, 1], 2, heads)
                    n = NT * heads * half
                    t = [rt[:, k * n:(k + 1) * n].rearrange("p (i h d) -> p i h d", i=NT, h=heads) for k in range(4)]
                    tt(t[0], x1, c, ALU.mult)
                    tt(t[1], x2, s, ALU.mult)
                    tt(t[2], x2, c, ALU.mult)
                    link(tt(t[3], x1, s, ALU.mult))
                    tt(x1, t[0], t[1], ALU.subtract)
                    link(tt(x2, t[2], t[3], ALU.add))

                for i in range(1, NT):
                    freed(("k1", i))
                V.tensor_copy(vA[:, :, :], qtok[:, :, 640:768])
                rope(qtok[:, :, 0:640].rearrange("p i (h d) -> p i h d", d=AD), 10, rope_a, 8)
                for g in range(2):
                    V.tensor_copy(kdup[:, :, g, :, :], bc(qtok[:, :, 512 + g * AD:512 + (g + 1) * AD], 2, 2))
                dve.wait_ge(*at("kn_ready", 1))
                link(V.reciprocal(krms, krms))
                link(tt(ik, ik, bc(krms, 2, ID), ALU.mult))
                link(tt(ik, ik, bc(ik_g, 1, NT), ALU.mult))
                rope(qtok[:, :, 768:1056].rearrange("p i (h d) -> p i h d", d=ID), 9, rope_i, 4)
                V.tensor_copy(ikdup[:, :, :, :], bc(ik, 2, 4)).then_inc(sem["rope_ready"], 1)

                fb = pr[:, :].rearrange("p (k u t) -> p k u t", k=4, u=2)
                done(("at", NT - 1))
                pads = r1[:, :].rearrange("p (a j t) -> p a j t", a=3 * HH, j=NT)
                V.memset(pads[:, :, 0, TS[0]:], 0.0)
                link(V.memset(pads[:, :, NT - 1, TS[NT - 1]:], 0.0))

                def gate_in(j):
                    done(("hf", j))
                    z = wide(("hf", j))
                    ts(fb[:, 0, j % 2, :], z, -1.0, 40.0, ALU.mult, ALU.min).then_inc(sem["e_ready"], 1)
                    ts(fb[:, 1, j % 2, :], z, -1.0, 40.0, ALU.mult, ALU.max).then_inc(*free(("hf", j)))

                def padded(dst, j):
                    flat = dst[:, j, :, :].rearrange("p j t -> p (j t)")
                    return (flat[:, 0:80], slice(0, 80)), (flat[:, P:P + LT - 80], slice(80, LT))

                def gate_out(j):
                    e, ov, l1, l2 = (fb[:, k, j % 2, :] for k in range(4))
                    dve.wait_ge(*at("lnf_ready", j + 1))
                    link(tt(l2, l2, l1, ALU.subtract))
                    n1 = chained(stt(l2, l2, 40.0, ov, ALU.add, ALU.subtract))
                    n2 = chained(V.tensor_scalar_add(l1, e, 1.0))
                    after(n2)
                    n2 = chained(V.reciprocal(l1, l1))
                    for dst, cols in padded(hb, j):
                        ts(dst, l2[:, cols], llb[:, j:j + 1], None, ALU.max)
                    after(n2)
                    for dst, cols in padded(hk, j):
                        last = stt(dst, e[:, cols], omlb[:, j:j + 1], l1[:, cols], ALU.mult, ALU.mult)
                    link(last)
                    flat = hb[:, j, :, :].rearrange("p j t -> p (j t)")
                    V.tensor_tensor_scan(flat, reset, flat, 0.0, ALU.mult, ALU.add).then_inc(sem["f_done"], 1)

                gate_in(0)
                for j in range(HH):
                    if j + 1 < HH:
                        gate_in(j + 1)
                    gate_out(j)

                for i in range(1, NT):
                    n = TS[i]
                    V.memset(sc[0:n, i, 0:4], SENT)
                    for hd in range(IH):
                        m = (i - 1) * IH + hd
                        freed(("ix", i, hd))
                        if hd > 0:
                            dve.wait_ge(*at("rel_used", m))
                        acc, r_, w_ = sc[0:n, i, 4:4 + W[i]], rel[0:n, m % 2, 0:W[i]], iw[0:n, i, hd:hd + 1]
                        (ts(acc, r_, w_, None, ALU.mult) if hd == 0 else stt(acc, r_, w_, acc, ALU.mult, ALU.add)).then_inc(
                            sem["rel_used"], 1)
                    if i < NT - 1:
                        dve.wait_ge(*at("rel_used", i * IH))
                        V.memset(sc[0:64, i, 4 + W[i] - 64:4 + W[i]], HIDDEN)

                def differences(m):
                    hd, l = m // 7, m % 7 + 1
                    half = 2 ** (l - 1)
                    if m >= 2:
                        dve.wait_ge(*at("qe_ready", m - 1))
                    b = hb[:, hd, :, :].rearrange("p j t -> p (j t)").rearrange("p (n a t) -> p n a t", a=2, t=half)
                    e = ebuf[:, m % 2, :].rearrange("p (n a t) -> p n a t", a=2, t=half)
                    mid = b[:, :, 0, half - 1:half].broadcast_to([P, 640 // (2 * half), half])
                    tt(e[:, :, 1, :], b[:, :, 1, :], mid, ALU.subtract)
                    tt(e[:, :, 0, :], mid, b[:, :, 0, :], ALU.subtract).then_inc(sem["d_ready"], 1)

                def take_level(hd, l):
                    done(("lv", hd, l))
                    if l > 0:
                        freed(("lv", hd, l - 1))
                    settle(dve)
                    V.copy_predicated(AT[:, hd, :, :], bc(lvm[:, l, :], 1, NT),
                                      job_slab(("lv", hd, l))[:, 0:640].rearrange("p (j t) -> p j t", j=NT)).then_inc(
                                          *free(("lv", hd, l)))

                dve.wait_ge(*at("f_done", HH))
                dve.wait_ge(sem["y_init"], 16 * XBLK * SLOTS // (2 * P))
                differences(0)
                differences(1)
                for m in range(HH * 7):
                    if m % 7 == 0:
                        take_level(m // 7, 0)
                    if m + 2 < HH * 7:
                        differences(m + 2)
                    take_level(m // 7, m % 7 + 1)

                for hd in range(HH):
                    if hd >= 2:
                        dve.wait_ge(*at("kw_ready", hd - 1))
                    else:
                        dve.wait_ge(*at("qe_ready", 27 + hd))
                    b = hb[:, hd, :, :]
                    tt(ebuf[:, hd % 2, :].rearrange("p (j t) -> p j t", j=NT), b[:, :, P - 1:P].broadcast_to([P, NT, P]), b,
                       ALU.subtract).then_inc(sem["d_ready"], 1)
                    dve.wait_ge(*at("ex_ready", 28 + 2 * hd + 1))
                    q_ = hq[:, hd, :, :].rearrange("p j t -> p (j t)")
                    k_ = hk[:, hd, :, :].rearrange("p j t -> p (j t)")
                    tt(q_, q_, qe[:, hd % 2, :], ALU.mult).then_inc(sem["qb_ready"], 1)
                    dve.wait_ge(*at("ex_ready", 28 + 2 * hd + 2))
                    tt(k_, k_, ebuf[:, hd % 2, :], ALU.mult).then_inc(sem["kw_ready"], 1)

                dve.wait_ge(*at("ex_ready", 37))
                for j in range(NT - 1):
                    done(("ot", j - 1) if j > 1 else ("su", j))
                    s = job_slab(("su", j))
                    if j == 0:
                        V.tensor_copy(S0[:, :, :].rearrange("p h e -> p (h e)"), s[:, 0:512]).then_inc(*free(("su", j)))
                    else:
                        freed(("su", j - 1))
                        for hd in range(HH):
                            last = stt(S[j % 2][:, hd, :], S[(j - 1) % 2][:, hd, :], dec[:, hd, j:j + 1], s[:, hd * P:(hd + 1) * P], ALU.mult, ALU.add)
                        last.then_inc(*free(("su", j)))

                for hd in range(HH):
                    freed(("on", hd))
                    q_, k_, b_ = (r[:, hd, :, :].rearrange("p j t -> p (j t)") for r in (hq, hk, hb))
                    link(V.reciprocal(b_, b_))
                    link(stt(q_, q_, hn_g[:, hd:hd + 1], b_, ALU.mult, ALU.mult))
                    last = tt(q_, q_, k_, ALU.mult)
                    if hd == HH - 1:
                        last.then_inc(sem["ya_ready"], 1)

                def gated(c):
                    freed(("ga", c))
                    done(("wa", c))
                    tt(sga[:, c, :], wide(("wa", c)), sga[:, c, :], ALU.mult).then_inc(*free(("wa", c)))

                prev, rounds = {}, (TOPK + 4) // 8
                for r in range(rounds):
                    if r >= rounds - 3:
                        for c in (0, 1):
                            gated(2 * (r - rounds + 3) + c)
                    cur = {}
                    for i in range(1, NT):
                        if r:
                            after(prev[i])
                            settle(dve)
                        cur[i] = chained(V.max(top8[0:TS[i], i - 1, :], sc[0:TS[i], i, 0:4 + W[i]]))
                    for i in range(1, NT):
                        after(cur[i])
                        settle(dve)
                        s_ = sc[0:TS[i], i, 0:4 + W[i]]
                        prev[i] = chained(V.match_replace(s_, top8[0:TS[i], i - 1, :], s_, REPL))
                for i in range(1, NT):
                    after(prev[i])
                    s_ = sc[0:TS[i], i, 4:4 + W[i]]
                    prev[i] = chained(ts(s_, s_, 0.5 * (REPL + HIDDEN), NEG, ALU.is_gt, ALU.mult))
                after(prev[NT - 1])

                for c in range(6, 8):
                    gated(c)
                for c in range(4, 8):
                    freed(("wa", c))
                settle(dve)

                def score_max(m):
                    i, hd = m // 8, m % 8
                    n = TS[i]
                    done(("qk", i, hd))
                    settle(dve)
                    V.tensor_tensor_reduce(out=pb[0:n, hd, 0:W[i]], in0=wide(("qk", i, hd))[0:n, 0:W[i]], in1=sc[0:n, i, 4:4 + W[i]],
                                           scale=1.0, scalar=SCALAR_MIN, op0=ALU.add, op1=ALU.max,
                                           accum_out=mx[0:n, hd:hd + 1]).then_inc(*free(("qk", i, hd)))
                    freed(("qk", i, hd))
                    ts(nmx[0:n, hd:hd + 1], mx[0:n, hd:hd + 1], -AD ** -0.5, None, ALU.mult).then_inc(sem["mx_ready"], 1)

                def normalise(m):
                    i, hd = m // 8, m % 8
                    n = TS[i]
                    dve.wait_ge(*at("p_ready", m + 1))
                    link(V.reciprocal(pinv[0:n, hd:hd + 1], psum_[0:n, hd:hd + 1]))
                    ts(pb[0:n, hd, 0:W[i]], pb[0:n, hd, 0:W[i]], pinv[0:n, hd:hd + 1], None, ALU.mult).then_inc(sem["pn_ready"], 1)

                score_max(0)
                score_max(1)
                for m in range(40):
                    if m + 2 < 40:
                        score_max(m + 2)
                    normalise(m)

                for c in range(8):
                    freed(("gb", c))
                    done(("wb", c))
                    tt(sgb[:, c, :], wide(("wb", c)), sgb[:, c, :], ALU.mult).then_inc(*free(("wb", c)))
                    freed(("wb", c))
                    tt(sga[:, c, :], sga[:, c, :], sgb[:, c, :], ALU.add).then_inc(sem["mg_ready"], 1)
                for half in range(2):
                    for i in range(NT):
                        n = TS[i]
                        done(("wo", half, i))
                        o = h[0:n, i, half * 512:(half + 1) * 512]
                        tt(o, job_slab(("wo", half, i))[0:n, 0:512], o, ALU.add).then_inc(*free(("wo", half, i)))

                def logits(i):
                    done(("ro", i))
                    tt(lg[0:TS[i], i, :], job_slab(("ro", i))[0:TS[i], 0:36], rb[0:TS[i], :], ALU.add).then_inc(*free(("ro", i)))

                norm_rows(NT, logits)
                logits(NT - 2)
                logits(NT - 1)
                for i in range(NT):
                    freed(("ro", i))

                lgg, lge = lg[:, :, 0:NG], lg[:, :, NG:].rearrange("p i (g e) -> p i g e", g=NG)
                link(V.tensor_reduce(gmax, lgg, AX, ALU.max))
                tt(ge, lgg, bc(gmax, 2, NG), ALU.subtract).then_inc(sem["rt_ready"], 1)

                def first_of(x, mval, oh_, desc, nn, tmp):
                    link(tt(tmp, x, bc(mval, 2, nn), ALU.is_equal))
                    link(tt(tmp, tmp, bc(desc, 1, NT), ALU.mult))
                    link(V.tensor_reduce(vmx, tmp, AX, ALU.max))
                    link(tt(oh_, tmp, bc(vmx, 2, nn), ALU.is_equal))

                first_of(lgg, gmax, goh, descg, NG, goh)
                link(tt(lm, lge, bc(goh, 3, EPG), ALU.mult))
                link(V.tensor_reduce(ls, lm.rearrange("p i g e -> p i e g"), AX, ALU.add))
                link(V.tensor_reduce(m12[:, 0], ls, AX, ALU.max))
                first_of(ls, m12[:, 0], oh[:, 0], desce, EPG, eq)
                link(stt(ls2, oh[:, 0], NEG, ls, ALU.mult, ALU.add))
                link(V.tensor_reduce(m12[:, 1], ls2, AX, ALU.max))
                tt(dd, m12[:, 1], m12[:, 0], ALU.subtract).then_inc(sem["rt_ready"], 1)
                first_of(ls2, m12[:, 1], oh[:, 1], desce, EPG, eq)
                for c in range(2):
                    for g in range(NG):
                        last = tt(CC[:, c].rearrange("p i (g e) -> p i g e", g=NG)[:, :, g, :], bc(goh[:, :, g], 2, EPG), oh[:, c], ALU.mult)
                link(last)
                tt(Cs, CC[:, 0], CC[:, 1], ALU.add).then_inc(sem["c_ready"], 1)
                dve.wait_ge(*at("rt_exp", 2))
                link(V.tensor_reduce(gs, ge, AX, ALU.add))
                link(stt(gs, ed, 1.0, gs, ALU.add, ALU.mult))
                link(V.reciprocal(wcomb[:, 0], gs))
                link(tt(wcomb[:, 1], wcomb[:, 0], ed, ALU.mult))
                link(tt(tmpC, CC, bc(bc(ioe, 1, NT), 1, 2), ALU.mult))
                link(V.tensor_reduce(esel, tmpC, AX, ALU.add))
                done(("rank",))
                V.tensor_copy(rk.rearrange("p i n -> p (i n)"), job_slab(("rank",))[:, 0:6 * NE]).then_inc(*free(("rank",)))
                freed(("rank",))
                for c in range(2):
                    last = tt(tmpC[:, c], CC[:, c], rk[:, 0:NT, :], ALU.mult)
                link(last)
                link(V.tensor_reduce(rsel, tmpC, AX, ALU.add))
                link(tt(nxk, bc(rk[:, NT, :], 2, KMAX), bc(kthr, 1, NE), ALU.is_gt))
                link(V.tensor_reduce(nx, nxk, AX, ALU.add))
                link(V.tensor_tensor_scan(inc, ones[:, 0:NE], nx, 0.0, ALU.mult, ALU.add))
                link(tt(off, inc, nx, ALU.subtract))
                link(tt(tmpC, CC, bc(bc(off, 1, NT), 1, 2), ALU.mult))
                link(V.tensor_reduce(osel, tmpC, AX, ALU.add))
                r_, e_, o_ = (x.rearrange("p a i -> p (a i)") for x in (rsel, esel, osel))
                link(tt(qk_, bc(r_, 2, KMAX), bc(kthr, 1, 2 * NT), ALU.is_ge))
                link(V.tensor_reduce(qq, qk_, AX, ALU.add))
                link(stt(pos, qq, -float(SLOTS), r_, ALU.mult, ALU.add))
                link(ts(isov, qq, 1.0, None, ALU.min))
                link(tt(blk, o_, qq, ALU.add))
                link(stt(blk, blk, float(NE - 1), e_, ALU.add, ALU.subtract))
                link(tt(blk, blk, isov, ALU.mult))
                link(tt(blk, blk, e_, ALU.add))
                link(stt(slotf, blk, float(SLOTS), pos, ALU.mult, ALU.add))
                V.tensor_copy(sidx[:, :], slotf).then_inc(sem["sidx_ready"], 1)
                tt(Am, bc(io64, 1, 2 * NT), bc(pos, 2, SLOTS), ALU.is_equal)
                link(tt(Bm, bc(ioblk, 1, 2 * NT), bc(blk, 2, NBLK), ALU.is_equal))
                bm4 = Bm.rearrange("p (c i) n -> p c i n", c=2)
                tt(bm4[:, 0], bm4[:, 0], bc(tokid, 2, NBLK), ALU.mult)
                tt(bm4[:, 1], bm4[:, 1], bc(tokid, 2, NBLK), ALU.mult).then_inc(sem["ab_ready"], 1)
                link(tt(xcm, bc(inc, 1, XBLK), bc(ioblk[:, 0:XBLK], 2, NE), ALU.is_le))
                link(V.tensor_reduce(xef, xcm, AX, ALU.add))
                link(ts(xei[0:1, :], xef[0:1, :], float(NE - 1), None, ALU.min))
                V.tensor_copy(nov[0:1, 0:1], inc[0:1, NE - 1:NE]).then_inc(sem["base_ready"], 1)
                done(("slot",))
                V.tensor_copy(idx[:, :], job_slab(("slot",))[0:SLOTS, 0:NBLK]).then_inc(*free(("slot",)))
                V.tensor_copy(lb, lb1)

                def weight_low(e, u, part):
                    n = ("gate", "up", "down").index(part)
                    dve.wait_ge(*at(("wh_gate", "wh_up", "wh_down")[n], e + 1))
                    w, high, low = ((dn_ring[:, u, :], dn_high[u], dn_low[u]) if n == 2 else
                                    (x[:, n * 2048:(n + 1) * 2048] for x in (gu_ring[:, u, :], gu_high[u], gu_low[u])))
                    tt(low, w, high.bitcast(F32), ALU.subtract).then_inc(sem["wl_" + part], 1)

                def rows_low(e, u):
                    dve.wait_ge(*at("xs_hi", e + 1))
                    tt(xs[:, u, :, 1, :], slab(0)[:, u * 512:(u + 1) * 512].rearrange("p (c s) -> p c s", c=KC),
                       xs[:, u, :, 0, :].bitcast(F32), ALU.subtract).then_inc(sem["xs_done"], 1)

                def product(e, u):
                    dve.wait_ge(*at("si_done", e + 1))
                    tt(amf[:, u, :], slab(3)[:, u * 512 + 128:u * 512 + 256], sg[:, u, :], ALU.mult).then_inc(sem["af_done"], 1)
                    dve.wait_ge(*at("af_done", e + 1))
                    dve.wait_ge(*at("d_done", e - 1))
                    x = amf[:, u, :].rearrange("p (j s) -> p j s", j=2)
                    V.tensor_copy(ams[:, u, :, 0, :], x).then_inc(sem["ah_done"], 1)
                    dve.wait_ge(*at("ah_done", e + 1))
                    tt(ams[:, u, :, 1, :], x, ams[:, u, :, 0, :].bitcast(F32), ALU.subtract).then_inc(sem["am_done"], 1)

                def expert(e, u, last=False):
                    if not last:
                        weight_low(e + 1, 1 - u, "gate")
                        weight_low(e + 1, 1 - u, "up")
                        rows_low(e + 1, 1 - u)
                    product(e, u)
                    weight_low(e, u, "down")

                for part in ("gate", "up"):
                    weight_low(0, 0, part)
                rows_low(0, 0)
                with dve.Fori(0, NE // 2 - 1) as ep:
                    for u in range(2):
                        expert(ep * 2 + u, u)
                expert(NE - 2, 0)
                expert(NE - 1, 1, last=True)
                dve.wait_ge(*at("base_ready", 1))
                settle(dve)
                n_over = dve.value_load(nov[0:1, 0:1], min_val=0, max_val=XBLK)
                with dve.If(n_over > 0):
                    with dve.Fori(0, XBLK) as x:
                        dve.wait_ge(sem["ov_si"], L * XBLK + x + 1)
                        tt(am.rearrange("p j s -> p (j s)"), slab(1)[:, 128:256], sg[:, 0, :], ALU.mult).then_inc(sem["ov_am"], 1)
                with dve.Else():
                    dve.sem_inc(sem["ov_am"], XBLK)

                for k in range(2 * NT):
                    i, c = k // 2, k % 2
                    n = TS[i]
                    dve.wait_ge(*at(f"yg{k % 4}", 16 * (k // 4 + 1)))
                    if c:
                        dve.wait_ge(*at("cb_done", k))
                    stt(h[0:n, i, :], yg[0:n, k % 4, :], wcomb[0:n, c, i:i + 1], h[0:n, i, :], ALU.mult, ALU.add).then_inc(
                        sem["cb_done"], 1)
                assert n_[0] == PER["dve"], n_[0]

            dve.wait_ge(sem["fin_rms"], 1)
            dve.wait_ge(sem["fin_g"], 16)
            V.reciprocal(rstd, rms).then_inc(sem["fin_rms"], 1)
            dve.wait_ge(sem["fin_rms"], 2)
            for i in range(NT):
                n = TS[i]
                stt(h[0:n, i, :], h[0:n, i, :], rstd[0:n, i:i + 1], gB[0:n, :], ALU.mult, ALU.mult).then_inc(sem["fin_y"], 1)

        @block.scalar
        def _(act):
            A = nc.scalar.activation
            act.wait_ge(sem["init"], INITS + 3)
            A(lb1, lb1, ACT.Exp).then_inc(sem["lbe"], 1)
            act.wait_ge(sem["x_load"], 16 * len(xslices))

            def squares(rms_sem, value):
                pass

            with act.Fori(0, DEPTH) as L:
                n_ = [0]

                def at(name, k):
                    return sem[name], L * PER[name] + (START.get(name, 0) + k)

                def link(ins):
                    n_[0] += 1
                    ins.then_inc(sem["act"], 1)
                    act.wait_ge(*at("act", n_[0]))

                def done(job):
                    act.wait_ge(*at("pe_done", JOBS[job] + 1))

                def free(job):
                    return sem[f"free{JOBS[job] % 4}"], 1

                def freed(job):
                    act.wait_ge(*at(f"free{JOBS[job] % 4}", JOBS[job] // 4 + 1))

                def row_rms(weight):
                    act.dma_start(gB, a[weight][bass.ds(L, 1), :].broadcast_to([P, D])).then_inc(sem["g_load"], 16)
                    for i in range(NT):
                        if weight == "ffn_norm_g":
                            freed(("wo", 0, i))
                            freed(("wo", 1, i))
                        else:
                            act.wait_ge(*at("cb_done", 2 * (i + 1) - 2 * NT))
                        n = TS[i]
                        link(A(pr[0:n, 2048:3072], h[0:n, i, :], ACT.Square, accum_out=ss[0:n, i:i + 1]))
                    A(rms, ss, ACT.Sqrt, scale=1.0 / D, bias=eps_t).then_inc(sem["rms_ready"], 1)

                def padded(dst, j):
                    flat = dst[:, j, :, :].rearrange("p j t -> p (j t)")
                    return (flat[:, 0:80], slice(0, 80)), (flat[:, P:P + LT - 80], slice(80, LT))

                def evacuate(job, key):
                    for i in range(NT):
                        done((key, i))
                        A(xnT[:, :, T0[i]:T0[i] + TS[i]], job_slab((key, i)).rearrange("p (c t) -> p c t", c=KC)[:, :, 0:TS[i]],
                          ACT.Copy).then_inc(*free((key, i)))

                act.wait_ge(*at("d_done", 0))
                act.dma_start(ik_g, a["idx_k_norm_g"][bass.ds(L, 1), :].broadcast_to([P, ID])).then_inc(sem["par_load"], 16)
                act.dma_start(rb, a["router_b"][bass.ds(L, 1), :].broadcast_to([P, 36])).then_inc(sem["par_load"], 16)
                act.dma_start(hn_g, a["hgrn_norm_g"][bass.ds(L * P, P), :]).then_inc(sem["par_load"], 16)
                row_rms("mix_norm_g")
                evacuate("xt", "xt")
                act.wait_ge(*at("lb_ready", 1))
                A(llb, llb, ACT.Ln).then_inc(sem["lb_ln"], 1)
                for name, c0, n in (("k3", 1024, 40), ("k2", 512, 512), ("k1", 0, 512), ("hi", None, 512)):
                    if name == "hi":
                        act.wait_ge(*at("ksq_ready", 1))
                        A(krms, kss, ACT.Sqrt, scale=1.0 / ID, bias=eps_t).then_inc(sem["kn_ready"], 1)
                    if name == "k3":
                        act.wait_ge(*at("r1_clear", 0))
                    for i in range(NT):
                        done((name, i))
                        dst = vH[0:TS[i], i, :] if name == "hi" else qtok[0:TS[i], i, c0:c0 + n]
                        A(dst, job_slab((name, i))[0:TS[i], 0:n], ACT.Copy).then_inc(*free((name, i)))
                for i in range(NT):
                    done(("it", i))
                    A(ixT[:, :, T0[i]:T0[i] + TS[i]], job_slab(("it", i))[:, 0:384].rearrange("p (c t) -> p c t", c=3)[:, :, 0:TS[i]],
                      ACT.Copy).then_inc(*free(("it", i)))
                    done(("at", i))
                    A(aqk[:, :, T0[i]:T0[i] + TS[i]], job_slab(("at", i))[:, 0:768].rearrange("p (c t) -> p c t", c=6)[:, :, 0:TS[i]],
                      ACT.Copy).then_inc(*free(("at", i)))
                fb = pr[:, :].rearrange("p (k u t) -> p k u t", k=4, u=2)
                for j in range(HH):
                    e, l1, l2 = fb[:, 0, j % 2, :], fb[:, 2, j % 2, :], fb[:, 3, j % 2, :]
                    act.wait_ge(*at("e_ready", j + 1))
                    link(A(e, e, ACT.Exp))
                    A(l1, e, ACT.Ln, bias=one_t)
                    A(l2, e, ACT.Ln, bias=one_t, scale=lb[:, j:j + 1]).then_inc(sem["lnf_ready"], 1)
                for j in range(HH):
                    done(("hq", j))
                    o = wide(("hq", j))
                    (d0, c0), (d1, c1) = padded(hq, j)
                    A(d0, o[:, c0], ACT.Copy)
                    A(d1, o[:, c1], ACT.Copy).then_inc(*free(("hq", j)))
                for i in range(1, NT):
                    for hd in range(IH):
                        m = (i - 1) * IH + hd
                        done(("ix", i, hd))
                        if m >= 2:
                            act.wait_ge(*at("rel_used", m - 1))
                        A(rel[0:TS[i], m % 2, 0:W[i]], wide(("ix", i, hd))[0:TS[i], 0:W[i]], ACT.Relu).then_inc(*free(("ix", i, hd)))
                for m in range(HH * 7):
                    act.wait_ge(*at("d_ready", m + 1))
                    A(ebuf[:, m % 2, :], ebuf[:, m % 2, :], ACT.Exp).then_inc(sem["ex_ready"], 1)
                for hd in range(HH):
                    done(("lv", HH - 1, LEVELS - 1))
                    if hd >= 2:
                        act.wait_ge(*at("qb_ready", hd - 1))
                    A(qe[:, hd % 2, :], hb[:, hd, :, :].rearrange("p j t -> p (j t)"), ACT.Exp).then_inc(sem["ex_ready"], 1)
                    act.wait_ge(*at("d_ready", 28 + hd + 1))
                    A(ebuf[:, hd % 2, :], ebuf[:, hd % 2, :], ACT.Exp).then_inc(sem["ex_ready"], 1)
                A(dec, hb[:, :, :, P - 1], ACT.Exp).then_inc(sem["ex_ready"], 1)
                def state_rows(j):
                    n = TS[j]
                    done(("kt", j))
                    A(kwT[0:n, j % 2, :], job_slab(("kt", j))[0:n, 0:512], ACT.Copy).then_inc(*free(("kt", j)))

                state_rows(0)
                for j in range(NT):
                    if j + 1 < NT - 1:
                        state_rows(j + 1)
                    n = TS[j]
                    done(("ot", j))
                    A(hq[:, :, j, 0:n], job_slab(("ot", j))[:, 0:512].rearrange("p (h t) -> p h t", h=HH)[:, :, 0:n], ACT.Copy).then_inc(
                        *free(("ot", j)))
                for j in range(HH):
                    done(("hg", j))
                    o = wide(("hg", j))
                    (d0, c0), (d1, c1) = padded(hk, j)
                    A(d0, o[:, c0], ACT.Silu)
                    A(d1, o[:, c1], ACT.Silu).then_inc(*free(("hg", j)))
                for hd in range(HH):
                    done(("on", hd))
                    A(hb[:, hd, :, :].rearrange("p j t -> p (j t)"), job_slab(("on", hd))[:, 0:640], ACT.Sqrt, scale=1.0 / HD, bias=eps_t).then_inc(
                        *free(("on", hd)))
                act.wait_ge(*at("ya_ready", 1))
                for c in range(8):
                    done(("ga", c))
                    A(sga[:, c, :], wide(("ga", c)), ACT.Sigmoid).then_inc(*free(("ga", c)))

                def softmax_exp(m):
                    i, hd = m // 8, m % 8
                    n = TS[i]
                    act.wait_ge(*at("mx_ready", m + 1))
                    A(pb[0:n, hd, 0:W[i]], pb[0:n, hd, 0:W[i]], ACT.Exp, bias=nmx[0:n, hd:hd + 1], scale=AD ** -0.5,
                      accum_out=psum_[0:n, hd:hd + 1]).then_inc(sem["p_ready"], 1)

                for m in range(4):
                    softmax_exp(m)
                for n0 in range(2 * NT):
                    i, g = n0 // 2, n0 % 2
                    n = TS[i]
                    if n0 + 1 < 2 * NT:
                        for m in range(4 * n0 + 4, 4 * n0 + 8):
                            softmax_exp(m)
                    for k in range(i + 1):
                        m = PTS.index((i, g, k))
                        done(("pt", i, g, k))
                        if m >= 4:
                            b = PTS[m - 4]
                            if b[2] < b[0]:
                                act.wait_ge(*at("pt_used", PT_COUNT[b]))
                            else:
                                done(("pv", b[0], b[1]))
                        A(ptq[0:TS[k], m % 4, 0:4 * n], job_slab(("pt", i, g, k))[0:TS[k], 0:4 * n], ACT.Copy).then_inc(*free(("pt", i, g, k)))
                    done(("pv", i, g))
                    A(ybT[:, 2 * g:2 * g + 2, T0[i]:T0[i] + n], job_slab(("pv", i, g))[:, 0:2 * n].rearrange("p (c t) -> p c t", c=2),
                      ACT.Copy).then_inc(*free(("pv", i, g)))
                for c in range(8):
                    done(("gb", c))
                    A(sgb[:, c, :], wide(("gb", c)), ACT.Sigmoid).then_inc(*free(("gb", c)))
                row_rms("ffn_norm_g")
                for i in range(NT):
                    act.wait_ge(*at("xn_ready", NT + i + 1))
                    act.dma_start(xrow[T0[i]:T0[i] + TS[i], :], xn[0:TS[i], i % 2, :]).then_inc(sem[f"xw{i % 2}"], 16)
                    done(("xt2", i))
                    A(xnT[:, :, T0[i]:T0[i] + TS[i]], job_slab(("xt2", i)).rearrange("p (c t) -> p c t", c=KC)[:, :, 0:TS[i]],
                      ACT.Copy).then_inc(*free(("xt2", i)))
                act.wait_ge(*at("rt_ready", 1))
                A(ge, ge, ACT.Exp).then_inc(sem["rt_exp"], 1)
                act.wait_ge(*at("rt_ready", 2))
                A(ed, dd, ACT.Exp).then_inc(sem["rt_exp"], 1)

                def weight_high(e, u, part):
                    if part == "gate":
                        act.wait_ge(*at(f"gu{u}", 16 * len(CHUNKS) // 2 + (e - u) * 8 + 16))
                        act.wait_ge(*at("wg_done", e - 1))
                        w, high = gu_ring[:, u, 0:2048], gu_high[u][:, 0:2048]
                    elif part == "up":
                        act.wait_ge(*at(f"up{u}", (e - u) * 8 + 16))
                        act.wait_ge(*at("g_done", e - 1))
                        w, high = gu_ring[:, u, 2048:4096], gu_high[u][:, 2048:4096]
                    else:
                        act.wait_ge(*at(f"dn{u}", (e - u) * 8 + 16))
                        act.wait_ge(*at("d_done", e - 1))
                        w, high = dn_ring[:, u, :], dn_high[u]
                    A(high, w, ACT.Copy).then_inc(sem["wh_" + part], 1)

                def rows_high(e, u):
                    act.wait_ge(*at("t_done", e + 1))
                    act.wait_ge(*at("g_done", e - 1))
                    A(xs[:, u, :, 0, :], slab(0)[:, u * 512:(u + 1) * 512].rearrange("p (c s) -> p c s", c=KC),
                      ACT.Copy).then_inc(sem["xs_hi"], 1)

                def gate_up_out(e, u):
                    act.wait_ge(*at("g_done", e + 1))
                    act.wait_ge(*at("ft_done", e - 1))
                    A(guo[:, u, :], slab(1)[:, u * 512:(u + 1) * 512], ACT.Copy).then_inc(sem["ge_done"], 1)

                def silu(e, u):
                    act.wait_ge(*at("ft_done", e + 1))
                    act.wait_ge(*at("af_done", e - 1))
                    A(sg[:, u, :], slab(3)[:, u * 512:u * 512 + 128], ACT.Silu).then_inc(sem["si_done"], 1)

                def rows_out(e, u, first=False):
                    act.wait_ge(*at("d_done", e + 1))
                    if not first:
                        act.wait_ge(*at(f"yd{u}", (e - u) * 8))
                    A(ysb[0:SLOTS, u, :], slab(2)[0:SLOTS, :], ACT.Copy).then_inc(sem["y_done"], 1)
                    act.wait_ge(*at("y_done", e + 1))
                    act.dma_start(yrow[bass.ds(e * SLOTS, SLOTS), :] if not isinstance(e, int) else yrow[e * SLOTS:(e + 1) * SLOTS, :],
                                  ysb[0:SLOTS, u, :]).then_inc(sem[f"yd{u}"], 16)

                def expert(e, u, first=False, last=False):
                    if not last:
                        weight_high(e + 1, 1 - u, "gate")
                        weight_high(e + 1, 1 - u, "up")
                    gate_up_out(e, u)
                    if not last:
                        rows_high(e + 1, 1 - u)
                    if not first:
                        rows_out(e - 1, 1 - u, first=isinstance(e, int) and e <= 2)
                    silu(e, u)
                    weight_high(e, u, "down")

                for part in ("gate", "up"):
                    weight_high(0, 0, part)
                rows_high(0, 0)
                done(("slot",))
                expert(0, 0, first=True)
                expert(1, 1)
                expert(2, 0)
                expert(3, 1)
                with act.Fori(2, NE // 2 - 1) as ep:
                    for u in range(2):
                        expert(ep * 2 + u, u)
                expert(NE - 2, 0)
                expert(NE - 1, 1, last=True)
                rows_out(NE - 1, 1)
                for u in range(2):
                    act.wait_ge(*at(f"yd{u}", 8 * NE))
                act.wait_ge(*at("base_ready", 1))
                settle(act)
                n_over = act.value_load(nov[0:1, 0:1], min_val=0, max_val=XBLK)
                with act.If(n_over > 0):
                    with act.Fori(0, XBLK) as x:
                        def ov(name):
                            return sem[name], (L * XBLK + x) * OV[name] + OV[name]

                        act.wait_ge(*ov("ov_t"))
                        A(xgT.rearrange("p c s -> p (c s)"), slab(0)[:, 0:512], ACT.Copy).then_inc(sem["ov_xt"], 1)
                        act.wait_ge(*ov("ov_g"))
                        A(sg[:, 0, :], slab(1)[:, 0:128], ACT.Silu).then_inc(sem["ov_si"], 1)
                        act.wait_ge(*ov("ov_d"))
                        A(ysb[0:SLOTS, 0, :], slab(2)[0:SLOTS, :], ACT.Copy).then_inc(sem["ov_y"], 1)
                        act.wait_ge(*ov("ov_y"))
                        act.dma_start(yrow[bass.ds((x + NE) * SLOTS, SLOTS), :], ysb[0:SLOTS, 0, :]).then_inc(sem["ov_yd"], 16)
                        act.wait_ge(*ov("ov_yd"))
                with act.Else():
                    for name in ("ov_xt", "ov_si", "ov_y", "ov_yd"):
                        act.sem_inc(sem[name], XBLK * OV[name])
                assert n_[0] == PER["act"], n_[0]

            act.wait_ge(sem["d_done"], DEPTH * PER["d_done"] + START["d_done"])
            act.dma_start(gB, a["final_norm_g"].broadcast_to([P, D])).then_inc(sem["fin_g"], 16)
            for i in range(NT):
                n = TS[i]
                act.wait_ge(sem["cb_done"], (DEPTH - 1) * PER["cb_done"] + START["cb_done"] + 2 * (i + 1))
                A(pr[0:n, 2048:3072], h[0:n, i, :], ACT.Square, accum_out=ss[0:n, i:i + 1]).then_inc(sem["fin_ss"], 1)
                act.wait_ge(sem["fin_ss"], i + 1)
            A(rms, ss, ACT.Sqrt, scale=1.0 / D, bias=eps_t).then_inc(sem["fin_rms"], 1)
            outs = [(0, NMETA, 64, 0)] + [(i, 0, TS[i], T0[i] - NMETA) for i in range(1, NT)]
            for i, r, n, s0 in outs:
                act.wait_ge(sem["fin_y"], i + 1)
                act.dma_start(out[s0:s0 + n, :], h[r:r + n, i, :]).then_inc(sem["out_done"], 16)
            act.wait_ge(sem["out_done"], 16 * len(outs))

        @block.gpsimd
        def _(pool):
            G = nc.gpsimd
            for r in (pr[:, :], ptb[:, :, :], AT[:, :, :, :], vA[:, :, :], S0[:, :, :]):
                G.memset(r, 0.0).then_inc(sem["init"], 1)
            pool.wait_ge(sem["init"], INITS - 1)
            G.memset(eps_t, EPS).then_inc(sem["init"], 1)
            pool.wait_ge(sem["init"], INITS)
            pool.wait_ge(sem["pe_done"], JOBS[("k2", 0)] + 1)
            for n in range(XBLK * SLOTS // (2 * P)):
                r0 = NE * SLOTS + n * 2 * P
                pool.dma_start(yrow[r0:r0 + 2 * P, :].rearrange("(p a) n -> p (a n)", a=2),
                               zrow).then_inc(sem["y_init"], 16)
            with pool.Fori(0, DEPTH) as L:
                def at(name, k):
                    return sem[name], L * PER[name] + (START.get(name, 0) + k)

                pool.wait_ge(*at(*freed_at(("hq", HH - 1))))
                for m in range(HH * 7):
                    hd, l, u = m // 7, m % 7 + 1, m % 2
                    half = 2 ** (l - 1)
                    pool.wait_ge(*at("ex_ready", m + 1))
                    if m >= 2:
                        pool.wait_ge(*at("pe_done", JOBS[("lv", (m - 2) // 7, (m - 2) % 7 + 1)] + 1))
                    q_, k_, e_, qo, ko = (x.rearrange("p (n a t) -> p n a t", a=2, t=half) for x in (
                        hq[:, hd, :, :].rearrange("p j t -> p (j t)"), hk[:, hd, :, :].rearrange("p j t -> p (j t)"),
                        ebuf[:, u, :], qe[:, u, :], ke[:, u, :]))
                    G.tensor_tensor(qo[:, :, 1, :], q_[:, :, 1, :], e_[:, :, 1, :], ALU.mult)
                    G.tensor_tensor(ko[:, :, 0, :], k_[:, :, 0, :], e_[:, :, 0, :], ALU.mult).then_inc(sem["qe_ready"], 1)
                for hd in range(HH):
                    pool.wait_ge(*at(*freed_at(("ot", NT - 1))))
                    q_ = hq[:, hd, :, :].rearrange("p j t -> p (j t)")
                    G.tensor_tensor(osq[:, hd, :], q_, q_, ALU.mult).then_inc(sem["sq_ready"], 1)

                pool.wait_ge(*at("xw0", 48))
                pool.wait_ge(*at("xw1", 32))
                pool.wait_ge(*at(*freed_at(("slot",))))
                settle(pool)
                with pool.Fori(0, NE // 2) as ep:
                    for u in range(2):
                        e = ep * 2 + u
                        pool.wait_ge(*at("t_done", e - 1))
                        G.tensor_copy(stage[:, u:u + 1], idx[:, bass.ds(e, 1)]).then_inc(sem["stg"], 1)
                        pool.wait_ge(*at("stg", e + 1))
                        settle(pool)
                        pool.indirect_dma_start(xg[0:SLOTS, u, :], None, xrow, bass.IndirectOffsetOnAxis(ap=stage[:, u:u + 1], axis=0)).then_inc(
                            sem[f"xg{u}"], 16)
                pool.wait_ge(*at("base_ready", 1))
                settle(pool)
                n_over = pool.value_load(nov[0:1, 0:1], min_val=0, max_val=XBLK)
                with pool.If(n_over > 0):
                    pool.wait_ge(*at("d_done", NE))
                    settle(pool)
                    with pool.Fori(0, XBLK) as x:
                        def ov(name, k=0):
                            return sem[name], (L * XBLK + x) * OV[name] + OV[name]

                        ex = pool.value_load(xei[0:1, bass.ds(x, 1)], min_val=0, max_val=NE - 1)
                        for m, name in enumerate(("w_expert_gate", "w_expert_up")):
                            pool.dma_start(ovw[:, m * 2048:(m + 1) * 2048],
                                           a[name][bass.ds((L * NE + ex) * D, D), :].rearrange("(p c) f -> p (c f)", p=P)).then_inc(sem["ov_w"], 16)
                        pool.dma_start(ovw[:, 4096:6144].rearrange("p (j n) -> p j n", j=2),
                                       a["w_expert_down"][bass.ds((L * NE + ex) * FF, FF), :].rearrange("(j p) n -> p j n", p=P)).then_inc(
                                           sem["ov_w"], 16)
                        G.tensor_copy(stage[:, 0:1], idx[:, bass.ds(x + NE, 1)]).then_inc(sem["ov_stg"], 1)
                        pool.wait_ge(*ov("ov_stg"))
                        settle(pool)
                        pool.indirect_dma_start(xg[0:SLOTS, 0, :], None, xrow, bass.IndirectOffsetOnAxis(ap=stage[:, 0:1], axis=0)).then_inc(
                            sem["ov_x"], 16)
                        pool.wait_ge(*ov("ov_yd"))
                with pool.Else():
                    for name in ("ov_w", "ov_stg", "ov_x"):
                        pool.sem_inc(sem[name], XBLK * OV[name])

                pool.wait_ge(*at("t_done", NE))
                for u in range(2):
                    pool.wait_ge(*at(f"yd{u}", 8 * NE))
                pool.wait_ge(sem["ov_yd"], L * (16 * XBLK) + 16 * XBLK)
                pool.wait_ge(*at("sidx_ready", 1))
                settle(pool)
                for k in range(2 * NT):
                    if k >= 4:
                        pool.wait_ge(*at("cb_done", k - 3))
                        settle(pool)
                    i, c = k // 2, k % 2
                    n = TS[i]
                    pool.indirect_dma_start(yg[0:n, k % 4, :], None, yrow,
                                            bass.IndirectOffsetOnAxis(ap=sidx[0:n, c * NT + i:c * NT + i + 1], axis=0)).then_inc(
                                                sem[f"yg{k % 4}"], 16)
                G.memset(r1[:, 4096:], 0.0).then_inc(sem["r1_clear"], 1)


def kernel(x, meta_tokens, mix_norm_g, w_in, hgrn_lb_logits, hgrn_norm_g, idx_k_norm_g, w_branch_hgrn,
           w_branch_dsa, w_out, ffn_norm_g, router_group_w, router_group_b, router_expert_w, router_expert_b,
           w_expert_gate, w_expert_up, w_expert_down, final_norm_g):
    import concourse.bacc as bacc
    from concourse.bass_utils import run_bass_kernel_spmd

    consts, _, lvm = shape_constants()
    arrays = dict(
        consts=consts, level_masks=lvm,
        x=x.reshape(SEQ, D), meta_tokens=meta_tokens, mix_norm_g=mix_norm_g, w_in=w_in.reshape(DEPTH * D, -1),
        hgrn_lb_logits=hgrn_lb_logits.reshape(DEPTH, HH, P).transpose(2, 0, 1).reshape(P, DEPTH * HH),
        hgrn_norm_g=hgrn_norm_g.reshape(DEPTH, HH, P).transpose(0, 2, 1).reshape(DEPTH * P, HH), idx_k_norm_g=idx_k_norm_g,
        w_branch_hgrn=w_branch_hgrn.reshape(-1, D), w_branch_dsa=w_branch_dsa.reshape(-1, D), w_out=w_out.reshape(-1, D),
        ffn_norm_g=ffn_norm_g, router_w=np.concatenate([router_group_w, router_expert_w], -1).reshape(DEPTH * D, NG + NE),
        router_b=np.concatenate([router_group_b, router_expert_b], -1),
        w_expert_gate=w_expert_gate.reshape(-1, FF), w_expert_up=w_expert_up.reshape(-1, FF),
        w_expert_down=w_expert_down.reshape(-1, D), final_norm_g=final_norm_g.reshape(1, D),
    )
    nc = bacc.Bacc("TRN2", target_bir_lowering=False, num_devices=1)
    arrays = {n: np.ascontiguousarray(v) for n, v in arrays.items()}
    aps = {n: nc.dram_tensor(n, v.shape, mybir.dt.from_np(v.dtype), kind="ExternalInput").ap() for n, v in arrays.items()}
    out = nc.dram_tensor("out", (SEQ, D), F32, kind="ExternalOutput").ap()
    program(nc, aps, out)
    return run_bass_kernel_spmd(nc, [arrays], core_ids=[0]).results[0]["out"].reshape(1, SEQ, D)
```

```python
from contextlib import ExitStack

import concourse.bass as bass
from concourse import mybir
import numpy as np

F32 = mybir.dt.float32
F32R = mybir.dt.float32r
I32 = mybir.dt.int32
U8 = mybir.dt.uint8
ALU = mybir.AluOpType
ACT = mybir.ActivationFunctionType
AX = mybir.AxisListType.X

P = 128
D = 1024
KC = D // P
SEQ, NMETA = 512, 16
LT = SEQ + NMETA
DEPTH = 2
EPS = 1e-6
NT = 5
T0 = [0, 80, 208, 336, 464]
TS = [80, 128, 128, 128, 64]
W = [80, 208, 336, 464, 528]
TOPK = min(256, LT // 4)
HH, HD = 4, 128
AH, AD = 8, 64
IH, ID = 8, 32
NG, EPG = 4, 8
NE = NG * EPG
FF = D // 4
SLOTS = 64
XBLK = (2 * LT) // SLOTS
NBLK = NE + XBLK
KMAX = LT // SLOTS
REPL, HIDDEN, SENT, NEG = -3e38, -2e38, 3e38, -1e30
SCALAR_MIN = -3e38
INITS = 10

C_HQ, C_HF, C_HI, C_HG, C_AQ, C_AK, C_IK, C_GA, C_GB = 0, 512, 1024, 1536, 2048, 2560, 3072, 3112, 4136
CHUNKS = ["k3", "k2", "k1", "hi", "hf", "hq", "hg", "ga0", "ga1", "wa", "gb0", "gb1", "wb", "wo0", "wo1", "ro"]
SPLIT = ["k3", "k2", "k1", "hi", "hf", "hq", "hg", "ga0", "ga1", "gb0", "gb1", "wb", "wo0", "wo1"]
UNITS = {u: n for n, u in enumerate((c, q) for c in SPLIT for q in range(1 if c == "k3" else 4))}
HIGH_AFTER = {**{("hi", q): ("k2", NT - 1) for q in range(4)}, **{("hf", q): ("hi", NT - 1) for q in range(4)},
              **{("hq", q): ("hf", q) for q in range(4)}, **{("hg", q): ("hq", q) for q in range(4)},
              **{("ga0", q): ("hg", q) for q in range(4)}, **{("ga1", q): ("ga", q) for q in range(4)},
              **{("gb0", q): ("ga", 4 + q) for q in range(4)}, **{("gb1", q): ("gb", q) for q in range(4)}, **{("wo0", q): ("gb", 4 + q) for q in range(4)},
              **{("wb", q): ("qk", NT - 1, AH - 1) for q in range(4)},
              **{("wo1", q): ("wb", 7) for q in range(4)}}
LEVELS = 8


def mixed_jobs():
    for m in range(HH * LEVELS):
        yield ("lv", m // LEVELS, m % LEVELS)
        if m % 2:
            yield ("ix", 2 + m // 2 // IH, m // 2 % IH)


def plan_jobs():
    jobs, last = [], {}

    def add(*names):
        jobs.extend(names)
        return len(jobs) - 1

    add(*[("xt", i) for i in range(NT)])
    last["k3"] = add(("k3", 0))
    last["k2"] = add(*[("k2", i) for i in range(NT)])
    add(("k3t", 0))
    for c in ("k1", "hi"):
        last[c] = add(*[(c, i) for i in range(NT)])
    add(*[(n, i) for i in range(NT) for n in ("it", "at")])
    for c in ("hf", "hq"):
        last[c] = add(*[(c, j) for j in range(HH)])
    add(*[("ix", 1, h) for h in range(IH)])
    add(*mixed_jobs())
    add(*[("ix", NT - 1, h) for h in range(IH)])
    for j in range(NT - 1):
        add(("kt", j), ("su", j))
        if j > 0:
            add(("ot", j - 1))
    add(("ot", NT - 2), ("ot", NT - 1))
    last["hg"] = add(*[("hg", j) for j in range(HH)])
    add(*[("on", h) for h in range(HH)])
    last["ga0"] = add(*[("ga", c) for c in range(4)])
    last["ga1"] = add(*[("ga", c) for c in range(4, 8)])
    last["wa"] = add(*[("wa", c) for c in range(8)])
    groups = [(i, g) for i in range(NT) for g in range(2)]
    add(*[("qk", 0, h) for h in range(4)])
    for n, (i, g) in enumerate(groups):
        if n + 1 < len(groups):
            ni, ng = groups[n + 1]
            add(*[("qk", ni, 4 * ng + r) for r in range(4)])
        add(*[("pt", i, g, k) for k in range(i + 1)])
        add(("pv", i, g))
    last["gb0"] = add(*[("gb", c) for c in range(4)])
    last["gb1"] = add(*[("gb", c) for c in range(4, 8)])
    last["wb"] = add(*[("wb", c) for c in range(8)])
    last["wo0"] = add(*[("wo", 0, i) for i in range(NT)])
    last["wo1"] = add(*[("wo", 1, i) for i in range(NT)])
    add(("xt2", 0), ("xt2", 1))
    for i in range(2, NT):
        add(("ro", i - 2), ("xt2", i))
    last["ro"] = add(("ro", NT - 2), ("ro", NT - 1))
    add(("rank",), ("slot",))
    return {j: n for n, j in enumerate(jobs)}, last


JOBS, LAST = plan_jobs()
NJ = len(JOBS)
PER_SLAB = [len([n for n in JOBS.values() if n % 4 == s]) for s in range(4)]

DVE_OPS, ACT_OPS = 273, 14
PER = dict(
    pe_done=NJ, dve=DVE_OPS, act=ACT_OPS, ss_ready=0, rms_ready=2, xn_ready=2 * NT, ksq_ready=1,
    kn_ready=1, rope_ready=1, e_ready=HH, lnf_ready=HH, f_done=HH, rel_used=32, d_ready=32, ex_ready=37, qe_ready=28,
    qb_ready=HH, kw_ready=HH, sq_ready=HH, ya_ready=1, mx_ready=40, p_ready=40, pn_ready=40, pt_used=20, mg_ready=8,
    xw0=48, xw1=32, rt_ready=2, rt_exp=2, c_ready=1, ab_ready=1, idx_ready=1, base_ready=1, sidx_ready=1,
    g_load=32, par_load=48, lb_ready=1, lb_ln=1, stg=NE, xg0=16 * NE // 2, xg1=16 * NE // 2, t_done=NE, xs_hi=NE, xs_done=NE, wg_done=NE, g_done=NE,
    ge_done=NE, ft_done=NE, si_done=NE, af_done=NE, ah_done=NE, am_done=NE, wh_gate=NE, wh_up=NE, wh_down=NE, wl_gate=NE, wl_up=NE, wl_down=NE, d_done=NE, y_done=NE, yd0=16 * NE // 2, yd1=16 * NE // 2, yg0=48, yg1=48, yg2=32, yg3=32, cb_done=2 * NT, r1_clear=1,
    part_high=len(UNITS), part_low=len(UNITS), xh_ready=NT, mh_ready=8, ml_ready=8, yh_ready=4, yl_ready=4, h_out=16 * NT, h_in=16 * NT,
)
for _s in range(4):
    PER[f"free{_s}"] = PER_SLAB[_s]
for _s in range(2):
    PER[f"gu{_s}"] = 16 * len(CHUNKS) // 2 + 16 * NE // 2
    PER[f"up{_s}"] = 16 * NE // 2
    PER[f"dn{_s}"] = 16 * NE // 2
START = {"free0": 1, "free1": 1, "free2": 1, "free3": 1, "cb_done": 2 * NT + 1,
         **{n: 2 for n in ("t_done", "xs_done", "wg_done", "g_done", "ge_done", "ft_done", "af_done", "am_done", "d_done", "y_done")}}
OV = dict(ov_w=48, ov_stg=1, ov_x=16, ov_t=1, ov_xt=1, ov_g=1, ov_si=1, ov_am=1, ov_d=1, ov_y=1, ov_yd=16)
for _n, _k in OV.items():
    PER[_n] = _k * XBLK



def freed_at(job):
    return f"free{JOBS[job] % 4}", JOBS[job] // 4 + 1


PTS = [(i, g, k) for i in range(NT) for g in range(2) for k in range(i + 1)]
PT_COUNT = {b: len([x for x in PTS[:n + 1] if x[2] < x[0]]) for n, b in enumerate(PTS)}


def shape_constants():
    def rope(hd):
        rot = hd // 4
        inv = np.float32(500000.0) ** (-np.arange(0, rot, 2, dtype=np.float32) / np.float32(rot))
        ang = np.arange(LT, dtype=np.float32)[:, None] * inv[None, :]
        out = np.zeros((P, 2, NT, rot // 2), np.float32)
        for i in range(NT):
            out[:TS[i], 0, i] = np.cos(ang[T0[i]:T0[i] + TS[i]])
            out[:TS[i], 1, i] = np.sin(ang[T0[i]:T0[i] + TS[i]])
        return out.reshape(P, -1)

    s, t = np.arange(P)[:, None], np.arange(P)[None, :]
    lv = np.zeros((P, LEVELS, P), np.float32)
    lv[:, 0] = s == t
    for l in range(1, LEVELS):
        half = 2 ** (l - 1)
        lv[:, l] = (s // (2 * half) == t // (2 * half)) & (s % (2 * half) < half) & (t % (2 * half) >= half)
    cols = [
        np.eye(P), np.ones((P, P)), (s < t),
        rope(AD), rope(ID),
        np.broadcast_to(np.arange(64.0), (P, 64)), np.broadcast_to(np.arange(NBLK, dtype=float), (P, NBLK)),
        np.broadcast_to(np.arange(NE, dtype=float), (P, NE)),
        np.broadcast_to(np.arange(NG, 0, -1.0), (P, NG)), np.broadcast_to(np.arange(EPG, 0, -1.0), (P, EPG)),
        np.broadcast_to(SLOTS * np.arange(1.0, KMAX + 1), (P, KMAX)),
        np.arange(P)[:, None] + np.array(T0)[None, :],
        np.broadcast_to((np.arange(NT * P) % P != 0), (P, NT * P)),
        np.where((s < NMETA) & (np.arange(W[0])[None] >= NMETA), NEG, 0.0),
        np.arange(P)[:, None] % SLOTS == np.arange(SLOTS)[None],
    ]
    sizes = [c.shape[1] for c in cols]
    return np.concatenate([np.asarray(c, np.float32) for c in cols], 1), sizes, lv.reshape(P, -1)


def program(nc, a, out):
    _, sizes, _ = shape_constants()
    with ExitStack() as ctx:
        start = {}

        def sb(name, shape, dt=F32):
            start[name] = -(-nc.sbuf_base // 32) * 32
            return ctx.enter_context(nc.sbuf_tensor(name, shape, dt))

        def rounded(name, over, first, n):
            return nc.alloc_sbuf_tensor_at(name, [P, n], F32R, offset=start[over] + 4 * first)[:, :]

        sem = {n: ctx.enter_context(nc.semaphore(n)) for n in PER}
        for n in ("const_load", "x_load", "init", "lbe", "out_done", "fin_ss", "fin_g", "fin_rms", "fin_y", "settled", "y_init"):
            sem[n] = ctx.enter_context(nc.semaphore(n))

        h = sb("resid", [P, NT, D])
        xnT = sb("xnT", [P, KC, LT])
        gu_ring = sb("gu_ring", [P, 2, 4096])
        dn_ring = sb("dn_ring", [P, 2, 2048])
        r1 = sb("r1", [P, 3 * 2560])
        pr = sb("pr", [P, 4224])
        r2 = sb("r2", [P, 3168 + 1584 + 2560])
        AT = sb("AT", [P, HH, NT, P])
        sc = sb("sc", [P, NT, 4 + LT])
        vA = sb("vA", [P, NT, 2 * AD])
        ptb = sb("ptb", [P, 2, 1024])
        S0 = sb("S", [P, HH, HD])
        consts = sb("tables", [P, sum(sizes)])
        lvm = sb("masks_u8", [P, LEVELS, P], U8)
        small = sb("small", [P, 1300])

        qtok = r1[:, 0:NT * 1064].rearrange("p (i n) -> p i n", i=NT)
        hq, hk, hb = (r1[:, n * 2560:(n + 1) * 2560].rearrange("p (h j t) -> p h j t", h=HH, j=NT) for n in range(3))
        sga = r1[:, 2560:2560 + 8 * LT].rearrange("p (c t) -> p c t", c=8)
        xg = r1[:, 0:2048].rearrange("p (u n) -> p u n", u=2)
        ysb = r1[:, 2048:4096].rearrange("p (u n) -> p u n", u=2)
        yg = r1[:, 0:4096].rearrange("p (u n) -> p u n", u=4)
        xs = rounded("x_parts", "r1", 4096, 2048).rearrange("p (u c a s) -> p u c a s", u=2, c=KC, a=2)
        guo = r1[:, 6144:7168].rearrange("p (u n) -> p u n", u=2)
        ams = rounded("act_parts", "r1", 7168, 512).rearrange("p (u j a s) -> p u j a s", u=2, j=2, a=2)
        xgT = r1[:, 4096:4608].rearrange("p (c s) -> p c s", c=KC)
        am = r1[:, 7168:7296].rearrange("p (j s) -> p j s", j=2)
        xn = pr[:, 0:2048].rearrange("p (u n) -> p u n", u=2)
        kdup = pr[:, 0:1280].rearrange("p (i g r d) -> p i g r d", i=NT, g=2, r=2)
        ikdup = pr[:, 1280:1920].rearrange("p (i r d) -> p i r d", i=NT, r=4)
        k3f = pr[:, 2048:2048 + LT]
        rt = pr[:, 1920:4224]
        ebuf, qe, ke = (pr[:, n * 1280:(n + 1) * 1280].rearrange("p (u t) -> p u t", u=2) for n in range(3))
        osq = pr[:, 0:2560].rearrange("p (h t) -> p h t", h=HH)
        pb = pr[:, :].rearrange("p (h t) -> p h t", h=8)
        sgb = pb
        aqk = r2[:, 0:3168].rearrange("p (c t) -> p c t", c=6)
        ixT = r2[:, 3168:4752].rearrange("p (c t) -> p c t", c=3)
        kwT = r2[:, 3168:4192].rearrange("p (u n) -> p u n", u=2)
        vH = r2[:, 4752:7312].rearrange("p (i n) -> p i n", i=NT)
        ybT = r2[:, 4752:4752 + 4 * LT].rearrange("p (c t) -> p c t", c=4)
        ovw = r2[:, 0:6144]
        sg, amf = (r2[:, 6144 + n * 256:6400 + n * 256].rearrange("p (u n) -> p u n", u=2) for n in range(2))
        gu_high = [rounded("gate_up_high0", "r2", 0, 4096), rounded("gate_up_high1", "xnT", 0, 4096)]
        dn_high = [rounded("down_high0", "r2", 4096, 2048), rounded("down_high1", "ptb", 0, 2048)]
        gu_low = [rounded(f"gate_up_low{u}", "gu_ring", 4096 * u, 4096) for u in range(2)]
        dn_low = [rounded(f"down_low{u}", "dn_ring", 2048 * u, 2048) for u in range(2)]
        gB = ptb[:, 0, :]
        rel = ptb[:, :, 0:LT]
        S = [S0, ptb[:, 1, 0:HH * HD].rearrange("p (h e) -> p h e", h=HH)]
        ptq = ptb[:, :, :].rearrange("p a (b n) -> p (a b) n", b=2)

        at_ = [0]

        def const(n):
            at_[0] += sizes[n]
            return consts[:, at_[0] - sizes[n]:at_[0]]

        ident, ones, tri, rope_a, rope_i, io64, ioblk, ioe, descg, desce, kthr, tokid, reset, mask0, fold = (
            const(n) for n in range(15))
        rope_a = rope_a.rearrange("p (a i d) -> p a i d", a=2, i=NT)
        rope_i = rope_i.rearrange("p (a i d) -> p a i d", a=2, i=NT)

        at_[0] = 0

        def tiny(n):
            at_[0] += n
            return small[:, at_[0] - n:at_[0]]

        ss, rms, rstd = tiny(NT), tiny(NT), tiny(NT)
        kss, krms = tiny(NT), tiny(NT)
        ik_g = tiny(ID)
        iw = tiny(NT * IH).rearrange("p (i h) -> p i h", i=NT)
        hn_g = tiny(HH)
        lb, lb1, omlb, llb = tiny(HH), tiny(HH), tiny(HH), tiny(HH)
        dec = tiny(HH * NT).rearrange("p (h j) -> p h j", h=HH)
        top8 = tiny(4 * 8).rearrange("p (i k) -> p i k", i=4)
        mx, nmx, psum_, pinv = tiny(8), tiny(8), tiny(8), tiny(8)
        rb = tiny(36)
        eps_t = tiny(1)
        one_t = tiny(1)
        lg = tiny(NT * 36).rearrange("p (i n) -> p i n", i=NT)
        wcomb = tiny(2 * NT).rearrange("p (a i) -> p a i", a=2)
        rto = [2048]

        def rtt(n):
            rto[0] += n
            return pr[:, rto[0] - n:rto[0]]

        gmax, gs = rtt(NT), rtt(NT)
        ge = rtt(NT * NG).rearrange("p (i g) -> p i g", i=NT)
        goh = rtt(NT * NG).rearrange("p (i g) -> p i g", i=NT)
        vmx = rtt(NT)
        lm = rtt(NT * NE).rearrange("p (i g e) -> p i g e", i=NT, g=NG)
        ls = rtt(NT * EPG).rearrange("p (i e) -> p i e", i=NT)
        ls2 = rtt(NT * EPG).rearrange("p (i e) -> p i e", i=NT)
        m12 = rtt(2 * NT).rearrange("p (a i) -> p a i", a=2)
        eq = rtt(NT * EPG).rearrange("p (i e) -> p i e", i=NT)
        oh = rtt(2 * NT * EPG).rearrange("p (a i e) -> p a i e", a=2, i=NT)
        dd = rtt(NT)
        ed = rtt(NT)
        CC = rtt(2 * NT * NE).rearrange("p (a i n) -> p a i n", a=2, i=NT)
        Cs = rtt(NT * NE).rearrange("p (i n) -> p i n", i=NT)
        tmpC = rtt(2 * NT * NE).rearrange("p (a i n) -> p a i n", a=2, i=NT)
        rk = rtt(6 * NE).rearrange("p (i n) -> p i n", i=6)
        rsel, esel, osel = (rtt(2 * NT).rearrange("p (a i) -> p a i", a=2) for _ in range(3))
        nxk = rtt(NE * KMAX).rearrange("p (n k) -> p n k", n=NE)
        nx, inc, off = rtt(NE), rtt(NE), rtt(NE)
        qk_ = rtt(2 * NT * KMAX).rearrange("p (a k) -> p a k", k=KMAX)
        qq, pos, blk, isov, slotf = (rtt(2 * NT) for _ in range(5))
        Bm = ptb[:, 0, 0:2 * NT * NBLK].rearrange("p (a n) -> p a n", n=NBLK)
        Am = ptb[:, 1, 0:2 * NT * SLOTS].rearrange("p (a n) -> p a n", n=SLOTS)
        xef = rtt(XBLK)
        xcm = r1[:, 5632:5632 + XBLK * NE].rearrange("p (x n) -> p x n", n=NE)
        lbl = sb("lbl", [P, 2, HH])
        sidx = sb("sidx", [P, 2 * NT], I32)
        idx = sb("idx", [SLOTS, NBLK], I32)
        stage = sb("stage", [SLOTS, 2], I32)
        xei = sb("xei", [1, XBLK], I32)
        nov = sb("nov", [1, 1], I32)

        zrow = AT[:, :, :, :].rearrange("p h j t -> p (h j t)")[:, 0:2 * D]

        xh = rounded("x_high", "xnT", 0, KC * LT).rearrange("p (c t) -> p c t", c=KC)
        xl = rounded("x_low", "resid", 0, KC * LT).rearrange("p (c t) -> p c t", c=KC)
        yh = rounded("y_dsa_high", "r1", 0, 4 * LT).rearrange("p (c t) -> p c t", c=4)
        yl = rounded("y_dsa_low", "r2", 4752, 4 * LT).rearrange("p (c t) -> p c t", c=4)
        ml = rounded("merged_low", "r1", 2560, KC * LT).rearrange("p (c t) -> p c t", c=KC)
        high_a, high_b = rounded("chunk_high_a", "dn_ring", 0, 4096), rounded("chunk_high_b", "r2", 0, 4416)

        def parts(name):
            slot, nk, nn = CHUNKS.index(name) % 2, 4 if name == "wb" else KC, {"k3": 40, "wb": 1024}.get(name, 512)
            high = {"k3": high_b[:, 4096:], "k1": high_b, "wb": high_b, "wo1": high_b}.get(name, high_a)
            return [x[:, 0:nk * nn].rearrange("p (c n) -> p c n", c=nk) for x in (gu_ring[:, slot, :], high, gu_low[slot])]

        def quarter(name, q):
            n = {"k3": 40, "wb": 2 * P}.get(name, P)
            return slice(q * n, (q + 1) * n)

        ps = ctx.enter_context(nc.psum_tensor("ps", [P, 4096], F32))

        def slab(n):
            return ps[:, (n % 4) * 1024:(n % 4 + 1) * 1024]

        def job_slab(job):
            return slab(JOBS[job])

        def wide(job):
            first = 512 - (LT // 2 if job[0] in ("k3", "hf", "hq", "hg", "ga", "gb", "wb") else 80)
            return job_slab(job)[:, first:first + LT]

        xrow = nc.dram_tensor("xrow", (LT, D), F32, kind="Internal").ap()
        hrow = nc.dram_tensor("hrow", (LT, D), F32, kind="Internal").ap()
        yrow = nc.dram_tensor("yrow", (NBLK * SLOTS, D), F32, kind="Internal").ap()

        def bc(ap, axis, n):
            ap = ap.unsqueeze(axis)
            shape = list(ap.shape)
            shape[axis] = n
            return ap.broadcast_to(shape)

        xslices = [(0, 0, NMETA, "meta", 0), (0, NMETA, 64, "x", 0)] + [
            (i, 0, TS[i], "x", T0[i] - NMETA) for i in range(1, NT)]
        block = ctx.enter_context(nc.Block())

        def settle(eng):
            eng.sem_inc(sem["settled"], 1)

        @block.sync
        def _(sp):
            sp.dma_start(consts[:, :], a["consts"]).then_inc(sem["const_load"], 16)
            sp.dma_start(dn_ring[:, 0, 0:LEVELS * P], a["level_masks"]).then_inc(sem["const_load"], 16)
            sp.dma_start(lbl[:, :, :].rearrange("p a h -> p (a h)"), a["hgrn_lb_logits"]).then_inc(sem["const_load"], 16)
            for i, r, n, src, s0 in xslices:
                s = a["meta_tokens"] if src == "meta" else a["x"][s0:s0 + n, :]
                sp.dma_start(h[r:r + n, i, :], s).then_inc(sem["x_load"], 16)

            w_in = a["w_in"].rearrange("(l p c) n -> l p c n", l=DEPTH, p=P)

            with sp.Fori(0, DEPTH) as L:
                def at(name, k):
                    return sem[name], L * PER[name] + (START.get(name, 0) + k)

                def rows(name, per, r):
                    w = a[name]
                    return w[bass.ds(L * per + r, P), :]

                def load_chunk(n, name):
                    slot = gu_ring[:, n % 2, :]
                    if n >= 2:
                        sp.wait_ge(*at("pe_done", LAST[CHUNKS[n - 2]] + 1))
                    else:
                        sp.wait_ge(*at("g_done", 0))
                    settle(sp)
                    if name in ("wa", "wb"):
                        w = a["w_branch_hgrn" if name == "wa" else "w_branch_dsa"]
                        sp.dma_start(slot.rearrange("p (c n) -> p c n", c=4),
                                     w[bass.ds(L * 512, 512), :].rearrange("(c p) n -> p c n", p=P)).then_inc(
                                         sem[f"gu{n % 2}"], 16)
                    elif name[:2] == "wo":
                        c0 = 512 * int(name[2])
                        sp.dma_start(slot.rearrange("p (c n) -> p c n", c=8),
                                     a["w_out"][bass.ds(L * D, D), c0:c0 + 512].rearrange("(c p) n -> p c n", p=P)).then_inc(
                                         sem[f"gu{n % 2}"], 16)
                    elif name == "ro":
                        sp.dma_start(slot[:, 0:288].rearrange("p (c n) -> p c n", c=8),
                                     a["router_w"][bass.ds(L * D, D), :].rearrange("(p c) n -> p c n", p=P)).then_inc(
                                         sem[f"gu{n % 2}"], 16)
                    else:
                        c0, nn = {"k3": (C_IK, 40), "k2": (C_AK, 512), "k1": (C_AQ, 512), "hi": (C_HI, 512),
                                  "hf": (C_HF, 512), "hq": (C_HQ, 512), "hg": (C_HG, 512), "ga0": (C_GA, 512),
                                  "ga1": (C_GA + 512, 512), "gb0": (C_GB, 512), "gb1": (C_GB + 512, 512)}[name]
                        sp.dma_start(slot[:, 0:8 * nn].rearrange("p (c n) -> p c n", c=8),
                                     a["w_in"][bass.ds(L * D, D), c0:c0 + nn].rearrange("(p c) n -> p c n", p=P)).then_inc(
                                         sem[f"gu{n % 2}"], 16)

                def load_expert(e, u, name, m, done):
                    sp.dma_start(gu_ring[:, u, m * 2048:(m + 1) * 2048],
                                 a[name][bass.ds((L * NE + e) * D, D), :].rearrange("(p c) f -> p (c f)", p=P)).then_inc(
                                     sem[done], 16)

                def load_down(e, u):
                    sp.dma_start(dn_ring[:, u, :].rearrange("p (j n) -> p j n", j=2),
                                 a["w_expert_down"][bass.ds((L * NE + e) * FF, FF), :].rearrange("(j p) n -> p j n", p=P)).then_inc(
                                     sem[f"dn{u}"], 16)

                for n, name in enumerate(CHUNKS):
                    load_chunk(n, name)
                    if name == "wo0":
                        sp.wait_ge(*at("h_out", 16 * NT))
                        for i in range(NT):
                            sp.dma_start(h[0:TS[i], i, :], hrow[T0[i]:T0[i] + TS[i], :]).then_inc(sem["h_in"], 16)
                settle(sp)
                for u in range(2):
                    sp.wait_ge(*at("pe_done", LAST[CHUNKS[len(CHUNKS) - 2 + u]] + 1))
                    load_expert(u, u, "w_expert_gate", 0, f"gu{u}")
                    load_expert(u, u, "w_expert_up", 1, f"up{u}")
                sp.wait_ge(*at("d_done", 0))
                load_down(0, 0)
                load_down(1, 1)

                def load(e, u, down_too=True):
                    sp.wait_ge(*at("wg_done", e - 1))
                    load_expert(e, u, "w_expert_gate", 0, f"gu{u}")
                    sp.wait_ge(*at("g_done", e - 1))
                    load_expert(e, u, "w_expert_up", 1, f"up{u}")
                    if down_too:
                        sp.wait_ge(*at("d_done", e - 2))
                        load_down(e - 1, 1 - u)

                load(2, 0, down_too=False)
                load(3, 1)
                with sp.Fori(2, NE // 2) as ep:
                    for u in range(2):
                        load(ep * 2 + u, u)
                sp.wait_ge(*at("d_done", NE - 2))
                load_down(NE - 1, 1)

        @block.tensor
        def _(pe):
            mm, tr = nc.tensor.matmul, nc.tensor.transpose
            pe.wait_ge(sem["const_load"], 48)
            pe.wait_ge(sem["init"], INITS)
            with pe.Fori(0, DEPTH) as L:
                def at(name, k):
                    return sem[name], L * PER[name] + (START.get(name, 0) + k)

                def take(job):
                    n = JOBS[job]
                    pe.wait_ge(*at(f"free{n % 4}", n // 4))
                    return job_slab(job)

                def freed(job):
                    pe.wait_ge(*at(f"free{JOBS[job] % 4}", JOBS[job] // 4 + 1))

                def chunk(name):
                    n = CHUNKS.index(name)
                    pe.wait_ge(*at(f"gu{n % 2}", 16 * (n // 2 + 1)))
                    return gu_ring[:, n % 2, :]

                def norm_transposes(job, k0, then=None):
                    for i in range(NT):
                        if then and i >= 2:
                            then(i - 2)
                        s = take((job, i))
                        pe.wait_ge(*at("xn_ready", k0 + i + 1))
                        settle(pe)
                        for c in range(KC):
                            last = tr(s[:, c * P:c * P + TS[i]], xn[0:TS[i], i % 2, c:D:KC], ident[0:TS[i], 0:TS[i]])
                        last.then_inc(sem["pe_done"], 1)

                def low_parts(name, q):
                    pe.wait_ge(*at("part_low", UNITS[name, q] + 1))

                def token_major(name, n, x_low, job):
                    low_parts(name, 3)
                    _, wh, wl = parts(name)
                    for i in range(NT):
                        s = take((*job, i))
                        settle(pe)
                        for c in range(KC):
                            for k, (x, w) in enumerate(((xh, wh), (xh, wl), (x_low, wh))):
                                last = mm(s[0:TS[i], 0:n], x[:, c, T0[i]:T0[i] + TS[i]], w[:, c, :],
                                          start=c == 0 and k == 0, stop=c == KC - 1 and k == 2)
                        last.then_inc(sem["pe_done"], 1)

                def feature_major(job, lhs, rhs, nk):
                    take(job)
                    o = wide(job)
                    for lo, hi in ((0, 80), (80, LT)):
                        for c in range(nk):
                            last = mm(o[:, lo:hi], lhs(c), rhs(c, lo, hi), start=c == 0, stop=c == nk - 1)
                    last.then_inc(sem["pe_done"], 1)

                def project(name, key, j0, n):
                    _, wh, wl = parts(name)
                    for j in range(n):
                        low_parts(name, j)
                        take((key, j0 + j))
                        settle(pe)
                        o = wide((key, j0 + j))[0:40 if name == "k3" else P]
                        for lo, hi in ((0, LT // 2), (LT // 2, LT)):
                            for c in range(KC):
                                for k, (w, x) in enumerate(((wh, xh), (wh, xl), (wl, xh))):
                                    last = mm(o[:, lo:hi], w[:, c, quarter(name, j)], x[:, c, lo:hi],
                                              start=c == 0 and k == 0, stop=c == KC - 1 and k == 2)
                        last.then_inc(sem["pe_done"], 1)

                norm_transposes("xt", 0)
                freed(("xt", NT - 1))
                project("k3", "k3", 0, 1)
                token_major("k2", 512, xl, ("k2",))
                s = take(("k3t", 0))
                settle(pe)
                freed(("k3", 0))
                settle(pe)
                for i in range(NT):
                    last = tr(s[0:TS[i], i * 40:(i + 1) * 40], k3f[0:40, T0[i]:T0[i] + TS[i]], ident[0:40, 0:40])
                last.then_inc(sem["pe_done"], 1)
                token_major("k1", 512, xl, ("k1",))
                token_major("hi", 512, xl, ("hi",))
                pe.wait_ge(*at("rope_ready", 1))
                for i in range(NT):
                    s = take(("it", i))
                    settle(pe)
                    n = TS[i]
                    idn = ident[0:n, 0:n]
                    tr(s[:, 0:n], qtok[0:n, i, 768:896], idn)
                    tr(s[:, 128:128 + n], qtok[0:n, i, 896:1024], idn)
                    tr(s[:, 256:256 + n], ikdup[0:n, i, :, :].rearrange("p r d -> p (r d)"), idn).then_inc(sem["pe_done"], 1)
                    s = take(("at", i))
                    settle(pe)
                    for c in range(4):
                        tr(s[:, c * P:c * P + n], qtok[0:n, i, c * P:(c + 1) * P], idn)
                    for g in range(2):
                        last = tr(s[:, (4 + g) * P:(4 + g) * P + n], kdup[0:n, i, g, :, :].rearrange("p r d -> p (r d)"), idn)
                    last.then_inc(sem["pe_done"], 1)
                project("hf", "hf", 0, 4)
                project("hq", "hq", 0, 4)

                freed(("it", NT - 1))
                freed(("at", NT - 1))
                def index_scores(i, hd):
                    take(("ix", i, hd))
                    o = wide(("ix", i, hd))
                    r = 32 * (hd % 4)
                    for lo, hi in ((0, 80), (80, W[i])):
                        last = mm(o[0:TS[i], lo:hi], ixT[r:r + 32, hd // 4, T0[i]:T0[i] + TS[i]], ixT[r:r + 32, 2, lo:hi],
                                  start=True, stop=True, tile_position=(r, 0))
                    last.then_inc(sem["pe_done"], 1)

                def level(hd, l):
                    s = take(("lv", hd, l))
                    if l > 0:
                        pe.wait_ge(*at("qe_ready", hd * 7 + l))
                    u = (hd * 7 + l - 1) % 2
                    for j in range(NT):
                        k_, q_ = (hk[:, hd, j, :], hq[:, hd, j, :]) if l == 0 else (
                            ke[:, u, j * P:(j + 1) * P], qe[:, u, j * P:(j + 1) * P])
                        last = mm(s[:, j * P:(j + 1) * P], k_, q_, start=True, stop=True)
                    last.then_inc(sem["pe_done"], 1)

                for hd in range(IH):
                    index_scores(1, hd)
                freed(("hq", HH - 1))
                pe.wait_ge(*at("f_done", HH))
                for kind, m, n in mixed_jobs():
                    (level if kind == "lv" else index_scores)(m, n)
                for hd in range(IH):
                    index_scores(NT - 1, hd)
                pe.wait_ge(*at("qb_ready", HH))
                pe.wait_ge(*at("kw_ready", HH))
                freed(("lv", HH - 1, LEVELS - 1))
                def update(j):
                    n = TS[j]
                    s = take(("kt", j))
                    settle(pe)
                    for hd in range(HH):
                        last = tr(s[0:n, hd * P:(hd + 1) * P], hk[:, hd, j, 0:n], ident[:, :])
                    last.then_inc(sem["pe_done"], 1)
                    s = take(("su", j))
                    settle(pe)
                    freed(("kt", j))
                    for hd in range(HH):
                        last = mm(s[:, hd * P:(hd + 1) * P], kwT[0:n, j % 2, hd * P:(hd + 1) * P],
                                  vH[0:n, j, hd * P:(hd + 1) * P], start=True, stop=True)
                    last.then_inc(sem["pe_done"], 1)

                def output(j):
                    n = TS[j]
                    s = take(("ot", j))
                    if j > 0:
                        settle(pe)
                        freed(("su", j - 1))
                    for hd in range(HH):
                        o = s[:, hd * P:hd * P + n]
                        if j > 0:
                            mm(o, S[(j - 1) % 2][:, hd, :], hq[:, hd, j, 0:n], start=True, stop=False)
                        last = mm(o, vH[0:n, j, hd * P:(hd + 1) * P], AT[0:n, hd, j, 0:n], start=j == 0, stop=True)
                    last.then_inc(sem["pe_done"], 1)

                for j in range(NT - 1):
                    update(j)
                    if j > 0:
                        output(j - 1)
                output(NT - 2)
                output(NT - 1)
                project("hg", "hg", 0, 4)
                for hd in range(HH):
                    s = take(("on", hd))
                    pe.wait_ge(*at("sq_ready", hd + 1))
                    mm(s[:, 0:512], ones[:, :], osq[:, hd, 0:512], start=True, stop=True)
                    mm(s[:, 512:640], ones[:, :], osq[:, hd, 512:640], start=True, stop=True).then_inc(sem["pe_done"], 1)
                project("ga0", "ga", 0, 4)
                project("ga1", "ga", 4, 4)
                w = chunk("wa").rearrange("p (c n) -> p c n", c=4)
                pe.wait_ge(*at("ya_ready", 1))
                yflat = [hq[:, k, :, :].rearrange("p j t -> p (j t)") for k in range(HH)]
                for c in range(8):
                    feature_major(("wa", c), lambda k: w[:, k, c * P:(c + 1) * P],
                                  lambda k, lo, hi: yflat[k][:, 0:80] if lo == 0 else yflat[k][:, P:P + LT - 80], HH)

                def scores(i, g):
                    for hd in range(4 * g, 4 * g + 4):
                        take(("qk", i, hd))
                        if TS[i] <= 64:
                            settle(pe)
                        o = wide(("qk", i, hd))
                        r = 64 * (hd % 2)
                        for lo, hi in ((0, 80), (80, W[i])):
                            if lo < hi:
                                last = mm(o[0:TS[i], lo:hi], aqk[r:r + 64, hd // 2, T0[i]:T0[i] + TS[i]],
                                          aqk[r:r + 64, 4 + g, lo:hi], start=True, stop=True, tile_position=(r, 0))
                        last.then_inc(sem["pe_done"], 1)

                scores(0, 0)
                groups = [(i, g) for i in range(NT) for g in range(2)]
                kts = 0
                for n_, (i, g) in enumerate(groups):
                    if n_ + 1 < len(groups):
                        scores(*groups[n_ + 1])
                    n = TS[i]
                    pe.wait_ge(*at("pn_ready", 4 * n_ + 4))
                    for k in range(i + 1):
                        s = take(("pt", i, g, k))
                        settle(pe)
                        for r in range(4):
                            hd = 4 * g + (0, 2, 1, 3)[r]
                            last = tr(s[0:TS[k], r * n:(r + 1) * n], pb[0:n, hd, T0[k]:T0[k] + TS[k]], ident[0:n, 0:n])
                        last.then_inc(sem["pe_done"], 1)
                    s = take(("pv", i, g))
                    for k in range(i + 1):
                        freed(("pt", i, g, k))
                        settle(pe)
                        for par in range(2):
                            last = mm(s[64 * par:64 * par + 64, 0:2 * n], vA[0:TS[k], k, g * AD:(g + 1) * AD],
                                      ptq[0:TS[k], (kts + k) % 4, par * 2 * n:(par + 1) * 2 * n],
                                      start=k == 0, stop=k == i, tile_position=(0, 64 * par))
                        if k < i:
                            last.then_inc(sem["pt_used"], 1)
                    last.then_inc(sem["pe_done"], 1)
                    kts += i + 1
                project("gb0", "gb", 0, 4)
                project("gb1", "gb", 4, 4)
                pe.wait_ge(*at("yl_ready", 4))
                _, wh, wl = parts("wb")
                for c in range(8):
                    low_parts("wb", c // 2)
                    take(("wb", c))
                    settle(pe)
                    o = wide(("wb", c))
                    for lo, hi in ((0, LT // 2), (LT // 2, LT)):
                        for j in range(4):
                            for k, (w, y) in enumerate(((wh, yh), (wh, yl), (wl, yh))):
                                last = mm(o[:, lo:hi], w[:, j, c * P:(c + 1) * P], y[:, j, lo:hi],
                                          start=j == 0 and k == 0, stop=j == 3 and k == 2)
                    last.then_inc(sem["pe_done"], 1)
                for half in range(2):
                    pe.wait_ge(*at("ml_ready", 8))
                    token_major(f"wo{half}", 512, ml, ("wo", half))

                def router(i):
                    s = take(("ro", i))
                    settle(pe)
                    freed(("xt2", i))
                    w = gu_ring[:, CHUNKS.index("ro") % 2, 0:288].rearrange("p (c n) -> p c n", c=KC)
                    for c in range(KC):
                        last = mm(s[0:TS[i], 0:36], xnT[:, c, T0[i]:T0[i] + TS[i]], w[:, c, :], start=c == 0, stop=c == KC - 1)
                    last.then_inc(sem["pe_done"], 1)

                chunk("ro")
                norm_transposes("xt2", NT, router)
                router(NT - 2)
                router(NT - 1)
                s = take(("rank",))
                pe.wait_ge(*at("c_ready", 1))
                for m, lhs in enumerate((tri, ones)):
                    for k in range(NT):
                        last = mm(s[:, (m * NT + k) * NE:(m * NT + k + 1) * NE], lhs[0:TS[k], :], Cs[0:TS[k], k, :],
                                  start=True, stop=True)
                last.then_inc(sem["pe_done"], 1)
                s = take(("slot",))
                pe.wait_ge(*at("ab_ready", 1))
                for n in range(2 * NT):
                    last = mm(s[0:SLOTS, 0:NBLK], Am[0:TS[n % NT], n, :], Bm[0:TS[n % NT], n, :], start=n == 0, stop=n == 2 * NT - 1)
                last.then_inc(sem["pe_done"], 1)

                for s_ in range(4):
                    pe.wait_ge(*at(f"free{s_}", PER_SLAB[s_]))

                def transposes(e, u):
                    pe.wait_ge(*at(f"xg{u}", (e - u) * 8 + 16))
                    settle(pe)
                    for c in range(KC):
                        last = tr(slab(0)[:, u * 512 + c * SLOTS:u * 512 + (c + 1) * SLOTS], xg[0:SLOTS, u, c:D:KC], ident[0:SLOTS, 0:SLOTS])
                    last.then_inc(sem["t_done"], 1)

                def gate_or_up(e, u, m):
                    pe.wait_ge(*at(("wl_gate", "wl_up")[m], e + 1))
                    settle(pe)
                    parts = [w[:, m * 2048:(m + 1) * 2048].rearrange("p (c f) -> p c f", c=KC)
                             for w in (gu_high[u], gu_low[u])]
                    o = slab(1)[:, u * 512 + m * FF:u * 512 + (m + 1) * FF]
                    for c in range(KC):
                        for w in parts:
                            last = mm(o, xs[:, u, c, :, :].rearrange("p a s -> p (a s)"), w[:, c, :],
                                      start=c == 0 and w is parts[0], stop=c == KC - 1 and w is parts[1])
                    last.then_inc(sem[("wg_done", "g_done")[m]], 1)

                def gate_up(e, u):
                    pe.wait_ge(*at("xs_done", e + 1))
                    pe.wait_ge(*at("ge_done", e - 1))
                    gate_or_up(e, u, 0)
                    gate_or_up(e, u, 1)

                def fold_transposed(e, u):
                    pe.wait_ge(*at("ge_done", e + 1))
                    pe.wait_ge(*at("af_done", e - 1))
                    settle(pe)
                    for j in range(4):
                        last = mm(slab(3)[:, u * 512 + j * SLOTS:u * 512 + (j + 1) * SLOTS], guo[:, u, j * P:(j + 1) * P],
                                  fold, start=True, stop=True)
                    last.then_inc(sem["ft_done"], 1)

                def down(e, u):
                    pe.wait_ge(*at("am_done", e + 1))
                    pe.wait_ge(*at("wl_down", e + 1))
                    pe.wait_ge(*at("y_done", e))
                    settle(pe)
                    high, low = (w.rearrange("p (j n) -> p j n", j=2) for w in (dn_high[u], dn_low[u]))
                    for half in range(2):
                        cols = slice(half * 512, (half + 1) * 512)
                        for j in range(2):
                            for n, (part, w) in enumerate(((0, high), (0, low), (1, high))):
                                last = mm(slab(2)[0:SLOTS, cols], ams[:, u, j, part, :], w[:, j, cols],
                                          start=j == 0 and n == 0, stop=j == 1 and n == 2)
                    last.then_inc(sem["d_done"], 1)

                def expert(e, u, first=False, last=False):
                    gate_up(e, u)
                    if not last:
                        pe.wait_ge(*at("xs_done", e))
                        transposes(e + 1, 1 - u)
                    if not first:
                        down(e - 1, 1 - u)
                    fold_transposed(e, u)

                transposes(0, 0)
                expert(0, 0, first=True)
                expert(1, 1)
                with pe.Fori(1, NE // 2 - 1) as ep:
                    for u in range(2):
                        expert(ep * 2 + u, u)
                expert(NE - 2, 0)
                expert(NE - 1, 1, last=True)
                down(NE - 1, 1)

                pe.wait_ge(*at("base_ready", 1))
                settle(pe)
                n_over = pe.value_load(nov[0:1, 0:1], min_val=0, max_val=XBLK)
                with pe.If(n_over > 0):
                    with pe.Fori(0, XBLK) as x:
                        def ov(name, k=1):
                            return sem[name], (L * XBLK + x) * OV[name] + k * OV[name]

                        pe.wait_ge(*ov("ov_x"))
                        settle(pe)
                        for c in range(KC):
                            last = tr(slab(0)[:, c * SLOTS:(c + 1) * SLOTS], xg[0:SLOTS, 0, c:D:KC], ident[0:SLOTS, 0:SLOTS])
                        last.then_inc(sem["ov_t"], 1)
                        pe.wait_ge(*ov("ov_xt"))
                        pe.wait_ge(*ov("ov_w"))
                        w = ovw[:, 0:4096].rearrange("p (m c f) -> p m c f", m=2, c=KC)
                        for m in range(2):
                            for j in range(2):
                                o = slab(1)[:, (2 * m + j) * SLOTS:(2 * m + j + 1) * SLOTS]
                                for c in range(KC):
                                    last = mm(o, w[:, m, c, j * P:(j + 1) * P], xgT[:, c, :], start=c == 0, stop=c == KC - 1)
                        last.then_inc(sem["ov_g"], 1)
                        pe.wait_ge(*ov("ov_am"))
                        settle(pe)
                        w = ovw[:, 4096:6144].rearrange("p (j n) -> p j n", j=2)
                        for half in range(2):
                            for j in range(2):
                                last = mm(slab(2)[0:SLOTS, half * 512:(half + 1) * 512], am[:, j, :],
                                          w[:, j, half * 512:(half + 1) * 512], start=j == 0, stop=j == 1)
                        last.then_inc(sem["ov_d"], 1)
                with pe.Else():
                    for name in ("ov_t", "ov_g", "ov_d"):
                        pe.sem_inc(sem[name], XBLK)

        @block.vector
        def _(dve):
            V = nc.vector
            tt, ts, stt = V.tensor_tensor, V.tensor_scalar, V.scalar_tensor_tensor
            V.memset(r1[:, 0:2560], 0.0).then_inc(sem["init"], 1)
            V.memset(small[:, :], 1.0).then_inc(sem["init"], 1)
            V.memset(sc[:, :, :], 0.0).then_inc(sem["init"], 1)
            for name in START:
                dve.sem_inc(sem[name], START[name])
            dve.wait_ge(sem["const_load"], 48)
            V.tensor_copy(lvm[:, :, :].rearrange("p l t -> p (l t)"), dn_ring[:, 0, 0:LEVELS * P]).then_inc(sem["init"], 1)
            dve.wait_ge(sem["init"], INITS)
            V.tensor_copy(sc[:, 0, 4:4 + W[0]], mask0).then_inc(sem["init"], 1)
            V.memset(lb, 0.0).then_inc(sem["init"], 1)
            tt(lb1, lbl[:, 0, :], lbl[:, 1, :], ALU.subtract).then_inc(sem["init"], 1)
            dve.wait_ge(sem["lbe"], 1)
            V.tensor_scalar_add(lb1, lb1, 1.0).then_inc(sem["init"], 1)
            dve.wait_ge(sem["init"], INITS + 4)
            V.reciprocal(lb1, lb1).then_inc(sem["init"], 1)
            dve.wait_ge(sem["init"], INITS + 5)

            with dve.Fori(0, DEPTH) as L:
                n_ = [0]

                def at(name, k):
                    return sem[name], L * PER[name] + (START.get(name, 0) + k)

                def chained(ins):
                    n_[0] += 1
                    ins.then_inc(sem["dve"], 1)
                    return n_[0]

                def after(n):
                    dve.wait_ge(*at("dve", n))

                def link(ins):
                    after(chained(ins))

                def done(job):
                    dve.wait_ge(*at("pe_done", JOBS[job] + 1))

                def free(job):
                    return sem[f"free{JOBS[job] % 4}"], 1

                def freed(job):
                    dve.wait_ge(*at(f"free{JOBS[job] % 4}", JOBS[job] // 4 + 1))

                def norm_rows(k0, then=None):
                    dve.wait_ge(*at("rms_ready", 1 + (k0 > 0)))
                    dve.wait_ge(*at("g_load", 16 * (1 + (k0 > 0))))
                    link(V.reciprocal(rstd, rms))
                    for i in range(NT):
                        n = TS[i]
                        if i >= 2:
                            done(("xt2" if k0 else "xt", i - 2))
                            if k0:
                                dve.wait_ge(*at(f"xw{i % 2}", 16 * (i // 2)))
                        stt(xn[0:n, i % 2, :], h[0:n, i, :], rstd[0:n, i:i + 1], gB[0:n, :], ALU.mult, ALU.mult).then_inc(
                            sem["xn_ready"], 1)
                        if then and i >= 2:
                            then(i - 2)

                norm_rows(0)
                dve.wait_ge(*at("xn_ready", NT))
                dve.wait_ge(*at("h_out", 16 * NT))
                settle(dve)
                for i in range(NT):
                    dve.wait_ge(*at("xh_ready", i + 1))
                    cols = slice(T0[i], T0[i] + TS[i])
                    tt(xl[:, :, cols], job_slab(("xt", i)).rearrange("p (c t) -> p c t", c=KC)[:, :, 0:TS[i]],
                       xh[:, :, cols].bitcast(F32), ALU.subtract).then_inc(*free(("xt", i)))

                dve.wait_ge(*at("par_load", 48))
                link(ts(llb, lb, 1e-18, None, ALU.max))
                ts(omlb, lb, -1.0, 1.0, ALU.mult, ALU.add).then_inc(sem["lb_ready"], 1)
                link(ts(dec[:, :, 0], lb, 1e-18, NEG, ALU.is_lt, ALU.mult))
                dve.wait_ge(*at("lb_ln", 1))
                link(tt(llb, llb, dec[:, :, 0], ALU.add))

                ik = qtok[:, :, 1024:1056]
                freed(("k3t", 0))
                ikq = rt[:, 0:NT * ID].rearrange("p (i d) -> p i d", i=NT)
                link(tt(ikq, ik, ik, ALU.mult))
                V.tensor_reduce(kss, ikq, AX, ALU.add).then_inc(sem["ksq_ready"], 1)
                ts(iw, qtok[:, :, 1056:1064], IH ** -0.5 * ID ** -0.5, None, ALU.mult)
                dve.wait_ge(*at("ksq_ready", 1))

                def rope(x, heads, tab, half):
                    x1, x2 = x[:, :, :, 0:half], x[:, :, :, half:2 * half]
                    c, s = bc(tab[:, 0], 2, heads), bc(tab[:, 1], 2, heads)
                    n = NT * heads * half
                    t = [rt[:, k * n:(k + 1) * n].rearrange("p (i h d) -> p i h d", i=NT, h=heads) for k in range(4)]
                    tt(t[0], x1, c, ALU.mult)
                    tt(t[1], x2, s, ALU.mult)
                    tt(t[2], x2, c, ALU.mult)
                    link(tt(t[3], x1, s, ALU.mult))
                    tt(x1, t[0], t[1], ALU.subtract)
                    link(tt(x2, t[2], t[3], ALU.add))

                for i in range(1, NT):
                    freed(("k1", i))
                V.tensor_copy(vA[:, :, :], qtok[:, :, 640:768])
                rope(qtok[:, :, 0:640].rearrange("p i (h d) -> p i h d", d=AD), 10, rope_a, 8)
                for g in range(2):
                    V.tensor_copy(kdup[:, :, g, :, :], bc(qtok[:, :, 512 + g * AD:512 + (g + 1) * AD], 2, 2))
                dve.wait_ge(*at("kn_ready", 1))
                link(V.reciprocal(krms, krms))
                link(tt(ik, ik, bc(krms, 2, ID), ALU.mult))
                link(tt(ik, ik, bc(ik_g, 1, NT), ALU.mult))
                rope(qtok[:, :, 768:1056].rearrange("p i (h d) -> p i h d", d=ID), 9, rope_i, 4)
                V.tensor_copy(ikdup[:, :, :, :], bc(ik, 2, 4)).then_inc(sem["rope_ready"], 1)

                fb = pr[:, :].rearrange("p (k u t) -> p k u t", k=4, u=2)
                done(("at", NT - 1))
                pads = r1[:, :].rearrange("p (a j t) -> p a j t", a=3 * HH, j=NT)
                V.memset(pads[:, :, 0, TS[0]:], 0.0)
                link(V.memset(pads[:, :, NT - 1, TS[NT - 1]:], 0.0))

                def gate_in(j):
                    done(("hf", j))
                    z = wide(("hf", j))
                    ts(fb[:, 0, j % 2, :], z, -1.0, 40.0, ALU.mult, ALU.min).then_inc(sem["e_ready"], 1)
                    ts(fb[:, 1, j % 2, :], z, -1.0, 40.0, ALU.mult, ALU.max).then_inc(*free(("hf", j)))

                def padded(dst, j):
                    flat = dst[:, j, :, :].rearrange("p j t -> p (j t)")
                    return (flat[:, 0:80], slice(0, 80)), (flat[:, P:P + LT - 80], slice(80, LT))

                def gate_out(j):
                    e, ov, l1, l2 = (fb[:, k, j % 2, :] for k in range(4))
                    dve.wait_ge(*at("lnf_ready", j + 1))
                    link(tt(l2, l2, l1, ALU.subtract))
                    n1 = chained(stt(l2, l2, 40.0, ov, ALU.add, ALU.subtract))
                    n2 = chained(V.tensor_scalar_add(l1, e, 1.0))
                    after(n2)
                    n2 = chained(V.reciprocal(l1, l1))
                    for dst, cols in padded(hb, j):
                        ts(dst, l2[:, cols], llb[:, j:j + 1], None, ALU.max)
                    after(n2)
                    for dst, cols in padded(hk, j):
                        last = stt(dst, e[:, cols], omlb[:, j:j + 1], l1[:, cols], ALU.mult, ALU.mult)
                    link(last)
                    flat = hb[:, j, :, :].rearrange("p j t -> p (j t)")
                    V.tensor_tensor_scan(flat, reset, flat, 0.0, ALU.mult, ALU.add).then_inc(sem["f_done"], 1)

                gate_in(0)
                for j in range(HH):
                    if j + 1 < HH:
                        gate_in(j + 1)
                    gate_out(j)

                def index_score(i, hd):
                    n = TS[i]
                    if hd == 0:
                        V.memset(sc[0:n, i, 0:4], SENT)
                    m = (i - 1) * IH + hd
                    freed(("ix", i, hd))
                    if hd > 0:
                        dve.wait_ge(*at("rel_used", m))
                    acc, r_, w_ = sc[0:n, i, 4:4 + W[i]], rel[0:n, m % 2, 0:W[i]], iw[0:n, i, hd:hd + 1]
                    (ts(acc, r_, w_, None, ALU.mult) if hd == 0 else stt(acc, r_, w_, acc, ALU.mult, ALU.add)).then_inc(
                        sem["rel_used"], 1)
                    if hd == IH - 1 and i < NT - 1:
                        dve.wait_ge(*at("rel_used", i * IH))
                        V.memset(sc[0:64, i, 4 + W[i] - 64:4 + W[i]], HIDDEN)

                def differences(m):
                    hd, l = m // 7, m % 7 + 1
                    half = 2 ** (l - 1)
                    if m >= 2:
                        dve.wait_ge(*at("qe_ready", m - 1))
                    b = hb[:, hd, :, :].rearrange("p j t -> p (j t)").rearrange("p (n a t) -> p n a t", a=2, t=half)
                    e = ebuf[:, m % 2, :].rearrange("p (n a t) -> p n a t", a=2, t=half)
                    mid = b[:, :, 0, half - 1:half].broadcast_to([P, 640 // (2 * half), half])
                    tt(e[:, :, 1, :], b[:, :, 1, :], mid, ALU.subtract)
                    tt(e[:, :, 0, :], mid, b[:, :, 0, :], ALU.subtract).then_inc(sem["d_ready"], 1)

                def take_level(hd, l):
                    done(("lv", hd, l))
                    if l > 0:
                        freed(("lv", hd, l - 1))
                    settle(dve)
                    V.copy_predicated(AT[:, hd, :, :], bc(lvm[:, l, :], 1, NT),
                                      job_slab(("lv", hd, l))[:, 0:640].rearrange("p (j t) -> p j t", j=NT)).then_inc(
                                          *free(("lv", hd, l)))

                dve.wait_ge(*at("f_done", HH))
                dve.wait_ge(sem["y_init"], 16 * XBLK * SLOTS // (2 * P))
                differences(0)
                differences(1)
                for hd in range(IH):
                    index_score(1, hd)
                for kind, a_, b_ in mixed_jobs():
                    if kind == "ix":
                        index_score(a_, b_)
                        continue
                    m = a_ * 7 + b_ - 1
                    if b_ > 0 and m + 2 < HH * 7:
                        differences(m + 2)
                    take_level(a_, b_)

                for hd in range(HH):
                    if hd >= 2:
                        dve.wait_ge(*at("kw_ready", hd - 1))
                    else:
                        dve.wait_ge(*at("qe_ready", 27 + hd))
                    b = hb[:, hd, :, :]
                    tt(ebuf[:, hd % 2, :].rearrange("p (j t) -> p j t", j=NT), b[:, :, P - 1:P].broadcast_to([P, NT, P]), b,
                       ALU.subtract).then_inc(sem["d_ready"], 1)
                    dve.wait_ge(*at("ex_ready", 28 + 2 * hd + 1))
                    q_ = hq[:, hd, :, :].rearrange("p j t -> p (j t)")
                    k_ = hk[:, hd, :, :].rearrange("p j t -> p (j t)")
                    tt(q_, q_, qe[:, hd % 2, :], ALU.mult).then_inc(sem["qb_ready"], 1)
                    dve.wait_ge(*at("ex_ready", 28 + 2 * hd + 2))
                    tt(k_, k_, ebuf[:, hd % 2, :], ALU.mult).then_inc(sem["kw_ready"], 1)
                    for n in range(2):
                        index_score(NT - 1, 2 * hd + n)

                dve.wait_ge(*at("ex_ready", 37))
                for j in range(NT - 1):
                    done(("ot", j - 1) if j > 1 else ("su", j))
                    s = job_slab(("su", j))
                    if j == 0:
                        V.tensor_copy(S0[:, :, :].rearrange("p h e -> p (h e)"), s[:, 0:512]).then_inc(*free(("su", j)))
                    else:
                        freed(("su", j - 1))
                        for hd in range(HH):
                            last = stt(S[j % 2][:, hd, :], S[(j - 1) % 2][:, hd, :], dec[:, hd, j:j + 1], s[:, hd * P:(hd + 1) * P], ALU.mult, ALU.add)
                        last.then_inc(*free(("su", j)))

                def hgrn_output():
                    for hd in range(HH):
                        freed(("on", hd))
                        q_, k_, b_ = (r[:, hd, :, :].rearrange("p j t -> p (j t)") for r in (hq, hk, hb))
                        link(V.reciprocal(b_, b_))
                        link(stt(q_, q_, hn_g[:, hd:hd + 1], b_, ALU.mult, ALU.mult))
                        last = tt(q_, q_, k_, ALU.mult)
                        if hd == HH - 1:
                            last.then_inc(sem["ya_ready"], 1)

                def gated(c):
                    freed(("ga", c))
                    done(("wa", c))
                    tt(sga[:, c, :], wide(("wa", c)), sga[:, c, :], ALU.mult).then_inc(*free(("wa", c)))

                prev, rounds = {}, (TOPK + 4) // 8
                for r in range(rounds):
                    if r == 7:
                        hgrn_output()
                    if r == rounds - 1:
                        for c in range(2):
                            gated(c)
                    cur = {}
                    for i in range(1, NT):
                        if r:
                            after(prev[i])
                            settle(dve)
                        cur[i] = chained(V.max(top8[0:TS[i], i - 1, :], sc[0:TS[i], i, 0:4 + W[i]]))
                    for i in range(1, NT):
                        after(cur[i])
                        settle(dve)
                        s_ = sc[0:TS[i], i, 0:4 + W[i]]
                        prev[i] = chained(V.match_replace(s_, top8[0:TS[i], i - 1, :], s_, REPL))
                for i in range(1, NT):
                    after(prev[i])
                    s_ = sc[0:TS[i], i, 4:4 + W[i]]
                    prev[i] = chained(ts(s_, s_, 0.5 * (REPL + HIDDEN), NEG, ALU.is_gt, ALU.mult))
                after(prev[NT - 1])

                for c in range(2, 8):
                    gated(c)
                for c in range(4, 8):
                    freed(("wa", c))
                settle(dve)

                def score_max(m):
                    i, hd = m // 8, m % 8
                    n = TS[i]
                    done(("qk", i, hd))
                    settle(dve)
                    V.tensor_tensor_reduce(out=pb[0:n, hd, 0:W[i]], in0=wide(("qk", i, hd))[0:n, 0:W[i]], in1=sc[0:n, i, 4:4 + W[i]],
                                           scale=1.0, scalar=SCALAR_MIN, op0=ALU.add, op1=ALU.max,
                                           accum_out=mx[0:n, hd:hd + 1]).then_inc(*free(("qk", i, hd)))
                    freed(("qk", i, hd))
                    ts(nmx[0:n, hd:hd + 1], mx[0:n, hd:hd + 1], -AD ** -0.5, None, ALU.mult).then_inc(sem["mx_ready"], 1)

                def normalise(m):
                    i, hd = m // 8, m % 8
                    n = TS[i]
                    dve.wait_ge(*at("p_ready", m + 1))
                    link(V.reciprocal(pinv[0:n, hd:hd + 1], psum_[0:n, hd:hd + 1]))
                    ts(pb[0:n, hd, 0:W[i]], pb[0:n, hd, 0:W[i]], pinv[0:n, hd:hd + 1], None, ALU.mult).then_inc(sem["pn_ready"], 1)

                score_max(0)
                score_max(1)
                for m in range(40):
                    if m + 2 < 40:
                        score_max(m + 2)
                    normalise(m)

                def merged_low(c):
                    dve.wait_ge(*at("mh_ready", c + 1))
                    tt(ml[:, c, :], sga[:, c, :], xh[:, c, :].bitcast(F32), ALU.subtract).then_inc(sem["ml_ready"], 1)

                for c in range(8):
                    freed(("gb", c))
                    done(("wb", c))
                    tt(sgb[:, c, :], wide(("wb", c)), sgb[:, c, :], ALU.mult).then_inc(*free(("wb", c)))
                    freed(("wb", c))
                    tt(sga[:, c, :], sga[:, c, :], sgb[:, c, :], ALU.add).then_inc(sem["mg_ready"], 1)
                    if c > 0:
                        merged_low(c - 1)
                merged_low(7)
                dve.wait_ge(*at("h_in", 16 * NT))
                settle(dve)
                for half in range(2):
                    for i in range(NT):
                        n = TS[i]
                        done(("wo", half, i))
                        o = h[0:n, i, half * 512:(half + 1) * 512]
                        tt(o, job_slab(("wo", half, i))[0:n, 0:512], o, ALU.add).then_inc(*free(("wo", half, i)))

                def logits(i):
                    done(("ro", i))
                    tt(lg[0:TS[i], i, :], job_slab(("ro", i))[0:TS[i], 0:36], rb[0:TS[i], :], ALU.add).then_inc(*free(("ro", i)))

                norm_rows(NT, logits)
                logits(NT - 2)
                logits(NT - 1)
                for i in range(NT):
                    freed(("ro", i))

                lgg, lge = lg[:, :, 0:NG], lg[:, :, NG:].rearrange("p i (g e) -> p i g e", g=NG)
                link(V.tensor_reduce(gmax, lgg, AX, ALU.max))
                tt(ge, lgg, bc(gmax, 2, NG), ALU.subtract).then_inc(sem["rt_ready"], 1)

                def first_of(x, mval, oh_, desc, nn, tmp):
                    link(tt(tmp, x, bc(mval, 2, nn), ALU.is_equal))
                    link(tt(tmp, tmp, bc(desc, 1, NT), ALU.mult))
                    link(V.tensor_reduce(vmx, tmp, AX, ALU.max))
                    link(tt(oh_, tmp, bc(vmx, 2, nn), ALU.is_equal))

                first_of(lgg, gmax, goh, descg, NG, goh)
                link(tt(lm, lge, bc(goh, 3, EPG), ALU.mult))
                link(V.tensor_reduce(ls, lm.rearrange("p i g e -> p i e g"), AX, ALU.add))
                link(V.tensor_reduce(m12[:, 0], ls, AX, ALU.max))
                first_of(ls, m12[:, 0], oh[:, 0], desce, EPG, eq)
                link(stt(ls2, oh[:, 0], NEG, ls, ALU.mult, ALU.add))
                link(V.tensor_reduce(m12[:, 1], ls2, AX, ALU.max))
                tt(dd, m12[:, 1], m12[:, 0], ALU.subtract).then_inc(sem["rt_ready"], 1)
                first_of(ls2, m12[:, 1], oh[:, 1], desce, EPG, eq)
                for c in range(2):
                    for g in range(NG):
                        last = tt(CC[:, c].rearrange("p i (g e) -> p i g e", g=NG)[:, :, g, :], bc(goh[:, :, g], 2, EPG), oh[:, c], ALU.mult)
                link(last)
                tt(Cs, CC[:, 0], CC[:, 1], ALU.add).then_inc(sem["c_ready"], 1)
                dve.wait_ge(*at("rt_exp", 2))
                link(V.tensor_reduce(gs, ge, AX, ALU.add))
                link(stt(gs, ed, 1.0, gs, ALU.add, ALU.mult))
                link(V.reciprocal(wcomb[:, 0], gs))
                link(tt(wcomb[:, 1], wcomb[:, 0], ed, ALU.mult))
                link(tt(tmpC, CC, bc(bc(ioe, 1, NT), 1, 2), ALU.mult))
                link(V.tensor_reduce(esel, tmpC, AX, ALU.add))
                done(("rank",))
                s_ = job_slab(("rank",))
                V.tensor_copy(rk[:, 0, :], s_[:, 0:NE])
                link(V.tensor_copy(rk[:, 1:, :].rearrange("p i n -> p (i n)"), s_[:, NT * NE:2 * NT * NE]))
                for i in range(2, NT + 1):
                    link(tt(rk[:, i, :], rk[:, i, :], rk[:, i - 1, :], ALU.add))
                tt(rk[:, 1:NT, :].rearrange("p i n -> p (i n)"), rk[:, 1:NT, :].rearrange("p i n -> p (i n)"), s_[:, NE:NT * NE],
                   ALU.add).then_inc(*free(("rank",)))
                freed(("rank",))
                for c in range(2):
                    last = tt(tmpC[:, c], CC[:, c], rk[:, 0:NT, :], ALU.mult)
                link(last)
                link(V.tensor_reduce(rsel, tmpC, AX, ALU.add))
                link(tt(nxk, bc(rk[:, NT, :], 2, KMAX), bc(kthr, 1, NE), ALU.is_gt))
                link(V.tensor_reduce(nx, nxk, AX, ALU.add))
                link(V.tensor_tensor_scan(inc, ones[:, 0:NE], nx, 0.0, ALU.mult, ALU.add))
                link(tt(off, inc, nx, ALU.subtract))
                link(tt(tmpC, CC, bc(bc(off, 1, NT), 1, 2), ALU.mult))
                link(V.tensor_reduce(osel, tmpC, AX, ALU.add))
                r_, e_, o_ = (x.rearrange("p a i -> p (a i)") for x in (rsel, esel, osel))
                link(tt(qk_, bc(r_, 2, KMAX), bc(kthr, 1, 2 * NT), ALU.is_ge))
                link(V.tensor_reduce(qq, qk_, AX, ALU.add))
                link(stt(pos, qq, -float(SLOTS), r_, ALU.mult, ALU.add))
                link(ts(isov, qq, 1.0, None, ALU.min))
                link(tt(blk, o_, qq, ALU.add))
                link(stt(blk, blk, float(NE - 1), e_, ALU.add, ALU.subtract))
                link(tt(blk, blk, isov, ALU.mult))
                link(tt(blk, blk, e_, ALU.add))
                tt(Am, bc(io64, 1, 2 * NT), bc(pos, 2, SLOTS), ALU.is_equal)
                link(tt(Bm, bc(ioblk, 1, 2 * NT), bc(blk, 2, NBLK), ALU.is_equal))
                bm4 = Bm.rearrange("p (c i) n -> p c i n", c=2)
                tt(bm4[:, 0], bm4[:, 0], bc(tokid, 2, NBLK), ALU.mult)
                tt(bm4[:, 1], bm4[:, 1], bc(tokid, 2, NBLK), ALU.mult).then_inc(sem["ab_ready"], 1)
                link(stt(slotf, blk, float(SLOTS), pos, ALU.mult, ALU.add))
                V.tensor_copy(sidx[:, :], slotf).then_inc(sem["sidx_ready"], 1)
                link(tt(xcm, bc(inc, 1, XBLK), bc(ioblk[:, 0:XBLK], 2, NE), ALU.is_le))
                link(V.tensor_reduce(xef, xcm, AX, ALU.add))
                link(ts(xei[0:1, :], xef[0:1, :], float(NE - 1), None, ALU.min))
                V.tensor_copy(nov[0:1, 0:1], inc[0:1, NE - 1:NE]).then_inc(sem["base_ready"], 1)
                done(("slot",))
                V.tensor_copy(idx[:, :], job_slab(("slot",))[0:SLOTS, 0:NBLK]).then_inc(*free(("slot",)))
                V.tensor_copy(lb, lb1)

                def weight_low(e, u, part):
                    n = ("gate", "up", "down").index(part)
                    dve.wait_ge(*at(("wh_gate", "wh_up", "wh_down")[n], e + 1))
                    w, high, low = ((dn_ring[:, u, :], dn_high[u], dn_low[u]) if n == 2 else
                                    (x[:, n * 2048:(n + 1) * 2048] for x in (gu_ring[:, u, :], gu_high[u], gu_low[u])))
                    tt(low, w, high.bitcast(F32), ALU.subtract).then_inc(sem["wl_" + part], 1)

                def rows_low(e, u):
                    dve.wait_ge(*at("xs_hi", e + 1))
                    tt(xs[:, u, :, 1, :], slab(0)[:, u * 512:(u + 1) * 512].rearrange("p (c s) -> p c s", c=KC),
                       xs[:, u, :, 0, :].bitcast(F32), ALU.subtract).then_inc(sem["xs_done"], 1)

                def product(e, u):
                    dve.wait_ge(*at("si_done", e + 1))
                    tt(amf[:, u, :], slab(3)[:, u * 512 + 128:u * 512 + 256], sg[:, u, :], ALU.mult).then_inc(sem["af_done"], 1)
                    dve.wait_ge(*at("af_done", e + 1))
                    dve.wait_ge(*at("d_done", e - 1))
                    x = amf[:, u, :].rearrange("p (j s) -> p j s", j=2)
                    V.tensor_copy(ams[:, u, :, 0, :], x).then_inc(sem["ah_done"], 1)
                    dve.wait_ge(*at("ah_done", e + 1))
                    tt(ams[:, u, :, 1, :], x, ams[:, u, :, 0, :].bitcast(F32), ALU.subtract).then_inc(sem["am_done"], 1)

                def expert(e, u, last=False):
                    if not last:
                        weight_low(e + 1, 1 - u, "gate")
                        weight_low(e + 1, 1 - u, "up")
                        rows_low(e + 1, 1 - u)
                    product(e, u)
                    weight_low(e, u, "down")

                for part in ("gate", "up"):
                    weight_low(0, 0, part)
                rows_low(0, 0)
                with dve.Fori(0, NE // 2 - 1) as ep:
                    for u in range(2):
                        expert(ep * 2 + u, u)
                expert(NE - 2, 0)
                expert(NE - 1, 1, last=True)
                dve.wait_ge(*at("base_ready", 1))
                settle(dve)
                n_over = dve.value_load(nov[0:1, 0:1], min_val=0, max_val=XBLK)
                with dve.If(n_over > 0):
                    with dve.Fori(0, XBLK) as x:
                        dve.wait_ge(sem["ov_si"], L * XBLK + x + 1)
                        tt(am.rearrange("p j s -> p (j s)"), slab(1)[:, 128:256], sg[:, 0, :], ALU.mult).then_inc(sem["ov_am"], 1)
                with dve.Else():
                    dve.sem_inc(sem["ov_am"], XBLK)

                for k in range(2 * NT):
                    i, c = k // 2, k % 2
                    n = TS[i]
                    dve.wait_ge(*at(f"yg{k % 4}", 16 * (k // 4 + 1)))
                    if c:
                        dve.wait_ge(*at("cb_done", k))
                    stt(h[0:n, i, :], yg[0:n, k % 4, :], wcomb[0:n, c, i:i + 1], h[0:n, i, :], ALU.mult, ALU.add).then_inc(
                        sem["cb_done"], 1)
                assert n_[0] == PER["dve"], n_[0]

            dve.wait_ge(sem["fin_rms"], 1)
            dve.wait_ge(sem["fin_g"], 16)
            V.reciprocal(rstd, rms).then_inc(sem["fin_rms"], 1)
            dve.wait_ge(sem["fin_rms"], 2)
            for i in range(NT):
                n = TS[i]
                stt(h[0:n, i, :], h[0:n, i, :], rstd[0:n, i:i + 1], gB[0:n, :], ALU.mult, ALU.mult).then_inc(sem["fin_y"], 1)

        @block.scalar
        def _(act):
            A = nc.scalar.activation
            act.wait_ge(sem["init"], INITS + 3)
            A(lb1, lb1, ACT.Exp).then_inc(sem["lbe"], 1)
            act.wait_ge(sem["x_load"], 16 * len(xslices))

            with act.Fori(0, DEPTH) as L:
                n_ = [0]

                def at(name, k):
                    return sem[name], L * PER[name] + (START.get(name, 0) + k)

                def link(ins):
                    n_[0] += 1
                    ins.then_inc(sem["act"], 1)
                    act.wait_ge(*at("act", n_[0]))

                def done(job):
                    act.wait_ge(*at("pe_done", JOBS[job] + 1))

                def free(job):
                    return sem[f"free{JOBS[job] % 4}"], 1

                def freed(job):
                    act.wait_ge(*at(f"free{JOBS[job] % 4}", JOBS[job] // 4 + 1))

                def row_rms(weight):
                    act.dma_start(gB, a[weight][bass.ds(L, 1), :].broadcast_to([P, D])).then_inc(sem["g_load"], 16)
                    for i in range(NT):
                        if weight == "ffn_norm_g":
                            freed(("wo", 0, i))
                            freed(("wo", 1, i))
                        else:
                            act.wait_ge(*at("cb_done", 2 * (i + 1) - 2 * NT))
                        n = TS[i]
                        link(A(pr[0:n, 2048:3072], h[0:n, i, :], ACT.Square, accum_out=ss[0:n, i:i + 1]))
                    A(rms, ss, ACT.Sqrt, scale=1.0 / D, bias=eps_t).then_inc(sem["rms_ready"], 1)

                def padded(dst, j):
                    flat = dst[:, j, :, :].rearrange("p j t -> p (j t)")
                    return (flat[:, 0:80], slice(0, 80)), (flat[:, P:P + LT - 80], slice(80, LT))

                def high_part(name, q):
                    n = CHUNKS.index(name)
                    act.wait_ge(*at(f"gu{n % 2}", 16 * (n // 2 + 1)))
                    if (name, q) in HIGH_AFTER:
                        done(HIGH_AFTER[name, q])
                    settle(act)
                    w, high, _ = parts(name)
                    cols = quarter(name, q)
                    A(high[:, :, cols], w[:, :, cols], ACT.Copy).then_inc(sem["part_high"], 1)

                act.wait_ge(*at("d_done", 0))
                act.dma_start(ik_g, a["idx_k_norm_g"][bass.ds(L, 1), :].broadcast_to([P, ID])).then_inc(sem["par_load"], 16)
                act.dma_start(rb, a["router_b"][bass.ds(L, 1), :].broadcast_to([P, 36])).then_inc(sem["par_load"], 16)
                act.dma_start(hn_g, a["hgrn_norm_g"][bass.ds(L * P, P), :]).then_inc(sem["par_load"], 16)
                for name, q in (("k3", 0), ("k2", 0), ("k2", 1), ("k2", 2), ("k2", 3)):
                    high_part(name, q)
                row_rms("mix_norm_g")
                for i in range(NT):
                    done(("xt", i))
                    A(xh[:, :, T0[i]:T0[i] + TS[i]], job_slab(("xt", i)).rearrange("p (c t) -> p c t", c=KC)[:, :, 0:TS[i]],
                      ACT.Copy).then_inc(sem["xh_ready"], 1)
                act.wait_ge(*at("lb_ready", 1))
                A(llb, llb, ACT.Ln).then_inc(sem["lb_ln"], 1)
                for name, c0, n in (("k3", 1024, 40), ("k2", 512, 512), ("k1", 0, 512), ("hi", None, 512)):
                    if name == "hi":
                        act.wait_ge(*at("ksq_ready", 1))
                        A(krms, kss, ACT.Sqrt, scale=1.0 / ID, bias=eps_t).then_inc(sem["kn_ready"], 1)
                    if name == "k3":
                        done(("k3", 0))
                        A(k3f[0:40, :], wide(("k3", 0))[0:40, :], ACT.Copy).then_inc(*free(("k3", 0)))
                        act.wait_ge(*at("r1_clear", 1))
                    for i in range(NT if name != "k3" else 0):
                        done((name, i))
                        dst = vH[0:TS[i], i, :] if name == "hi" else qtok[0:TS[i], i, c0:c0 + n]
                        A(dst, job_slab((name, i))[0:TS[i], 0:n], ACT.Copy).then_inc(*free((name, i)))
                    if name == "k2":
                        done(("k3t", 0))
                        for i in range(NT):
                            last = A(qtok[0:TS[i], i, 1024:1064], job_slab(("k3t", 0))[0:TS[i], i * 40:(i + 1) * 40], ACT.Copy)
                        last.then_inc(*free(("k3t", 0)))
                    if name != "k1":
                        for q in range(4):
                            high_part({"k3": "k1", "k2": "hi", "hi": "hf"}[name], q)
                for i in range(NT):
                    done(("it", i))
                    A(ixT[:, :, T0[i]:T0[i] + TS[i]], job_slab(("it", i))[:, 0:384].rearrange("p (c t) -> p c t", c=3)[:, :, 0:TS[i]],
                      ACT.Copy).then_inc(*free(("it", i)))
                    done(("at", i))
                    A(aqk[:, :, T0[i]:T0[i] + TS[i]], job_slab(("at", i))[:, 0:768].rearrange("p (c t) -> p c t", c=6)[:, :, 0:TS[i]],
                      ACT.Copy).then_inc(*free(("at", i)))
                fb = pr[:, :].rearrange("p (k u t) -> p k u t", k=4, u=2)
                for j in range(HH):
                    e, l1, l2 = fb[:, 0, j % 2, :], fb[:, 2, j % 2, :], fb[:, 3, j % 2, :]
                    act.wait_ge(*at("e_ready", j + 1))
                    link(A(e, e, ACT.Exp))
                    A(l1, e, ACT.Ln, bias=one_t)
                    A(l2, e, ACT.Ln, bias=one_t, scale=lb[:, j:j + 1]).then_inc(sem["lnf_ready"], 1)
                    high_part("hq", j)
                for j in range(HH):
                    done(("hq", j))
                    o = wide(("hq", j))
                    (d0, c0), (d1, c1) = padded(hq, j)
                    A(d0, o[:, c0], ACT.Copy)
                    A(d1, o[:, c1], ACT.Copy).then_inc(*free(("hq", j)))
                def relu(i, hd):
                    m = (i - 1) * IH + hd
                    done(("ix", i, hd))
                    if m >= 2:
                        act.wait_ge(*at("rel_used", m - 1))
                    A(rel[0:TS[i], m % 2, 0:W[i]], wide(("ix", i, hd))[0:TS[i], 0:W[i]], ACT.Relu).then_inc(*free(("ix", i, hd)))

                def level_exp(m):
                    act.wait_ge(*at("d_ready", m + 1))
                    A(ebuf[:, m % 2, :], ebuf[:, m % 2, :], ACT.Exp).then_inc(sem["ex_ready"], 1)

                for hd in range(IH):
                    relu(1, hd)
                level_exp(0)
                level_exp(1)
                for kind, a_, b_ in mixed_jobs():
                    m = a_ * 7 + b_ - 1
                    if kind == "ix":
                        relu(a_, b_)
                    elif b_ == 0:
                        high_part("hg", a_)
                    elif m + 2 < HH * 7:
                        level_exp(m + 2)
                for hd in range(HH):
                    done(("lv", HH - 1, LEVELS - 1))
                    if hd >= 2:
                        act.wait_ge(*at("qb_ready", hd - 1))
                    A(qe[:, hd % 2, :], hb[:, hd, :, :].rearrange("p j t -> p (j t)"), ACT.Exp).then_inc(sem["ex_ready"], 1)
                    act.wait_ge(*at("d_ready", 28 + hd + 1))
                    A(ebuf[:, hd % 2, :], ebuf[:, hd % 2, :], ACT.Exp).then_inc(sem["ex_ready"], 1)
                    for n in range(2):
                        relu(NT - 1, 2 * hd + n)
                A(dec, hb[:, :, :, P - 1], ACT.Exp).then_inc(sem["ex_ready"], 1)
                def state_rows(j):
                    n = TS[j]
                    done(("kt", j))
                    A(kwT[0:n, j % 2, :], job_slab(("kt", j))[0:n, 0:512], ACT.Copy).then_inc(*free(("kt", j)))

                state_rows(0)
                for j in range(NT):
                    if j + 1 < NT - 1:
                        state_rows(j + 1)
                    n = TS[j]
                    done(("ot", j))
                    A(hq[:, :, j, 0:n], job_slab(("ot", j))[:, 0:512].rearrange("p (h t) -> p h t", h=HH)[:, :, 0:n], ACT.Copy).then_inc(
                        *free(("ot", j)))
                for j in range(HH):
                    done(("hg", j))
                    o = wide(("hg", j))
                    (d0, c0), (d1, c1) = padded(hk, j)
                    A(d0, o[:, c0], ACT.Silu)
                    A(d1, o[:, c1], ACT.Silu).then_inc(*free(("hg", j)))
                    high_part("ga0", j)
                for hd in range(HH):
                    done(("on", hd))
                    A(hb[:, hd, :, :].rearrange("p j t -> p (j t)"), job_slab(("on", hd))[:, 0:640], ACT.Sqrt, scale=1.0 / HD, bias=eps_t).then_inc(
                        *free(("on", hd)))
                act.wait_ge(*at("ya_ready", 1))
                for c in range(8):
                    done(("ga", c))
                    A(sga[:, c, :], wide(("ga", c)), ACT.Sigmoid).then_inc(*free(("ga", c)))
                    if c < 4:
                        high_part("ga1", c)

                def softmax_exp(m):
                    i, hd = m // 8, m % 8
                    n = TS[i]
                    act.wait_ge(*at("mx_ready", m + 1))
                    A(pb[0:n, hd, 0:W[i]], pb[0:n, hd, 0:W[i]], ACT.Exp, bias=nmx[0:n, hd:hd + 1], scale=AD ** -0.5,
                      accum_out=psum_[0:n, hd:hd + 1]).then_inc(sem["p_ready"], 1)

                for m in range(4):
                    softmax_exp(m)
                for n0 in range(2 * NT):
                    i, g = n0 // 2, n0 % 2
                    n = TS[i]
                    if n0 + 1 < 2 * NT:
                        for m in range(4 * n0 + 4, 4 * n0 + 8):
                            softmax_exp(m)
                    for k in range(i + 1):
                        m = PTS.index((i, g, k))
                        done(("pt", i, g, k))
                        if m >= 4:
                            b = PTS[m - 4]
                            if b[2] < b[0]:
                                act.wait_ge(*at("pt_used", PT_COUNT[b]))
                            else:
                                done(("pv", b[0], b[1]))
                        A(ptq[0:TS[k], m % 4, 0:4 * n], job_slab(("pt", i, g, k))[0:TS[k], 0:4 * n], ACT.Copy).then_inc(*free(("pt", i, g, k)))
                    if 2 <= n0 < 6:
                        high_part("gb0", n0 - 2)
                    done(("pv", i, g))
                    A(ybT[:, 2 * g:2 * g + 2, T0[i]:T0[i] + n], job_slab(("pv", i, g))[:, 0:2 * n].rearrange("p (c t) -> p c t", c=2),
                      ACT.Copy).then_inc(*free(("pv", i, g)))
                for c in range(8):
                    done(("gb", c))
                    A(sgb[:, c, :], wide(("gb", c)), ACT.Sigmoid).then_inc(*free(("gb", c)))
                    if c < 4:
                        high_part("gb1", c)
                    else:
                        if c == 4:
                            freed(("pv", NT - 1, 1))
                            settle(act)
                        A(yh[:, c - 4, :], ybT[:, c - 4, :], ACT.Copy).then_inc(sem["yh_ready"], 1)
                        high_part("wb", c - 4)
                for q in range(4):
                    high_part("wo0", q)
                for c in range(8):
                    act.wait_ge(*at("mg_ready", c + 1))
                    A(xh[:, c, :], sga[:, c, :], ACT.Copy).then_inc(sem["mh_ready"], 1)
                for q in range(4):
                    high_part("wo1", q)
                row_rms("ffn_norm_g")
                for i in range(NT):
                    act.wait_ge(*at("xn_ready", NT + i + 1))
                    act.dma_start(xrow[T0[i]:T0[i] + TS[i], :], xn[0:TS[i], i % 2, :]).then_inc(sem[f"xw{i % 2}"], 16)
                    done(("xt2", i))
                    A(xnT[:, :, T0[i]:T0[i] + TS[i]], job_slab(("xt2", i)).rearrange("p (c t) -> p c t", c=KC)[:, :, 0:TS[i]],
                      ACT.Copy).then_inc(*free(("xt2", i)))
                act.wait_ge(*at("rt_ready", 1))
                A(ge, ge, ACT.Exp).then_inc(sem["rt_exp"], 1)
                act.wait_ge(*at("rt_ready", 2))
                A(ed, dd, ACT.Exp).then_inc(sem["rt_exp"], 1)

                def weight_high(e, u, part):
                    if part == "gate":
                        act.wait_ge(*at(f"gu{u}", 16 * len(CHUNKS) // 2 + (e - u) * 8 + 16))
                        act.wait_ge(*at("wg_done", e - 1))
                        w, high = gu_ring[:, u, 0:2048], gu_high[u][:, 0:2048]
                    elif part == "up":
                        act.wait_ge(*at(f"up{u}", (e - u) * 8 + 16))
                        act.wait_ge(*at("g_done", e - 1))
                        w, high = gu_ring[:, u, 2048:4096], gu_high[u][:, 2048:4096]
                    else:
                        act.wait_ge(*at(f"dn{u}", (e - u) * 8 + 16))
                        act.wait_ge(*at("d_done", e - 1))
                        w, high = dn_ring[:, u, :], dn_high[u]
                    A(high, w, ACT.Copy).then_inc(sem["wh_" + part], 1)

                def rows_high(e, u):
                    act.wait_ge(*at("t_done", e + 1))
                    act.wait_ge(*at("g_done", e - 1))
                    A(xs[:, u, :, 0, :], slab(0)[:, u * 512:(u + 1) * 512].rearrange("p (c s) -> p c s", c=KC),
                      ACT.Copy).then_inc(sem["xs_hi"], 1)

                def gate_up_out(e, u):
                    act.wait_ge(*at("g_done", e + 1))
                    act.wait_ge(*at("ft_done", e - 1))
                    A(guo[:, u, :], slab(1)[:, u * 512:(u + 1) * 512], ACT.Copy).then_inc(sem["ge_done"], 1)

                def silu(e, u):
                    act.wait_ge(*at("ft_done", e + 1))
                    act.wait_ge(*at("af_done", e - 1))
                    A(sg[:, u, :], slab(3)[:, u * 512:u * 512 + 128], ACT.Silu).then_inc(sem["si_done"], 1)

                def rows_out(e, u, first=False):
                    act.wait_ge(*at("d_done", e + 1))
                    if not first:
                        act.wait_ge(*at(f"yd{u}", (e - u) * 8))
                    A(ysb[0:SLOTS, u, :], slab(2)[0:SLOTS, :], ACT.Copy).then_inc(sem["y_done"], 1)
                    act.wait_ge(*at("y_done", e + 1))
                    act.dma_start(yrow[bass.ds(e * SLOTS, SLOTS), :] if not isinstance(e, int) else yrow[e * SLOTS:(e + 1) * SLOTS, :],
                                  ysb[0:SLOTS, u, :]).then_inc(sem[f"yd{u}"], 16)

                def expert(e, u, first=False, last=False):
                    if not last:
                        weight_high(e + 1, 1 - u, "gate")
                        weight_high(e + 1, 1 - u, "up")
                    gate_up_out(e, u)
                    if not last:
                        rows_high(e + 1, 1 - u)
                    if not first:
                        rows_out(e - 1, 1 - u, first=isinstance(e, int) and e <= 2)
                    silu(e, u)
                    weight_high(e, u, "down")

                for part in ("gate", "up"):
                    weight_high(0, 0, part)
                rows_high(0, 0)
                done(("slot",))
                expert(0, 0, first=True)
                expert(1, 1)
                expert(2, 0)
                expert(3, 1)
                with act.Fori(2, NE // 2 - 1) as ep:
                    for u in range(2):
                        expert(ep * 2 + u, u)
                expert(NE - 2, 0)
                expert(NE - 1, 1, last=True)
                rows_out(NE - 1, 1)
                for u in range(2):
                    act.wait_ge(*at(f"yd{u}", 8 * NE))
                act.wait_ge(*at("base_ready", 1))
                settle(act)
                n_over = act.value_load(nov[0:1, 0:1], min_val=0, max_val=XBLK)
                with act.If(n_over > 0):
                    with act.Fori(0, XBLK) as x:
                        def ov(name):
                            return sem[name], (L * XBLK + x) * OV[name] + OV[name]

                        act.wait_ge(*ov("ov_t"))
                        A(xgT.rearrange("p c s -> p (c s)"), slab(0)[:, 0:512], ACT.Copy).then_inc(sem["ov_xt"], 1)
                        act.wait_ge(*ov("ov_g"))
                        A(sg[:, 0, :], slab(1)[:, 0:128], ACT.Silu).then_inc(sem["ov_si"], 1)
                        act.wait_ge(*ov("ov_d"))
                        A(ysb[0:SLOTS, 0, :], slab(2)[0:SLOTS, :], ACT.Copy).then_inc(sem["ov_y"], 1)
                        act.wait_ge(*ov("ov_y"))
                        act.dma_start(yrow[bass.ds((x + NE) * SLOTS, SLOTS), :], ysb[0:SLOTS, 0, :]).then_inc(sem["ov_yd"], 16)
                        act.wait_ge(*ov("ov_yd"))
                with act.Else():
                    for name in ("ov_xt", "ov_si", "ov_y", "ov_yd"):
                        act.sem_inc(sem[name], XBLK * OV[name])
                assert n_[0] == PER["act"], n_[0]

            act.wait_ge(sem["d_done"], DEPTH * PER["d_done"] + START["d_done"])
            act.dma_start(gB, a["final_norm_g"].broadcast_to([P, D])).then_inc(sem["fin_g"], 16)
            for i in range(NT):
                n = TS[i]
                act.wait_ge(sem["cb_done"], (DEPTH - 1) * PER["cb_done"] + START["cb_done"] + 2 * (i + 1))
                A(pr[0:n, 2048:3072], h[0:n, i, :], ACT.Square, accum_out=ss[0:n, i:i + 1]).then_inc(sem["fin_ss"], 1)
                act.wait_ge(sem["fin_ss"], i + 1)
            A(rms, ss, ACT.Sqrt, scale=1.0 / D, bias=eps_t).then_inc(sem["fin_rms"], 1)
            outs = [(0, NMETA, 64, 0)] + [(i, 0, TS[i], T0[i] - NMETA) for i in range(1, NT)]
            for i, r, n, s0 in outs:
                act.wait_ge(sem["fin_y"], i + 1)
                act.dma_start(out[s0:s0 + n, :], h[r:r + n, i, :]).then_inc(sem["out_done"], 16)
            act.wait_ge(sem["out_done"], 16 * len(outs))

        @block.gpsimd
        def _(pool):
            G = nc.gpsimd
            for r in (pr[:, :], ptb[:, :, :], AT[:, :, :, :], vA[:, :, :], S0[:, :, :]):
                G.memset(r, 0.0).then_inc(sem["init"], 1)
            pool.wait_ge(sem["init"], INITS - 1)
            G.memset(eps_t, EPS).then_inc(sem["init"], 1)
            pool.wait_ge(sem["x_load"], 16 * len(xslices))
            with pool.Fori(0, DEPTH) as L:
                def at(name, k):
                    return sem[name], L * PER[name] + (START.get(name, 0) + k)

                def low_part(name, q):
                    pool.wait_ge(*at("part_high", UNITS[name, q] + 1))
                    w, high, low = parts(name)
                    cols = quarter(name, q)
                    G.tensor_tensor(low[:, :, cols], w[:, :, cols], high[:, :, cols].bitcast(F32), ALU.subtract).then_inc(
                        sem["part_low"], 1)

                for i in range(NT):
                    pool.wait_ge(*at("cb_done", 2 * (i + 1) - 2 * NT))
                    settle(pool)
                    pool.dma_start(hrow[T0[i]:T0[i] + TS[i], :], h[0:TS[i], i, :]).then_inc(sem["h_out"], 16)
                for name in SPLIT[:SPLIT.index("hg")]:
                    for q in range(1 if name == "k3" else 4):
                        low_part(name, q)
                    if name == "k2":
                        pool.wait_ge(*at("d_done", 0))
                        settle(pool)
                        G.memset(r1[:, :], 0.0).then_inc(sem["r1_clear"], 1)

                with pool.If(L < 1):
                    for n in range(XBLK * SLOTS // (2 * P)):
                        r0 = NE * SLOTS + n * 2 * P
                        pool.dma_start(yrow[r0:r0 + 2 * P, :].rearrange("(p a) n -> p (a n)", a=2),
                                       zrow).then_inc(sem["y_init"], 16)

                pool.wait_ge(*at(*freed_at(("hq", HH - 1))))
                for m in range(HH * 7):
                    hd, l, u = m // 7, m % 7 + 1, m % 2
                    half = 2 ** (l - 1)
                    pool.wait_ge(*at("ex_ready", m + 1))
                    if m >= 2:
                        pool.wait_ge(*at("pe_done", JOBS[("lv", (m - 2) // 7, (m - 2) % 7 + 1)] + 1))
                    q_, k_, e_, qo, ko = (x.rearrange("p (n a t) -> p n a t", a=2, t=half) for x in (
                        hq[:, hd, :, :].rearrange("p j t -> p (j t)"), hk[:, hd, :, :].rearrange("p j t -> p (j t)"),
                        ebuf[:, u, :], qe[:, u, :], ke[:, u, :]))
                    G.tensor_tensor(qo[:, :, 1, :], q_[:, :, 1, :], e_[:, :, 1, :], ALU.mult)
                    G.tensor_tensor(ko[:, :, 0, :], k_[:, :, 0, :], e_[:, :, 0, :], ALU.mult).then_inc(sem["qe_ready"], 1)
                for q in range(4):
                    low_part("hg", q)
                for hd in range(HH):
                    pool.wait_ge(*at(*freed_at(("ot", NT - 1))))
                    q_ = hq[:, hd, :, :].rearrange("p j t -> p (j t)")
                    G.tensor_tensor(osq[:, hd, :], q_, q_, ALU.mult).then_inc(sem["sq_ready"], 1)

                for name in SPLIT[SPLIT.index("hg") + 1:]:
                    for q in range(4):
                        if name == "wb":
                            pool.wait_ge(*at("yh_ready", q + 1))
                            G.tensor_tensor(yl[:, q, :], ybT[:, q, :], yh[:, q, :].bitcast(F32), ALU.subtract).then_inc(sem["yl_ready"], 1)
                        low_part(name, q)

                pool.wait_ge(*at("xw0", 48))
                pool.wait_ge(*at("xw1", 32))
                pool.wait_ge(*at(*freed_at(("slot",))))
                settle(pool)
                with pool.Fori(0, NE // 2) as ep:
                    for u in range(2):
                        e = ep * 2 + u
                        pool.wait_ge(*at("t_done", e - 1))
                        G.tensor_copy(stage[:, u:u + 1], idx[:, bass.ds(e, 1)]).then_inc(sem["stg"], 1)
                        pool.wait_ge(*at("stg", e + 1))
                        settle(pool)
                        pool.indirect_dma_start(xg[0:SLOTS, u, :], None, xrow, bass.IndirectOffsetOnAxis(ap=stage[:, u:u + 1], axis=0)).then_inc(
                            sem[f"xg{u}"], 16)
                pool.wait_ge(*at("base_ready", 1))
                settle(pool)
                n_over = pool.value_load(nov[0:1, 0:1], min_val=0, max_val=XBLK)
                with pool.If(n_over > 0):
                    pool.wait_ge(*at("d_done", NE))
                    settle(pool)
                    with pool.Fori(0, XBLK) as x:
                        def ov(name, k=0):
                            return sem[name], (L * XBLK + x) * OV[name] + OV[name]

                        ex = pool.value_load(xei[0:1, bass.ds(x, 1)], min_val=0, max_val=NE - 1)
                        for m, name in enumerate(("w_expert_gate", "w_expert_up")):
                            pool.dma_start(ovw[:, m * 2048:(m + 1) * 2048],
                                           a[name][bass.ds((L * NE + ex) * D, D), :].rearrange("(p c) f -> p (c f)", p=P)).then_inc(sem["ov_w"], 16)
                        pool.dma_start(ovw[:, 4096:6144].rearrange("p (j n) -> p j n", j=2),
                                       a["w_expert_down"][bass.ds((L * NE + ex) * FF, FF), :].rearrange("(j p) n -> p j n", p=P)).then_inc(
                                           sem["ov_w"], 16)
                        G.tensor_copy(stage[:, 0:1], idx[:, bass.ds(x + NE, 1)]).then_inc(sem["ov_stg"], 1)
                        pool.wait_ge(*ov("ov_stg"))
                        settle(pool)
                        pool.indirect_dma_start(xg[0:SLOTS, 0, :], None, xrow, bass.IndirectOffsetOnAxis(ap=stage[:, 0:1], axis=0)).then_inc(
                            sem["ov_x"], 16)
                        pool.wait_ge(*ov("ov_yd"))
                with pool.Else():
                    for name in ("ov_w", "ov_stg", "ov_x"):
                        pool.sem_inc(sem[name], XBLK * OV[name])

                pool.wait_ge(*at("t_done", NE))
                for u in range(2):
                    pool.wait_ge(*at(f"yd{u}", 8 * NE))
                pool.wait_ge(sem["ov_yd"], L * (16 * XBLK) + 16 * XBLK)
                pool.wait_ge(*at("sidx_ready", 1))
                settle(pool)
                for k in range(2 * NT):
                    if k >= 4:
                        pool.wait_ge(*at("cb_done", k - 3))
                        settle(pool)
                    i, c = k // 2, k % 2
                    n = TS[i]
                    pool.indirect_dma_start(yg[0:n, k % 4, :], None, yrow,
                                            bass.IndirectOffsetOnAxis(ap=sidx[0:n, c * NT + i:c * NT + i + 1], axis=0)).then_inc(
                                                sem[f"yg{k % 4}"], 16)


def kernel(x, meta_tokens, mix_norm_g, w_in, hgrn_lb_logits, hgrn_norm_g, idx_k_norm_g, w_branch_hgrn,
           w_branch_dsa, w_out, ffn_norm_g, router_group_w, router_group_b, router_expert_w, router_expert_b,
           w_expert_gate, w_expert_up, w_expert_down, final_norm_g):
    import concourse.bacc as bacc
    from concourse.bass_utils import run_bass_kernel_spmd

    consts, _, lvm = shape_constants()
    arrays = dict(
        consts=consts, level_masks=lvm,
        x=x.reshape(SEQ, D), meta_tokens=meta_tokens, mix_norm_g=mix_norm_g, w_in=w_in.reshape(DEPTH * D, -1),
        hgrn_lb_logits=hgrn_lb_logits.reshape(DEPTH, HH, P).transpose(2, 0, 1).reshape(P, DEPTH * HH),
        hgrn_norm_g=hgrn_norm_g.reshape(DEPTH, HH, P).transpose(0, 2, 1).reshape(DEPTH * P, HH), idx_k_norm_g=idx_k_norm_g,
        w_branch_hgrn=w_branch_hgrn.reshape(-1, D), w_branch_dsa=w_branch_dsa.reshape(-1, D), w_out=w_out.reshape(-1, D),
        ffn_norm_g=ffn_norm_g, router_w=np.concatenate([router_group_w, router_expert_w], -1).reshape(DEPTH * D, NG + NE),
        router_b=np.concatenate([router_group_b, router_expert_b], -1),
        w_expert_gate=w_expert_gate.reshape(-1, FF), w_expert_up=w_expert_up.reshape(-1, FF),
        w_expert_down=w_expert_down.reshape(-1, D), final_norm_g=final_norm_g.reshape(1, D),
    )
    nc = bacc.Bacc("TRN2", target_bir_lowering=False, num_devices=1)
    arrays = {n: np.ascontiguousarray(v) for n, v in arrays.items()}
    aps = {n: nc.dram_tensor(n, v.shape, mybir.dt.from_np(v.dtype), kind="ExternalInput").ap() for n, v in arrays.items()}
    out = nc.dram_tensor("out", (SEQ, D), F32, kind="ExternalOutput").ap()
    program(nc, aps, out)
    return run_bass_kernel_spmd(nc, [arrays], core_ids=[0]).results[0]["out"].reshape(1, SEQ, D)
```
